# Optimizing a Trainium2 kernel written in Bass

```python
import math
import jax, jax.numpy as jnp
from jax import lax
import numpy as np

D_MODEL = 1024
BATCH = 1
SEQ = 256
DEPTH = 2

GRID_W = 64
CTX_LEN = 256
EPS = 1e-6

N_BRANCH = 4
BRANCH_W = 512

POOL_GROUPS = 4
POOL_GC = BRANCH_W // POOL_GROUPS
POOL_WINDOWS = (2, 4, 8, 16)

DIFF_HEADS = 4
DIFF_DH = 64
DIFF_DV = BRANCH_W // DIFF_HEADS
DIFF_QBLOCK = 128
ROPE_BASE = 10000.0

SGU_GROUPS = 4
SGU_GC = BRANCH_W // SGU_GROUPS
SGU_CHUNK = 128

NA_HEADS = 8
NA_DH = BRANCH_W // NA_HEADS
NA_WIN_R = 8
NA_WIN_C = 16

N_EXPERTS = 16
EC_CAPACITY = 2
D_EXPERT = 1024

COL_SIZES = (
    DIFF_HEADS * 2 * DIFF_DH,
    BRANCH_W,
    BRANCH_W,
    BRANCH_W,
    DIFF_HEADS * 2 * DIFF_DH,
    BRANCH_W,
    BRANCH_W,
    BRANCH_W,
    BRANCH_W,
    N_BRANCH * D_MODEL,
)
KV_COLS = sum(COL_SIZES[:4])
IN_COLS = sum(COL_SIZES)

kernel_name = "hybrid_gated_branch_dit_block"

def rmsnorm(x, g):
    xf = x.astype(jnp.float32)
    y = xf * lax.rsqrt(jnp.mean(xf * xf, axis=-1, keepdims=True) + EPS)
    return y.astype(x.dtype) * g

def layernorm(x, g):
    xf = x.astype(jnp.float32)
    xc = xf - jnp.mean(xf, axis=-1, keepdims=True)
    y = xc * lax.rsqrt(jnp.mean(xc * xc, axis=-1, keepdims=True) + EPS)
    return y.astype(x.dtype) * g

def modulate(h, shift, scale):
    return h * (1 + scale) + shift

def split_cols(z, sizes):
    offs = np.cumsum(sizes)[:-1]
    return jnp.split(z, [int(o) for o in offs], axis=-1)

def rope_tables(T):
    t = jnp.arange(T)
    row = (t // GRID_W).astype(jnp.float32)
    col = (t % GRID_W).astype(jnp.float32)
    nf = DIFF_DH // 4
    inv = ROPE_BASE ** (-jnp.arange(nf, dtype=jnp.float32) / nf)
    ar = row[:, None] * inv
    ac = col[:, None] * inv
    return (jnp.cos(ar), jnp.sin(ar), jnp.cos(ac), jnp.sin(ac))

def rotate(x, cos, sin):
    x1, x2 = jnp.split(x, 2, axis=-1)
    return jnp.concatenate([x1 * cos - x2 * sin, x1 * sin + x2 * cos], axis=-1).astype(x.dtype)

def rope2d(x, tabs):
    cr, sr, cc, sc = [a[None, :, None, None, :] for a in tabs]
    xr, xcol = jnp.split(x, 2, axis=-1)
    return jnp.concatenate([rotate(xr, cr, sr), rotate(xcol, cc, sc)], axis=-1)

def pool_mixer(z, w_pool, scale):
    B, T, _ = z.shape
    zf = z.reshape(B, T, POOL_GROUPS, POOL_GC).astype(jnp.float32)
    cs = jnp.concatenate([jnp.zeros((B, 1, POOL_GROUPS, POOL_GC), jnp.float32),
                          jnp.cumsum(zf, axis=1)], axis=1)
    t = jnp.arange(T)
    means = []
    for g, w in enumerate(POOL_WINDOWS):
        lo = jnp.clip(t - w // 2, 0, T)
        hi = jnp.clip(t + w // 2, 0, T)
        cnt = (hi - lo).astype(jnp.float32)[None, :, None]
        means.append((cs[:, hi, g] - cs[:, lo, g]) / cnt)
    pooled = jnp.stack(means, axis=2)
    d = (pooled - zf).astype(z.dtype)
    y = jnp.einsum('btgc,gce->btge', d, w_pool)
    return y.reshape(B, T, BRANCH_W) * scale

def compute_lambda(lam_p, lam_init):
    lp = lam_p.astype(jnp.float32)
    return jnp.exp(jnp.sum(lp[0] * lp[1])) - jnp.exp(jnp.sum(lp[2] * lp[3])) + lam_init

def diff_attend(q, k, v, lam, lam_init, g):
    s = jnp.einsum('bqhmd,bkhmd->bhmqk', q, k).astype(jnp.float32) * (DIFF_DH ** -0.5)
    p = jax.nn.softmax(s, axis=-1)
    a = (p[:, :, 0] - lam * p[:, :, 1]).astype(v.dtype)
    o = jnp.einsum('bhqk,bkhe->bqhe', a, v)
    o = rmsnorm(o, g) * (1.0 - lam_init)
    return o.reshape(o.shape[0], o.shape[1], BRANCH_W)

def diff_latent(q, k, v, lam, lam_init, g):
    B, T = q.shape[0], q.shape[1]
    nb = T // DIFF_QBLOCK
    qb = jnp.moveaxis(q.reshape(B, nb, DIFF_QBLOCK, DIFF_HEADS, 2, DIFF_DH), 1, 0)
    ob = lax.map(lambda qi: diff_attend(qi, k, v, lam, lam_init, g), qb)
    return jnp.moveaxis(ob, 0, 1).reshape(B, T, BRANCH_W)

def dense_attend(q, k, v, heads, dh):
    B, Q, _ = q.shape
    K = k.shape[1]
    qh = q.reshape(B, Q, heads, dh)
    kh = k.reshape(B, K, heads, dh)
    vh = v.reshape(B, K, heads, dh)
    s = jnp.einsum('bqhd,bkhd->bhqk', qh, kh).astype(jnp.float32) * (dh ** -0.5)
    p = jax.nn.softmax(s, axis=-1).astype(v.dtype)
    return jnp.einsum('bhqk,bkhd->bqhd', p, vh).reshape(B, Q, heads * dh)

def na_latent(q, k, v, k_ctx, v_ctx, rpb):
    B, T, _ = q.shape
    rows = T // GRID_W
    kr = min(NA_WIN_R, rows)
    grid = lambda a: a.reshape(B, rows, GRID_W, NA_HEADS, NA_DH)
    qg, kg, vg = grid(q), grid(k), grid(v)
    kc = k_ctx.reshape(B, -1, NA_HEADS, NA_DH)
    vc = v_ctx.reshape(B, -1, NA_HEADS, NA_DH)
    cols = np.arange(GRID_W)
    col_start = np.clip(cols - NA_WIN_C // 2, 0, GRID_W - NA_WIN_C)
    col_idx = col_start[:, None] + np.arange(NA_WIN_C)[None, :]
    dc_idx = col_idx - cols[:, None] + (NA_WIN_C - 1)
    nloc = kr * NA_WIN_C
    scale = NA_DH ** -0.5

    def row_fn(args):
        r, q_row = args
        r0 = jnp.clip(r - kr // 2, 0, rows - kr)
        kwin = lax.dynamic_slice_in_dim(kg, r0, kr, axis=1)[:, :, col_idx]
        vwin = lax.dynamic_slice_in_dim(vg, r0, kr, axis=1)[:, :, col_idx]
        dr_idx = r0 + jnp.arange(kr) - r + (NA_WIN_R - 1)
        bias = rpb[:, dr_idx][:, :, dc_idx].transpose(0, 2, 1, 3)
        s_loc = jnp.einsum('bqhd,biqjhd->bhqij', q_row, kwin).astype(jnp.float32) * scale \
            + bias.astype(jnp.float32)[None]
        s_ctx = jnp.einsum('bqhd,bkhd->bhqk', q_row, kc).astype(jnp.float32) * scale
        s = jnp.concatenate([s_loc.reshape(B, NA_HEADS, GRID_W, nloc), s_ctx], axis=-1)
        p = jax.nn.softmax(s, axis=-1).astype(v.dtype)
        p_loc = p[..., :nloc].reshape(B, NA_HEADS, GRID_W, kr, NA_WIN_C)
        p_ctx = p[..., nloc:]
        return jnp.einsum('bhqij,biqjhd->bqhd', p_loc, vwin) + jnp.einsum('bhqk,bkhd->bqhd', p_ctx, vc)

    out = lax.map(row_fn, (jnp.arange(rows), jnp.moveaxis(qg, 1, 0)))
    return jnp.moveaxis(out, 0, 1).reshape(B, T, BRANCH_W)

def sgu_mixer(u, v, g, w_s, b):
    B, T, _ = u.shape
    n = T // SGU_CHUNK
    u = jax.nn.gelu(u)
    v = layernorm(jax.nn.gelu(v), g)
    vr = v.reshape(B, n, SGU_CHUNK, SGU_GROUPS, SGU_GC)
    f = jnp.einsum('gpq,bnqgc->bnpgc', w_s, vr) + b.T[None, None, :, :, None]
    return u * f.reshape(B, T, BRANCH_W)

def merge(branches, gates, w_br, w_out):
    B, T, _ = gates.shape
    br = jnp.stack(branches, axis=2)
    proj = jnp.einsum('btie,ied->btid', br, w_br)
    gsig = jax.nn.sigmoid(gates.reshape(B, T, N_BRANCH, D_MODEL))
    return jnp.sum(gsig * proj, axis=2) @ w_out

def token_mixer(hx, hc, tabs, p, lam, lam_init, with_ctx_out):
    B, T, _ = hx.shape
    w_in = p['w_in']
    dk, dv, nk, nv, dq, nq, pz, su, sv, gz = split_cols(hx @ w_in, COL_SIZES)
    dk_c, dv_c, nk_c, nv_c = split_cols(hc @ w_in[:, :KV_COLS], COL_SIZES[:4])
    dshape = lambda a: a.reshape(a.shape[0], a.shape[1], DIFF_HEADS, 2, DIFF_DH)
    vshape = lambda a: a.reshape(a.shape[0], a.shape[1], DIFF_HEADS, DIFF_DV)
    k_all = jnp.concatenate([dshape(dk_c), rope2d(dshape(dk), tabs)], axis=1)
    v_all = jnp.concatenate([vshape(dv_c), vshape(dv)], axis=1)
    diff_x = diff_latent(rope2d(dshape(dq), tabs), k_all, v_all, lam, lam_init, p['diff_subln_g'])
    na_x = na_latent(nq, nk, nv, nk_c, nv_c, p['na_rpb'])
    pool_x = pool_mixer(pz, p['pool_w'], p['pool_scale'])
    sgu_x = sgu_mixer(su, sv, p['sgu_norm_g'], p['sgu_w'], p['sgu_b'])
    out_x = merge([pool_x, diff_x, sgu_x, na_x], gz, p['w_br'], p['w_out'])
    if not with_ctx_out:
        return out_x, None
    dq_c, nq_c, pz_c, su_c, sv_c, gz_c = split_cols(hc @ w_in[:, KV_COLS:], COL_SIZES[4:])
    diff_c = diff_attend(dshape(dq_c), dshape(dk_c), vshape(dv_c), lam, lam_init, p['diff_subln_g'])
    na_c = dense_attend(nq_c, nk_c, nv_c, NA_HEADS, NA_DH)
    pool_c = pool_mixer(pz_c, p['pool_w'], p['pool_scale'])
    sgu_c = sgu_mixer(su_c, sv_c, p['sgu_norm_g'], p['sgu_w'], p['sgu_b'])
    out_c = merge([pool_c, diff_c, sgu_c, na_c], gz_c, p['w_br'], p['w_out'])
    return out_x, out_c

def ec_moe(h, router_w, w1, w3, w2):
    B, T, D = h.shape
    cap = EC_CAPACITY * T // N_EXPERTS
    aff = jax.nn.softmax((h @ router_w).astype(jnp.float32), axis=-1)
    gate, idx = lax.top_k(jnp.swapaxes(aff, 1, 2), cap)
    xs = jax.vmap(lambda hb, ib: hb[ib])(h, idx)
    hid = jax.nn.silu(jnp.einsum('becd,edf->becf', xs, w1)) * jnp.einsum('becd,edf->becf', xs, w3)
    y = jnp.einsum('becf,efd->becd', hid, w2) * gate[..., None].astype(h.dtype)
    return jax.vmap(lambda ib, yb: jnp.zeros((T, D), h.dtype).at[ib.reshape(-1)].add(yb.reshape(-1, D)))(idx, y)

def setup_inputs(seed: int = 0) -> dict:
    key = jax.random.key(seed)
    ks = jax.random.split(key, 24)
    nrm = lambda k, shape, s: jax.random.normal(k, shape, jnp.float32) * s
    D, L, E, F = D_MODEL, DEPTH, N_EXPERTS, D_EXPERT
    return {
        'x': nrm(ks[0], (BATCH, SEQ, D), 1.0),
        'c': nrm(ks[1], (BATCH, D), 1.0),
        'ctx': nrm(ks[2], (BATCH, CTX_LEN, D), 1.0),
        'c_ctx': nrm(ks[3], (D,), 1.0),
        'w_mod': nrm(ks[4], (L, D, 6 * D), 0.5 * D ** -0.5),
        'b_mod': nrm(ks[5], (L, 6 * D), 0.02),
        'norm1_g': 1.0 + nrm(ks[6], (L, D), 0.02),
        'norm2_g': 1.0 + nrm(ks[7], (L, D), 0.02),
        'w_in': nrm(ks[8], (L, D, IN_COLS), D ** -0.5),
        'pool_w': nrm(ks[9], (L, POOL_GROUPS, POOL_GC, POOL_GC), POOL_GC ** -0.5),
        'pool_scale': 1.0 + nrm(ks[10], (L, BRANCH_W), 0.1),
        'diff_lambda': nrm(ks[11], (L, 4, DIFF_DH), 0.1),
        'diff_subln_g': 1.0 + nrm(ks[12], (L, DIFF_DV), 0.02),
        'sgu_norm_g': 1.0 + nrm(ks[13], (L, BRANCH_W), 0.02),
        'sgu_w': nrm(ks[14], (L, SGU_GROUPS, SGU_CHUNK, SGU_CHUNK), SGU_CHUNK ** -0.5),
        'sgu_b': 1.0 + nrm(ks[15], (L, SGU_GROUPS, SGU_CHUNK), 0.1),
        'na_rpb': nrm(ks[16], (L, NA_HEADS, 2 * NA_WIN_R - 1, 2 * NA_WIN_C - 1), 0.1),
        'w_br': nrm(ks[17], (L, N_BRANCH, BRANCH_W, D), BRANCH_W ** -0.5),
        'w_out': nrm(ks[18], (L, D, D), D ** -0.5),
        'router_w': nrm(ks[19], (L, D, E), D ** -0.5),
        'moe_w1': nrm(ks[20], (L, E, D, F), D ** -0.5),
        'moe_w3': nrm(ks[21], (L, E, D, F), D ** -0.5),
        'moe_w2': nrm(ks[22], (L, E, F, D), F ** -0.5),
        'final_g': 1.0 + nrm(ks[23], (D,), 0.02),
    }

def reference(x, c, ctx, c_ctx, w_mod, b_mod, norm1_g, norm2_g, w_in, pool_w, pool_scale,
              diff_lambda, diff_subln_g, sgu_norm_g, sgu_w, sgu_b, na_rpb, w_br, w_out,
              router_w, moe_w1, moe_w3, moe_w2, final_g):
    T = x.shape[1]
    tabs = rope_tables(T)
    silu_c = jax.nn.silu(c)
    silu_cc = jax.nn.silu(c_ctx)
    x_lat, x_ctx = x, ctx
    for l in range(DEPTH):
        last = l == DEPTH - 1
        lam_init = 0.8 - 0.6 * math.exp(-0.3 * l)
        p = {'w_in': w_in[l], 'pool_w': pool_w[l], 'pool_scale': pool_scale[l],
             'diff_subln_g': diff_subln_g[l], 'sgu_norm_g': sgu_norm_g[l], 'sgu_w': sgu_w[l],
             'sgu_b': sgu_b[l], 'na_rpb': na_rpb[l], 'w_br': w_br[l], 'w_out': w_out[l]}
        lam = compute_lambda(diff_lambda[l], lam_init)
        sh1, sc1, g1, sh2, sc2, g2 = jnp.split(silu_c @ w_mod[l] + b_mod[l], 6, axis=-1)
        csh1, csc1, cg1, csh2, csc2, cg2 = jnp.split(silu_cc @ w_mod[l] + b_mod[l], 6, axis=-1)
        hx = modulate(rmsnorm(x_lat, norm1_g[l]), sh1[:, None], sc1[:, None])
        hc = modulate(rmsnorm(x_ctx, norm1_g[l]), csh1, csc1)
        mix_x, mix_c = token_mixer(hx, hc, tabs, p, lam, lam_init, not last)
        x_lat = x_lat + g1[:, None] * mix_x
        hx2 = modulate(rmsnorm(x_lat, norm2_g[l]), sh2[:, None], sc2[:, None])
        x_lat = x_lat + g2[:, None] * ec_moe(hx2, router_w[l], moe_w1[l], moe_w3[l], moe_w2[l])
        if not last:
            x_ctx = x_ctx + cg1 * mix_c
            hc2 = modulate(rmsnorm(x_ctx, norm2_g[l]), csh2, csc2)
            x_ctx = x_ctx + cg2 * ec_moe(hc2, router_w[l], moe_w1[l], moe_w3[l], moe_w2[l])
    return rmsnorm(x_lat, final_g)


_drawn_inputs = setup_inputs


def setup_inputs(seed=0):
    import zlib

    import numpy as np

    out = dict(_drawn_inputs(seed))
    spreads = {}
    factors = {'norm1_g': 5.33,
     'norm2_g': 5.848,
     'diff_lambda': 3.451,
     'diff_subln_g': 8.0,
     'sgu_norm_g': 8.0,
     'sgu_b': 3.22,
     'na_rpb': 8.0,
     'final_g': 2.908}
    for name, (base, spread) in spreads.items():
        noise = np.random.default_rng([zlib.crc32(name.encode()), seed]).standard_normal(out[name].shape)
        drawn = base * np.exp(spread * noise) if base else spread * noise
        out[name] = __import__('jax').numpy.asarray(drawn.astype(out[name].dtype))
    for name, factor in factors.items():
        out[name] = (out[name] * factor).astype(out[name].dtype)
    return out
```

```python
import math
from contextlib import ExitStack

import numpy as np
import concourse.bass as bass
from concourse import mybir

D = 1024
T = 256
L = 2
GRID_W = 64
BW = 512
NBR = 4
E = 16
CAP = 2 * T // E
NA_C = 16
RPB_R, RPB_C = 15, 31
POOL_W = (2, 4, 8, 16)
EPS = 1e-6
KD = D // 128
NEG = -1.0e30

NSLOT = 6
SLOT = 2048
MC = 256

GROUPS = [("dk", "f"), ("dv", "t"), ("nk", "f"), ("nv", "t"), ("dq", "f"), ("nq", "f"),
          ("pz", "f"), ("su", "f"), ("sv", "t")]
KV_GROUPS = 4
GATE_COL = 512 * len(GROUPS)

C_ID, C_FLIP, C_PERM = 0, 128, 256
C_COS, C_SIN = 384, 640
C_TRI, C_ONE = 896, 1024
C_IOTA, C_MASK = 1152, 1184
C_SELC, C_SELR, C_SELY = 1248, 1250, 1506
C_CNT = 1634
C_ALL = C_CNT + 4 * 256

P_POOLW, P_SGUW, P_SGUB, P_LAM, P_RW = 0, 512, 1024, 1536, 1792
P_PSC, P_SUBG, P_SGUG = 1920, 1924, 1925
P_ALL = 1929
S_N1, S_N2, S_C = 0, 16, 32
S_ALL = 48


def shape_constants():
    c = np.zeros((128, C_ALL), np.float32)
    p = np.arange(128)
    c[:, C_ID:C_ID + 128] = np.eye(128)
    c[:, C_FLIP:C_FLIP + 128] = np.eye(128)[::-1]
    c[p ^ 16, C_PERM + p] = 1.0
    nf = 16
    inv = (10000.0 ** (-np.arange(nf, dtype=np.float32) / nf)).astype(np.float32)
    t = np.arange(T)
    pos = np.stack([(t // GRID_W), (t % GRID_W)]).astype(np.float32)
    f = p % 64
    ang = pos[f // 32] * inv[f % 16][:, None]
    c[:, C_COS:C_COS + T] = np.cos(ang.astype(np.float32))
    c[:, C_SIN:C_SIN + T] = np.sin(ang.astype(np.float32)) * np.where(f % 32 < 16, -1.0, 1.0)[:, None]
    c[:, C_TRI:C_TRI + 128] = p[:, None] <= p[None, :]
    c[:, C_ONE:C_ONE + 128] = 1.0
    c[:, C_IOTA:C_IOTA + CAP] = 1.0 + np.arange(CAP)
    col = 63 - p % 64
    start = np.clip(col - NA_C // 2, 0, GRID_W - NA_C)
    k = np.arange(GRID_W)
    inside = (k[None, :] >= start[:, None]) & (k[None, :] < start[:, None] + NA_C)
    c[:, C_MASK:C_MASK + GRID_W] = np.where(inside, 0.0, NEG)
    for s in range(2):
        c[p % 32 == s, C_SELC + s] = 1.0
        c[p % 32 == s, C_SELR + 128 * s:C_SELR + 128 * s + 128] = 1.0
        c[:, C_SELY:C_SELY + 128] += ((p % 32 == s)[:, None] & ((p // CAP) % 2 == s)[None, :])
    for g, w in enumerate(POOL_W):
        n = np.clip(t + w // 2, 0, T) - np.clip(t - w // 2, 0, T)
        c[:, C_CNT + g * T:C_CNT + (g + 1) * T] = 1.0 / n.astype(np.float32)
    return c


class Signal:

    def __init__(self, sem, per_layer):
        self.sem, self.per_layer = sem, per_layer

    def at(self, layer, count):
        return self.sem, sum(self.per_layer[:layer]) + count


def streams(l):
    return 2 if l < L - 1 else 1


def ring_plan():
    use = [0] * NSLOT
    pos = 0
    plan = {}

    def straight(name, n):
        nonlocal pos
        items = []
        for _ in range(n):
            items.append((pos, use[pos]))
            use[pos] += 1
            pos = (pos + 1) % NSLOT
        plan[name] = items

    def looped(name, per_pass, passes):
        nonlocal pos
        pos = 0
        plan[name] = (list(use), per_pass // NSLOT)
        for s in range(NSLOT):
            use[s] += per_pass // NSLOT * passes

    straight("M1", 8)
    plan["M1", 0] = plan.pop("M1")
    for l in range(L):
        straight(("W", l), 2 * len(GROUPS))
        looped(("G", l), 6, NBR)
        straight(("M2", l), 16)
        if l + 1 < L:
            straight(("M1", l + 1), 8)
        straight(("O", l), 4)
        g = 128 // (CAP * streams(l))
        looped(("E", l), 12 * g, E // g)
    return plan


def w_units(l):
    units, n = [], {"act": 0, "dve": 0}

    def add(**u):
        n[u["by"]] += 1
        u["nth"] = n[u["by"]]
        units.append(u)

    for q in range(2 * len(GROUPS)):
        gi, half = q // 2, q % 2
        name, kind = GROUPS[gi]
        wide = gi < KV_GROUPS or streams(l) == 2
        for c in range(2):
            if kind == "t" and c == 1 and not wide:
                continue
            by = "act" if name in ("su", "sv") or (q + c) % 2 else "dve"
            add(kind=kind, name=name, slot=q, half=half, c=c, tokens=2 * T if wide else T, by=by,
                frees=(kind == "f" and c == 1) or (kind == "t" and (c == 1 or not wide)))
        if name == "nq" and half == 1:
            for nm in ("dk", "dq"):
                for pair in range(2):
                    add(kind="rope", name=nm, pair=pair, by="dve")
    return units, n


def attention_blocks(l):
    return [(kind, s, qt, h) for kind in ("diff", "na") for s in range(streams(l)) for qt in range(2)
            for h in range(4)]


def tr_units(l):
    blocks = attention_blocks(l)
    nb = len(blocks)
    units, n = [], {"act": 0, "dve": 0}

    def add(**u):
        n[u["by"]] += 1
        u["nth"] = n[u["by"]]
        u["t"] = len(units)
        units.append(u)

    for i in range(nb + 6):
        if 0 <= i - 1 < nb:
            if blocks[i - 1][0] == "diff":
                add(kind="p", b=i - 1, a=0, by="act")
            else:
                add(kind="p", b=i - 1, a=0, by="act")
                add(kind="p", b=i - 1, a=1, by="dve")
        g = (i - 2 - 5) // 4
        if (i - 2 - 5) % 4 == 0 and 0 <= g < nb // 4:
            add(kind="o", g=g, by="act")
    assert sum(u["kind"] == "o" for u in units) >= nb // 4 - 1
    return units, n


def build(nc, A, out):
    f32 = mybir.dt.float32
    ACT = mybir.ActivationFunctionType
    ALU = mybir.AluOpType
    AX = mybir.AxisListType
    ds = bass.ds

    ctx = ExitStack()
    with ctx:
        def sb(name, shape):
            return ctx.enter_context(nc.sbuf_tensor(name, shape, f32))

        def signal(name, *per_layer):
            return Signal(ctx.enter_context(nc.semaphore(name)), list(per_layer))

        def counter(name):
            return ctx.enter_context(nc.semaphore(name))

        ring = sb("ring", [128, NSLOT, SLOT])
        x = sb("x", [128, 4, D])
        hT = sb("hT", [128, KD, 2 * T])
        arena = sb("arena", [128, 9, 2048])
        cst = sb("cst", [128, C_ALL])
        par = sb("par", [128, P_ALL])
        stay = sb("stay", [128, S_ALL])
        bm = sb("bm", [24, L, MC])
        nab = sb("nab", [128, 8, 6 * GRID_W])
        work = sb("work", [128, 8, 512])
        small = sb("small", [128, 256])
        cond = sb("cond", [128, KD, 32])
        modp = sb("modp", [128, 2, MC])
        modA = sb("modA", [128, 2, 2, KD])
        modB = sb("modB", [128, 2, 2, KD])
        PS = ctx.enter_context(nc.psum_tensor("PS", [128, 8, 512], f32))

        def unit_of(i, n=1):
            return arena[:, i:i + n, :].rearrange("p a b -> p (a b)")

        region = {nm: unit_of(i).rearrange("p (a b) -> p a b", a=4)
                  for nm, i in (("pz", 0), ("dq", 1), ("su", 2), ("nq", 3), ("dk", 4), ("nk", 5),
                                ("dv", 6), ("nv", 7), ("sv", 8))}
        branches = unit_of(0, 4)
        mT = unit_of(4, 2).rearrange("p (a b) -> p a b", a=KD)
        g1b = unit_of(6).rearrange("p (a b) -> p a b", a=2)
        g2r = unit_of(7)[:, 0:D]
        xn_mix = unit_of(6, 2).rearrange("p (a b) -> p a b", a=4)
        xn_moe = unit_of(0, 2).rearrange("p (a b) -> p a b", a=4)
        xsT = unit_of(2)[:, 0:1024].rearrange("p (a b) -> p a b", a=KD)
        hid = unit_of(2)[:, 1024:2048]
        sil = unit_of(3)[:, 0:1024]
        hidT = unit_of(3)[:, 1024:2048].rearrange("p (a b) -> p a b", a=KD)
        ysb = unit_of(4)[:, 0:1024]
        combT = unit_of(4)[:, 1024:1536].rearrange("p (a b) -> p a b", a=4)
        selg = unit_of(5)[:, 0:512].rearrange("p (a b) -> p a b", a=4)
        selp = unit_of(5)[:, 512:1024]
        afT = unit_of(5)[0:32, 1024:1280]
        afR = unit_of(5)[0:32, 1280:1792].rearrange("p (a b) -> p a b", a=2)
        top = unit_of(5)[0:32, 1792:1824]

        ident = cst[:, C_ID:C_ID + 128]
        cosT, sinT = cst[:, C_COS:C_COS + T], cst[:, C_SIN:C_SIN + T]
        iota1 = cst[:, C_IOTA:C_IOTA + CAP]

        ss, ms, rstd = small[:, 0:4], small[:, 4:8], small[:, 8:12]
        half = small[:, 12:16]
        nmx = small[:, 16:20].rearrange("p (a b) -> p a b", a=2)
        rs = small[:, 20:24].rearrange("p (a b) -> p a b", a=2)
        rr = small[:, 24:32].rearrange("p (a b) -> p a b", a=4)
        lam = small[:, 32:40]
        subg = small[:, 40:41]
        oss, oms, orstd = small[:, 44:48], small[:, 48:52], small[:, 52:56]
        vst = small[:, 56:80].rearrange("p (a b) -> p a b", a=4)
        vmv = small[:, 80:88].rearrange("p (a b) -> p a b", a=4)
        vms, vrstd = small[:, 88:92], small[:, 92:96]
        nar = small[:, 96:128].rearrange("p (a b) -> p a b", a=4)
        rmx, rsum, rinv = small[:, 128:132], small[:, 132:136], small[:, 136:140]
        rex = sb("rex", [128, 4, E])
        aff = sb("aff", [128, 2, 2, E])
        msk = sb("msk", [128, 2, 2 * E])
        place = sb("place", [128, 2, 2, E])

        p_t = work[:, 0:4, :].rearrange("p (a b) c -> p a b c", a=2)
        at = work[:, 4:6, :]
        on = work[:, 6, :]
        osq = work[:, 7, :]
        sq_junk = work[:, 0:2, :].rearrange("p a b -> p (a b)")
        sgt = work[:, 0:2, :]
        gtmp = work[:, 2:4, :]

        NT = [2 * streams(l) for l in range(L)]
        norms = [(0, 0, 2), (0, 1, streams(0)), (1, 0, 2), (1, 1, streams(1)), (2, 0, 1)]
        loaded = [counter(f"ring_loaded{i}") for i in range(NSLOT)]
        freed = [counter(f"ring_freed{i}") for i in range(NSLOT)]
        consts_loaded = counter("consts_loaded")
        par_loaded = counter("par_loaded")
        bias_loaded = counter("bias_loaded")
        bias_masked = signal("bias_masked", 1, 1)
        half_ready = counter("half_ready")
        cond_ready = counter("cond_ready")
        MS = [8 + 16 + 8, 16]
        mod_sum = signal("mod_sum", *MS)
        mod_part = signal("mod_part", *MS)
        mod_cols = signal("mod_cols", 3, 1)
        mod_ready = signal("mod_ready", 3, 1)
        gate_bc = signal("gate_bc", 8, 8)
        gate_rows = signal("gate_rows", 8, 8)
        NN = [2 * n for _, _, n in norms]
        sq_done = signal("sq_done", *NN)
        ms_done = signal("ms_done", *[1] * 5)
        rstd_done = signal("rstd_done", *[1] * 5)
        xn_ready = signal("xn_ready", *NN)
        xt_ready = signal("xt_ready", *[4 * n for _, _, n in norms[:4]])
        hT_act = signal("hT_act", *[2 * n * 2 for _, _, n in norms[:4]])
        hT_dve = signal("hT_dve", *[2 * n * 2 for _, _, n in norms[:4]])
        WU = [w_units(l) for l in range(L)]
        w_sum = signal("w_sum", *[len(u) for u, _ in WU])
        w_act = signal("w_act", *[n["act"] for _, n in WU])
        w_dve = signal("w_dve", *[n["dve"] for _, n in WU])
        dve_step = counter("dve_step")
        pool_step = counter("pool_step")
        lam_prod = signal("lam_prod", 1, 1)
        lam_exp = signal("lam_exp", 1, 1)
        lam_ready = signal("lam_ready", 1, 1)
        pooled = signal("pooled", 4, 4)
        pool_sum = signal("pool_sum", 4, 4)
        pool_out = signal("pool_out", 4, 4)
        v_stats = signal("v_stats", 1, 1)
        v_rstd = signal("v_rstd", 1, 1)
        v_norm = signal("v_norm", *NT)
        sgu_sum = signal("sgu_sum", 4, 4)
        sgu_out = signal("sgu_out", 4, 4)
        BL = [attention_blocks(l) for l in range(L)]
        NB = [len(b) for b in BL]
        TU = [tr_units(l) for l in range(L)]
        scores = signal("scores", *NB)
        maxes = signal("maxes", *NB)
        exps = signal("exps", *NB)
        probs = signal("probs", *NB)
        tr_made = signal("tr_made", *[len(u) for u, _ in TU])
        at_act = signal("at_act", *[n["act"] for _, n in TU])
        at_dve = signal("at_dve", *[n["dve"] for _, n in TU])
        pv = signal("pv", *NB)
        NG = [n // 4 for n in NB]
        o_square = signal("o_square", *[n // 2 for n in NG])
        o_ss = signal("o_ss", *[n // 2 for n in NG])
        o_rstd = signal("o_rstd", *[n // 2 for n in NG])
        o_norm = signal("o_norm", *NG)
        gates = signal("gates", 8 * NBR, 8 * NBR)
        projs = signal("projs", 8 * NBR, 8 * NBR)
        sigs = signal("sigs", 8 * NBR, 8 * NBR)
        gated = signal("gated", 8 * NBR, 8 * NBR)
        merged = signal("merged", 2 + 8 * NBR, 2 + 8 * NBR)
        mix_sum = signal("mix_sum", *[2 * n for n in NT])
        mix_x = signal("mix_x", *[2 * n for n in NT])
        logits = signal("logits", 1, 1)
        r_max = signal("r_max", 1, 1)
        r_exp = signal("r_exp", *NT)
        aff_ready = signal("aff_ready", 1, 1)
        affT_made = signal("affT_made", 1, 1)
        mask_ready = signal("mask_ready", 1, 1)
        maskT_made = signal("maskT_made", 1, 1)
        maskT_ready = signal("maskT_ready", 1, 1)
        count_made = signal("count_made", 1, 1)
        place_ready = signal("place_ready", 1, 1)
        GE = [128 // (CAP * streams(l)) for l in range(L)]
        NP = [E // g for g in GE]

        def packs(name, n0, n1):
            return signal(name, n0 * NP[0], n1 * NP[1])

        sel_ready = packs("sel_ready", 2, 1)
        selg_ready = packs("selg_ready", 2, 1)
        gathered = packs("gathered", 2, 2)
        xs_mul = packs("xs_mul", 4, 2)
        xs_ready = packs("xs_ready", 4, 2)
        combT_made = packs("combT_made", 1, 1)
        combT_ready = packs("combT_ready", 1, 1)
        h1_sum = packs("h1_sum", 1, 1)
        h3_sum = packs("h3_sum", 1, 1)
        sil_ready = packs("sil_ready", 2, 2)
        hid_ready = packs("hid_ready", 2, 2)
        hidT_made = packs("hidT_made", 2, 2)
        hidT_act = packs("hidT_act", 1, 1)
        hidT_dve = packs("hidT_dve", 1, 1)
        y_sum = packs("y_sum", 1, 1)
        y_ready = packs("y_ready", 2, 2)
        comb_sum = packs("comb_sum", 2 * NT[0], 2 * NT[1])
        comb_x = packs("comb_x", 2 * NT[0], 2 * NT[1])
        fin_ready = counter("fin_ready")
        out_stored = counter("out_stored")

        plan = ring_plan()
        block = ctx.enter_context(nc.Block())

        def own(u, a, d):
            return a if u["by"] == "act" else d

        @block.sync
        def _(sync):
            w_mod_v = A["w_mod"].rearrange("l (k p) n -> l p k n", p=128)
            w_in_v = A["w_in"].rearrange("l (k p) n -> l p k n", p=128)
            w_br_v = A["w_br"].rearrange("l i (k p) n -> l (i k) p n", p=128)
            w_out_v = A["w_out"].rearrange("l (k p) n -> l p k n", p=128)
            experts = [A[n].rearrange("l e (k p) n -> l (e k) p n", p=128) for n in ("moe_w1", "moe_w3", "moe_w2")]

            def load(slot, use, src, shape_k):
                if not (isinstance(use, int) and use == 0):
                    sync.wait_ge(freed[slot], use)
                dst = ring[:, slot, :].rearrange("p (k n) -> p k n", k=shape_k)
                sync.dma_start(dst, src).then_inc(loaded[slot], 16)

            def load_mod(l, first, items):
                for n, (slot, use) in enumerate(items):
                    q = first + n
                    load(slot, use, w_mod_v[l, :, :, q * MC:(q + 1) * MC], KD)

            sync.dma_start(cst[:, :], A["cst"]).then_inc(consts_loaded, 16)
            sync.dma_start(stay[:, :], A["stay"]).then_inc(consts_loaded, 16)
            sync.dma_start(bm[:, :, :], A["b_mod"].rearrange("l (a b) -> a l b", b=MC)).then_inc(consts_loaded, 16)
            load_mod(0, 0, plan["M1", 0])
            sync.dma_start(x[:, 0:2, :], A["x"].rearrange("o (m p) d -> p (o m) d", p=128)).then_inc(consts_loaded, 16)
            sync.dma_start(x[:, 2:4, :], A["ctx"].rearrange("o (m p) d -> p (o m) d", p=128)).then_inc(consts_loaded, 16)
            for l in range(L):
                for q, (slot, use) in enumerate(plan["W", l]):
                    load(slot, use, w_in_v[l, :, :, q * MC:(q + 1) * MC], KD)
                base, per = plan["G", l]
                with sync.Fori(0, NBR) as i:
                    for h in range(2):
                        load(3 * h, base[3 * h] + i * per,
                             w_br_v[l, ds(i * 4, 4), :, h * 512:(h + 1) * 512].rearrange("k p n -> p k n"), 4)
                        for g in range(2):
                            s = 3 * h + 1 + g
                            load(s, base[s] + i * per,
                                 w_in_v[l, :, :, ds(i * D + (GATE_COL + (2 * h + g) * MC), MC)], KD)
                load_mod(l, 8, plan["M2", l])
                if l + 1 < L:
                    load_mod(l + 1, 0, plan["M1", l + 1])
                for q, (slot, use) in enumerate(plan["O", l]):
                    load(slot, use, w_out_v[l, :, 2 * q:2 * q + 2, :], 2)
                if l == L - 1:
                    sync.wait_ge(*sgu_sum.at(l, 4))
                    sync.dma_start(arena[:, 8, 0:D], A["final_g"]).then_inc(consts_loaded, 16)
                base, per = plan["E", l]
                G = GE[l]
                with sync.Fori(0, NP[l]) as i:
                    n = 0
                    for w in experts:
                        for j in range(4):
                            for g in range(G):
                                s = n % NSLOT
                                load(s, base[s] + (i * per + n // NSLOT),
                                     w[l, ds(i * (G * KD) + (g * KD + 2 * j), 2), :, :].rearrange("k p n -> p k n"), 2)
                                n += 1
            out_v = out.rearrange("o (m p) d -> p (o m) d", p=128)
            for m in range(2):
                sync.wait_ge(fin_ready, m + 1)
                sync.dma_start(out_v[:, m, :], hT[:, 2 * m:2 * m + 2, :].rearrange("p a b -> p (a b)")).then_inc(out_stored, 16)
            sync.wait_ge(out_stored, 32)

        @block.tensor
        def _(pe):
            def mm(o, a, b, first, last):
                return nc.tensor.matmul(o, a, b, start=first, stop=last)

            def take(slot, use):
                if isinstance(use, int):
                    pe.wait_ge(loaded[slot], 16 * (use + 1))
                else:
                    pe.wait_ge(loaded[slot], use * 16 + 16)

            def mod_section(l, norm, first, items, layer, done, cols_no, gates_done):
                cols_bank = 2 + norm
                gb = gates_done

                def post(n):
                    nonlocal gb
                    q = first + n
                    part = q // 4
                    pe.wait_ge(*mod_part.at(layer, done + n + 1))
                    if part % 3 == 2:
                        nb = 0 if part == 5 else None
                        for s in range(1 if part == 5 else streams(l)):
                            if gb - gates_done >= 2:
                                pe.wait_ge(*gate_rows.at(l, gate_wait[gb] ))
                            pick = (cst[:, C_SELY:C_SELY + 128] if streams(l) == 2 else cst[:, C_SELR:C_SELR + 128]) \
                                if part == 5 else cst[:, C_SELR + 128 * s:C_SELR + 128 * s + 128]
                            i = mm(PS[:, 4 + q % 4, s * MC:(s + 1) * MC], pick, modp[:, n % 2, :], True, True)
                        i.then_inc(gate_bc.sem, 1)
                        gb += 1
                    else:
                        for c in range(2):
                            col = 2 * ((part % 3) * KD + (q % 4) * 2 + c)
                            i = mm(PS[:, cols_bank, col:col + 2], modp[:, n % 2, c * 128:(c + 1) * 128],
                                   cst[:, C_SELC:C_SELC + 2], True, True)
                        if part % 3 == 1 and q % 4 == 3:
                            i.then_inc(mod_cols.sem, 1)

                for n, (slot, use) in enumerate(items):
                    q = first + n
                    take(slot, use)
                    if n >= 2:
                        pe.wait_ge(*mod_part.at(layer, done + n - 1))
                    for kk in range(2):
                        for j in range(4):
                            k = 4 * kk + j
                            i = nc.tensor.matmul(PS[32 * j:32 * j + 32, n % 2, 0:MC], cond[:, k, :],
                                                 ring[:, slot, k * MC:(k + 1) * MC],
                                                 start=(kk == 0), stop=(kk == 1 and j > 0),
                                                 tile_position=(0, 32 * j), skip_group_check=True)
                            if kk == 1 and j == 3:
                                i.then_inc(freed[slot], 1)
                    i = nc.tensor.matmul(PS[0:2, n % 2, 0:MC], cst[0:24, C_ID + q:C_ID + q + 1].broadcast_to([24, 2]),
                                         bm[:, l, :], start=False, stop=True, tile_position=(0, 0),
                                         skip_group_check=True)
                    i.then_inc(mod_sum.sem, 1)
                    if n >= 1:
                        post(n - 1)
                post(len(items) - 1)

            gate_wait = {4: 1, 5: 2, 6: 3, 7: 4, 2: 0, 3: 0}

            def transposes(nn, n_streams, xn):
                for s in range(n_streams):
                    pe.wait_ge(*xn_ready.at(nn, 2 * s + 2))
                    for kp in range(4):
                        for kk in range(2):
                            for j in range(2):
                                i = nc.tensor.transpose(PS[:, 4 * s + kp, kk * T + j * 128:kk * T + (j + 1) * 128],
                                                        xn[:, 2 * s + j, (2 * kp + kk) * 128:(2 * kp + kk + 1) * 128],
                                                        ident)
                        i.then_inc(xt_ready.sem, 1)

            pe.wait_ge(consts_loaded, 48)
            pe.wait_ge(cond_ready, 2)
            mod_section(0, 0, 0, plan["M1", 0], 0, 0, 0, 0)

            for l in range(L):
                NS, W_ALL = streams(l), 2 * T * 1
                tok = NS * T
                transposes(2 * l, 2, xn_mix)
                units, _ = WU[l]
                for uu in range(2):
                    pe.wait_ge(*hT_act.at(2 * l, 8))
                    pe.wait_ge(*hT_dve.at(2 * l, 8))
                    break
                for n, u in enumerate(units):
                    bank = n % 8
                    if n >= 8:
                        o = units[n - 8]
                        pe.wait_ge(*own(o, w_act, w_dve).at(l, o["nth"]))
                    if u["kind"] == "rope":
                        src = [v for v in units if v["name"] == u["name"] and v["kind"] == "f" and v["half"] == u["pair"]]
                        for v in src:
                            pe.wait_ge(*own(v, w_act, w_dve).at(l, v["nth"]))
                        for c in range(2):
                            i = mm(PS[:, bank, c * T:(c + 1) * T], cst[:, C_PERM:C_PERM + 128],
                                   region[u["name"]][:, 2 * u["pair"] + c, 0:T], True, True)
                        i.then_inc(w_sum.sem, 1)
                        continue
                    slot, use = plan["W", l][u["slot"]]
                    take(slot, use)
                    if u["kind"] == "f":
                        for k in range(KD):
                            i = mm(PS[:, bank, 0:u["tokens"]],
                                   ring[:, slot, k * MC + u["c"] * 128:k * MC + (u["c"] + 1) * 128],
                                   hT[:, k, 0:u["tokens"]], k == 0, k == KD - 1)
                            if k == KD - 1 and u["frees"]:
                                pass
                    else:
                        for j in range(2):
                            m = 2 * u["c"] + j
                            for k in range(KD):
                                i = mm(PS[:, bank, j * MC:(j + 1) * MC], hT[:, k, m * 128:(m + 1) * 128],
                                       ring[:, slot, k * MC:(k + 1) * MC], k == 0, k == KD - 1)
                    i.then_inc(w_sum.sem, 1)
                    if u["frees"]:
                        pe.wait_ge(*w_sum.at(l, n + 1))
                        pe.sem_inc(freed[slot], 1)
                last = {"act": 0, "dve": 0}
                for u in units:
                    last[u["by"]] = u["nth"]
                pe.wait_ge(*w_act.at(l, last["act"]))
                pe.wait_ge(*w_dve.at(l, last["dve"]))
                pe.wait_ge(par_loaded, 16 * (l + 1))
                pe.wait_ge(*v_norm.at(l, 2 * NS))
                for g in range(4):
                    for m in range(2 * NS):
                        i = mm(PS[:, g, m * 128:(m + 1) * 128], region["sv"][:, m, g * 128:(g + 1) * 128],
                               par[:, P_SGUW + g * 128:P_SGUW + (g + 1) * 128], True, True)
                    i.then_inc(sgu_sum.sem, 1)
                for g in range(4):
                    pe.wait_ge(*pooled.at(l, g + 1))
                    mm(PS[:, 4 + g, 0:tok], par[:, P_POOLW + g * 128:P_POOLW + (g + 1) * 128],
                       region["pz"][:, g, 0:tok], True, True).then_inc(pool_sum.sem, 1)
                pe.wait_ge(*sgu_out.at(l, 4))
                pe.wait_ge(*pool_out.at(l, 4))
                blocks, nb = BL[l], NB[l]
                tr, _ = TU[l]
                pe.wait_ge(*bias_masked.at(l, 1))

                def score(b):
                    kind, s, qt, h = blocks[b]
                    q, k = (region["dq"], region["dk"]) if kind == "diff" else (region["nq"], region["nk"])
                    k0, nk = (0, 2 * T) if s == 0 else (T, T)
                    if b >= 2:
                        pe.wait_ge(*exps.at(l, b - 1))
                    local = kind == "na" and s == 0
                    for a in range(2):
                        i = mm(PS[:, 2 * (b % 2) + a, 0:nk],
                               q[64 * a:64 * a + 64, h, s * T + qt * 128:s * T + (qt + 1) * 128],
                               k[64 * a:64 * a + 64, h, k0:k0 + nk], True, not local)
                    if local:
                        for a in range(2):
                            i = mm(PS[:, 2 * (b % 2) + a, 0:T], cst[:, C_FLIP:C_FLIP + 128],
                                   nab[:, 2 * h + a, (2 - 2 * qt) * 64:(2 - 2 * qt) * 64 + T], False, True)
                    i.then_inc(scores.sem, 1)

                def emptied(t):
                    if t >= 2:
                        o = tr[t - 2]
                        pe.wait_ge(*own(o, at_act, at_dve).at(l, o["nth"]))

                def turn(u):
                    b = u["b"]
                    kind, s, qt, h = blocks[b]
                    nkt = 4 if s == 0 else 2
                    if kind == "diff":
                        pe.wait_ge(*probs.at(l, b + 1))
                    else:
                        pe.wait_ge(*exps.at(l, b + 1))
                    emptied(u["t"])
                    for kt in range(nkt):
                        i = nc.tensor.transpose(PS[:, 4 + u["t"] % 2, kt * 128:(kt + 1) * 128],
                                                p_t[:, b % 2, u["a"], kt * 128:(kt + 1) * 128], ident)
                    i.then_inc(tr_made.sem, 1)

                def values(b):
                    kind, s, qt, h = blocks[b]
                    nkt, m0 = (4, 0) if s == 0 else (2, 2)
                    g = b // 4
                    if b % 4 == 0 and g >= 2:
                        pe.wait_ge(*o_norm.at(l, g - 1))
                    mine = [u for u in tr if u["kind"] == "p" and u["b"] == b]
                    for u in mine:
                        pe.wait_ge(*own(u, at_act, at_dve).at(l, u["nth"]))
                    for u in mine:
                        w = 128 // len(mine)
                        c = h * 128 + u["a"] * w
                        v = region["dv"] if kind == "diff" else region["nv"]
                        for kt in range(nkt):
                            i = mm(PS[:, 6 + g % 2, c:c + w], at[:, u["t"] % 2, kt * 128:(kt + 1) * 128],
                                   v[:, m0 + kt, c:c + w], kt == 0, kt == nkt - 1)
                    i.then_inc(pv.sem, 1)

                def turn_out(u):
                    pe.wait_ge(*o_norm.at(l, u["g"] + 1))
                    emptied(u["t"])
                    for c in range(4):
                        i = nc.tensor.transpose(PS[:, 4 + u["t"] % 2, c * 128:(c + 1) * 128],
                                                on[:, c * 128:(c + 1) * 128], ident)
                    i.then_inc(tr_made.sem, 1)

                queue = list(tr)
                for i_ in range(nb + 6):
                    if i_ < nb:
                        score(i_)
                    while queue and queue[0]["kind"] == "p" and queue[0]["b"] == i_ - 1:
                        turn(queue.pop(0))
                    if 0 <= i_ - 2 < nb:
                        values(i_ - 2)
                    if queue and queue[0]["kind"] == "o" and 4 * queue[0]["g"] + 7 == i_:
                        turn_out(queue.pop(0))
                assert not queue
                pe.wait_ge(*at_act.at(l, TU[l][1]["act"]))

                base, per = plan["G", l]
                pe.wait_ge(*merged.at(l, 2))
                with pe.Fori(0, NBR) as i:
                    for v in range(8):
                        h, g, c = v // 4, (v // 2) % 2, v % 2
                        sb_, sg_ = 3 * h, 3 * h + 1 + g
                        if v % 4 == 0:
                            take(sb_, i * per + base[sb_])
                        if c == 0:
                            take(sg_, i * per + base[sg_])
                        sem, val = merged.at(l, 2 + v - 1)
                        pe.wait_ge(sem, i * 8 + val)
                        for k in range(KD):
                            ins = mm(PS[:, v % 2, 0:tok], ring[:, sg_, k * MC + c * 128:k * MC + (c + 1) * 128],
                                     hT[:, k, 0:tok], k == 0, k == KD - 1)
                        ins.then_inc(gates.sem, 1)
                        for k in range(4):
                            ins = mm(PS[:, 2 + v % 2, 0:tok],
                                     ring[:, sb_, k * 512 + (2 * g + c) * 128:k * 512 + (2 * g + c + 1) * 128],
                                     branches[:, ds(i * 2048 + k * 512, tok)], k == 0, k == 3)
                        ins.then_inc(projs.sem, 1)
                        if c == 1:
                            sem, val = projs.at(l, v + 1)
                            pe.wait_ge(sem, i * 8 + val)
                            pe.sem_inc(freed[sg_], 1)
                            if v % 4 == 3:
                                pe.sem_inc(freed[sb_], 1)
                pe.wait_ge(*merged.at(l, 2 + 8 * NBR))

                mod_section(l, 1, 8, plan["M2", l], l, 8 if l == 0 else 0, 0, 0)
                if l + 1 < L:
                    mod_section(l + 1, 0, 0, plan["M1", l + 1], 0, 24, 0, 0)
                pe.wait_ge(*mod_ready.at(l, 3 if l == 0 else 1))
                pe.wait_ge(*gate_rows.at(l, 8))
                for q, (slot, use) in enumerate(plan["O", l]):
                    take(slot, use)
                    for kk in range(2):
                        k = 2 * q + kk
                        for m in range(NT[l]):
                            for n in range(2):
                                i = mm(PS[:, 2 * m + n, :], mT[:, k, m * 128:(m + 1) * 128],
                                       ring[:, slot, kk * D + n * 512:kk * D + (n + 1) * 512], k == 0, k == KD - 1)
                                if k == KD - 1:
                                    i.then_inc(mix_sum.sem, 1)
                                elif kk == 1 and m == NT[l] - 1 and n == 1:
                                    i.then_inc(freed[slot], 1)
                pe.wait_ge(*mix_sum.at(l, 2 * NT[l]))
                pe.sem_inc(freed[plan["O", l][3][0]], 1)
                pe.wait_ge(*mix_x.at(l, 2 * NT[l]))
                transposes(2 * l + 1, NS, xn_moe)
                pe.wait_ge(*hT_act.at(2 * l + 1, 4 * NS))
                pe.wait_ge(*hT_dve.at(2 * l + 1, 4 * NS))
                for m in range(NT[l]):
                    for k in range(KD):
                        i = mm(PS[:, 0, m * E:(m + 1) * E], hT[:, k, m * 128:(m + 1) * 128],
                               par[:, P_RW + k * E:P_RW + (k + 1) * E], k == 0, k == KD - 1)
                i.then_inc(logits.sem, 1)
                pe.wait_ge(*aff_ready.at(l, 1))
                for j in range(2):
                    i = nc.tensor.transpose(PS[0:NS * E, 1, j * 128:(j + 1) * 128],
                                            aff[:, j, 0:NS, :].rearrange("p a b -> p (a b)"), ident)
                i.then_inc(affT_made.sem, 1)
                pe.wait_ge(*mask_ready.at(l, 1))
                for j in range(2):
                    i = nc.tensor.transpose(PS[:, 2, j * 32:j * 32 + NS * E], afR[0:NS * E, 0, j * 128:(j + 1) * 128],
                                            cst[0:NS * E, C_ID:C_ID + NS * E])
                i.then_inc(maskT_made.sem, 1)
                pe.wait_ge(*maskT_ready.at(l, 1))
                mm(PS[:, 3, 0:NS * E], cst[:, C_TRI:C_TRI + 128], msk[:, 0, 0:NS * E], True, True)
                mm(PS[:, 3, 32:32 + NS * E], cst[:, C_ONE:C_ONE + 128], msk[:, 0, 0:NS * E], True, False)
                mm(PS[:, 3, 32:32 + NS * E], cst[:, C_TRI:C_TRI + 128], msk[:, 1, 0:NS * E], False, True)\
                    .then_inc(count_made.sem, 1)
                G, R = GE[l], CAP * NS
                base, per = plan["E", l]
                with pe.Fori(0, NP[l]) as i:
                    def when(sig, n, k):
                        sem, val = sig.at(l, k)
                        pe.wait_ge(sem, i * n + val)

                    when(sel_ready, NS, NS)
                    for bk in range(2):
                        for k4 in range(4):
                            k = 4 * bk + k4
                            for s in range(NS):
                                o = PS[:, 6 + bk, k4 * 128:(k4 + 1) * 128].rearrange(
                                    "p (g s c) -> p g s c", g=G, s=NS)[:, :, s, :]
                                for j in range(2):
                                    m = 2 * s + j
                                    ins = mm(o, xn_moe[:, m, k * 128:(k + 1) * 128],
                                             selp[:, m * G * CAP:(m + 1) * G * CAP].rearrange("p (g c) -> p g c", g=G),
                                             j == 0, j == 1)
                        ins.then_inc(gathered.sem, 1)
                    when(selg_ready, NS, NS)
                    for m in range(NT[l]):
                        ins = nc.tensor.transpose(PS[:, 4, m * 128:(m + 1) * 128], selg[:, m, :], ident)
                    ins.then_inc(combT_made.sem, 1)
                    when(xs_ready, 2 * NS, 2 * NS)
                    n = 0
                    for w, (bank, done) in enumerate(((0, h1_sum), (2, h3_sum), (4, y_sum))):
                        src = xsT if w < 2 else hidT
                        if w == 2:
                            when(hid_ready, 2, 2)
                            for bk in range(2):
                                for k4 in range(4):
                                    k = 4 * bk + k4
                                    ins = nc.tensor.transpose(PS[:, 6 + bk, k4 * 128:(k4 + 1) * 128],
                                                              hid[:, k * 128:(k + 1) * 128], ident)
                                ins.then_inc(hidT_made.sem, 1)
                            when(combT_ready, 1, 1)
                            when(hidT_act, 1, 1)
                            when(hidT_dve, 1, 1)
                        for j in range(4):
                            for g in range(G):
                                s = (n + g) % NSLOT
                                take(s, i * per + (base[s] + (n + g) // NSLOT))
                            for kk in range(2):
                                k = 2 * j + kk
                                for h in range(2):
                                    for g in range(G):
                                        s = (n + g) % NSLOT
                                        ins = nc.tensor.matmul(
                                            PS[g * R:(g + 1) * R, bank + h, :], src[:, k, g * R:(g + 1) * R],
                                            ring[:, s, kk * D + h * 512:kk * D + (h + 1) * 512],
                                            start=(k == 0), stop=(k == KD - 1), tile_position=(0, g * R))
                                        if kk == 1 and h == 1 and not (j == 3 and g == G - 1):
                                            ins.then_inc(freed[s], 1)
                            n += G
                        ins.then_inc(done.sem, 1)
                        sem, val = done.at(l, 1)
                        pe.wait_ge(sem, i * 1 + val)
                        pe.sem_inc(freed[(n - 1) % NSLOT], 1)
                    when(y_ready, 2, 2)
                    for c in range(2 * NT[l]):
                        m, h = c // 2, c % 2
                        if c >= 4:
                            when(comb_x, 2 * NT[l], c - 3)
                        mm(PS[:, c % 4, :], combT[:, m, :], ysb[:, h * 512:(h + 1) * 512], True, True)\
                            .then_inc(comb_sum.sem, 1)
                pe.wait_ge(*comb_x.at(l, 2 * NT[l] * NP[l]))

        @block.scalar
        def _(act):
            act.wait_ge(consts_loaded, 48)
            act.wait_ge(cond_ready, 1)
            nc.scalar.activation(cond[:, :, 0:2], stay[:, S_C:S_C + 16].rearrange("p (s k) -> p k s", s=2),
                                 ACT.Silu).then_inc(cond_ready, 1)

            def gate_parts(l):
                for n in range(8):
                    act.wait_ge(*gate_bc.at(l, n + 1))
                    q = n % 4
                    if n < 4:
                        nc.scalar.activation(g1b[:, 0:streams(l), q * MC:(q + 1) * MC],
                                             PS[:, 4 + q, 0:streams(l) * MC].rearrange("p (s c) -> p s c", c=MC),
                                             ACT.Copy).then_inc(gate_rows.sem, 1)
                    else:
                        nc.scalar.activation(g2r[:, q * MC:(q + 1) * MC], PS[:, 4 + q, 0:MC],
                                             ACT.Copy).then_inc(gate_rows.sem, 1)

            def squares(nn, n_streams):
                for m in range(2 * n_streams):
                    nc.scalar.activation(sq_junk, x[:, m, :], ACT.Square, accum_out=ss[:, m:m + 1])\
                        .then_inc(sq_done.sem, 1)
                    act.wait_ge(*sq_done.at(nn, m + 1))

            def modulate(nn, norm, n_streams):
                for s in range(n_streams):
                    for kp in (0, 2):
                        act.wait_ge(*xt_ready.at(nn, 4 * s + kp + 1))
                        for kk in range(2):
                            k = 2 * kp + kk
                            nc.scalar.activation(hT[:, k, s * T:(s + 1) * T], PS[:, 4 * s + kp, kk * T:(kk + 1) * T],
                                                 ACT.Identity, bias=modB[:, norm, s, k:k + 1],
                                                 scale=modA[:, norm, s, k:k + 1]).then_inc(hT_act.sem, 1)

            act.wait_ge(consts_loaded, 80)
            for l in range(L):
                NS = streams(l)
                tok = NS * T
                if l:
                    act.wait_ge(*comb_x.at(l - 1, 2 * NT[l - 1] * NP[l - 1]))
                squares(2 * l, 2)
                act.wait_ge(*mod_ready.at(0, 1 if l == 0 else 3))
                modulate(2 * l, 0, 2)
                act.wait_ge(*lam_prod.at(l, 1))
                nc.scalar.activation(lam[:, 2:4], lam[:, 0:2], ACT.Exp).then_inc(lam_exp.sem, 1)
                for n, u in enumerate(WU[l][0]):
                    if u["by"] != "act":
                        continue
                    act.wait_ge(*w_sum.at(l, n + 1))
                    dst = region[u["name"]]
                    if u["kind"] == "f":
                        ch, w = 2 * u["half"] + u["c"], u["tokens"]
                        o, i_ = dst[:, ch, 0:w], PS[:, n % 8, 0:w]
                    else:
                        o = dst[:, 2 * u["c"]:2 * u["c"] + 2, u["half"] * MC:(u["half"] + 1) * MC]
                        i_ = PS[:, n % 8, :].rearrange("p (a b) -> p a b", a=2)
                    if u["name"] in ("su", "sv"):
                        nc.scalar.activation(o, i_, ACT.Gelu_apprx_tanh).then_inc(w_act.sem, 1)
                    elif u["name"] in ("dq", "nq"):
                        nc.scalar.activation(o, i_, ACT.Copy, scale=0.125).then_inc(w_act.sem, 1)
                    else:
                        nc.scalar.activation(o, i_, ACT.Copy).then_inc(w_act.sem, 1)
                for g in range(4):
                    act.wait_ge(*pool_sum.at(l, g + 1))
                    nc.scalar.activation(region["pz"][:, g, 0:tok], PS[:, 4 + g, 0:tok], ACT.Copy,
                                         scale=par[:, P_PSC + g:P_PSC + g + 1]).then_inc(pool_out.sem, 1)
                blocks, nb = BL[l], NB[l]
                tr = list(TU[l][0])
                for i_ in range(nb + 6):
                    if i_ < nb:
                        kind, s, qt, h = blocks[i_]
                        nk = 2 * T if s == 0 else T
                        act.wait_ge(*maxes.at(l, i_ + 1))
                        if i_ >= 2:
                            t_last = max(u["t"] for u in TU[l][0] if u["kind"] == "p" and u["b"] == i_ - 2)
                            act.wait_ge(*tr_made.at(l, t_last + 1))
                        for a in range(2):
                            ins = nc.scalar.activation(p_t[:, i_ % 2, a, 0:nk], PS[:, 2 * (i_ % 2) + a, 0:nk], ACT.Exp,
                                                       bias=nmx[:, i_ % 2, a:a + 1],
                                                       accum_out=rs[:, i_ % 2, a:a + 1])
                        ins.then_inc(exps.sem, 1)
                    while tr and ((tr[0]["kind"] == "p" and tr[0]["b"] == i_ - 1)
                                  or (tr[0]["kind"] == "o" and 4 * tr[0]["g"] + 7 == i_)):
                        u = tr.pop(0)
                        if u["by"] != "act":
                            continue
                        act.wait_ge(*tr_made.at(l, u["t"] + 1))
                        bank = PS[:, 4 + u["t"] % 2, :]
                        if u["kind"] == "p":
                            b = u["b"]
                            nkt = 4 if blocks[b][1] == 0 else 2
                            prev = [v for v in TU[l][0] if v["t"] in (u["t"] - 2, u["t"] - 1) and v["kind"] == "p"
                                    and v["b"] < b and v["t"] % 2 == u["t"] % 2]
                            for v in prev:
                                act.wait_ge(*pv.at(l, v["b"] + 1))
                            nc.scalar.activation(at[:, u["t"] % 2, 0:nkt * 128], bank[:, 0:nkt * 128], ACT.Copy)\
                                .then_inc(at_act.sem, 1)
                        else:
                            kind, s, qt, _ = blocks[4 * u["g"]]
                            dst = region["dq" if kind == "diff" else "nq"][:, :, s * T + qt * 128:s * T + (qt + 1) * 128]
                            src = bank.rearrange("p (a b) -> p a b", a=4)
                            if kind == "diff":
                                act.wait_ge(*lam_ready.at(l, 1))
                                nc.scalar.activation(dst, src, ACT.Copy, scale=subg).then_inc(at_act.sem, 1)
                            else:
                                nc.scalar.activation(dst, src, ACT.Copy).then_inc(at_act.sem, 1)
                    g = (i_ - 5) // 4
                    if (i_ - 5) % 4 == 0 and 0 <= g < NG[l] and blocks[4 * g][0] == "diff":
                        act.wait_ge(*pv.at(l, 4 * g + 4))
                        if g >= 1:
                            act.wait_ge(*o_ss.at(l, g))
                        nc.scalar.activation(osq, PS[:, 6 + g % 2, :], ACT.Square).then_inc(o_square.sem, 1)
                with act.Fori(0, NBR) as i:
                    for v in range(8):
                        sem, val = gates.at(l, v + 1)
                        act.wait_ge(sem, i * 8 + val)
                        sem, val = merged.at(l, 2 + v - 1)
                        act.wait_ge(sem, i * 8 + val)
                        nc.scalar.activation(sgt[:, v % 2, 0:tok], PS[:, v % 2, 0:tok], ACT.Sigmoid)\
                            .then_inc(sigs.sem, 1)
                gate_parts(l)
                act.wait_ge(*mix_x.at(l, 2 * NT[l]))
                squares(2 * l + 1, NS)
                act.wait_ge(*mod_ready.at(l, 2 if l == 0 else 1))
                modulate(2 * l + 1, 1, NS)
                act.wait_ge(*r_max.at(l, 1))
                for m in range(NT[l]):
                    nc.scalar.activation(rex[:, m, :], PS[:, 0, m * E:(m + 1) * E], ACT.Exp, bias=rmx[:, m:m + 1],
                                         accum_out=rsum[:, m:m + 1]).then_inc(r_exp.sem, 1)
                with act.Fori(0, NP[l]) as i:
                    def when(sig, n, k):
                        sem, val = sig.at(l, k)
                        act.wait_ge(sem, i * n + val)

                    when(combT_made, 1, 1)
                    nc.scalar.activation(combT[:, 0:NT[l], :].rearrange("p a b -> p (a b)"), PS[:, 4, 0:NT[l] * 128],
                                         ACT.Copy).then_inc(combT_ready.sem, 1)
                    when(h1_sum, 1, 1)
                    for h in range(2):
                        nc.scalar.activation(sil[:, h * 512:(h + 1) * 512], PS[:, h, :], ACT.Silu)\
                            .then_inc(sil_ready.sem, 1)
                    when(hidT_made, 2, 1)
                    nc.scalar.activation(hidT[:, 0:4, :].rearrange("p a b -> p (a b)"), PS[:, 6, :], ACT.Copy)\
                        .then_inc(hidT_act.sem, 1)
            act.wait_ge(*comb_x.at(L - 1, 2 * NT[L - 1] * NP[L - 1]))
            squares(4, 1)

        @block.gpsimd
        def _(pool):
            steps = [0]

            def step(ins):
                steps[0] += 1
                ins.then_inc(pool_step, 1)
                pool.wait_ge(pool_step, steps[0])

            rpb_v = A["na_rpb"]

            def load_layer(l):
                pool.dma_start(par[:, :], A["par"][l]).then_inc(par_loaded, 16)
                for h in range(8):
                    for r in range(2):
                        start = ((l * 8 + h) * RPB_R + (RPB_R // 2 - 3)) * RPB_C + RPB_C * r + RPB_C // 2 - 63
                        src = bass.AP(tensor=rpb_v.tensor, offset=rpb_v.offset + start,
                                      ap=[[1, 64], [RPB_C, 6], [1, GRID_W]])
                        pool.dma_start(nab[64 * r:64 * r + 64, h, :].rearrange("p (i c) -> p i c", i=6), src)\
                            .then_inc(bias_loaded, 16)

            def inverse_root(sq, mean, root, n, scale, ready, first=None):
                step(pool.tensor_scalar(mean[:, 0:n], sq, scale, EPS, ALU.mult, ALU.add))
                pool.tensor_tensor(root[:, 0:n], mean[:, 0:n], half[:, 0:n], ALU.pow).then_inc(ready, 1)

            pool.memset(half, -0.5).then_inc(half_ready, 1)
            pool.memset(cond[:, :, :], 0.0).then_inc(cond_ready, 1)
            pool.wait_ge(half_ready, 1)
            for l in range(L):
                NS = streams(l)
                if l:
                    pool.wait_ge(*logits.at(l - 1, 1))
                load_layer(l)
                pool.wait_ge(*sq_done.at(2 * l, 4))
                inverse_root(ss[:, 0:4], ms, rstd, 4, 1.0 / D, rstd_done.sem)
                pool.wait_ge(bias_loaded, 16 * 16 * (l + 1))
                pool.wait_ge(consts_loaded, 48)
                tb = nab[:, :, :].rearrange("p h (i c) -> p (h i) c", c=GRID_W)
                pool.tensor_tensor(tb, tb, cst[:, C_MASK:C_MASK + GRID_W].unsqueeze(1).broadcast_to([128, 48, GRID_W]),
                                   ALU.add).then_inc(bias_masked.sem, 1)
                pool.wait_ge(*v_stats.at(l, 1))
                inverse_root(vmv[:, 0:2 * NS, 1], vms, vrstd, 2 * NS, 1.0, v_rstd.sem)
                for g in range(NG[l] // 2):
                    pool.wait_ge(*o_ss.at(l, g + 1))
                    inverse_root(oss[:, 0:4], oms, orstd, 4, 1.0 / 128, o_rstd.sem)
                pool.wait_ge(*sq_done.at(2 * l + 1, 2 * NS))
                inverse_root(ss[:, 0:2 * NS], ms, rstd, 2 * NS, 1.0 / D, rstd_done.sem)
            pool.wait_ge(*sq_done.at(4, 2))
            inverse_root(ss[:, 0:2], ms, rstd, 2, 1.0 / D, rstd_done.sem)

        @block.vector
        def _(dve):
            steps = [0]

            def step(ins):
                steps[0] += 1
                ins.then_inc(dve_step, 1)
                dve.wait_ge(dve_step, steps[0])

            def mod_section(l, norm, first, n_items, layer, done, sec):
                for n in range(n_items):
                    dve.wait_ge(*mod_sum.at(layer, done + n + 1))
                    q = first + n
                    nc.vector.tensor_copy(modp[:, n % 2, :], PS[:, n % 2, 0:MC]).then_inc(mod_part.sem, 1)
                dve.wait_ge(*mod_cols.at(layer, sec))
                cols = PS[:, 2 + norm, 0:4 * KD].rearrange("p (a k s) -> p a s k", a=2, s=2)
                gain = stay[:, (S_N1 if norm == 0 else S_N2) + KD * l:(S_N1 if norm == 0 else S_N2) + KD * (l + 1)]
                step(nc.vector.tensor_scalar(modA[:, norm, :, :], cols[:, 1, :, :], 1.0, None, ALU.add))
                for s in range(2):
                    step(nc.vector.tensor_tensor(modA[:, norm, s, :], modA[:, norm, s, :], gain, ALU.mult))
                nc.vector.tensor_copy(modB[:, norm, :, :], cols[:, 0, :, :]).then_inc(mod_ready.sem, 1)

            def normalise(nn, n_streams, xn):
                dve.wait_ge(*rstd_done.at(nn, 1))
                for m in range(2 * n_streams):
                    nc.vector.tensor_scalar(xn[:, m, :], x[:, m, :], rstd[:, m:m + 1], None, ALU.mult)\
                        .then_inc(xn_ready.sem, 1)

            def modulate(nn, norm, n_streams):
                for s in range(n_streams):
                    for kp in (1, 3):
                        dve.wait_ge(*xt_ready.at(nn, 4 * s + kp + 1))
                        for kk in range(2):
                            k = 2 * kp + kk
                            nc.vector.tensor_scalar(hT[:, k, s * T:(s + 1) * T], PS[:, 4 * s + kp, kk * T:(kk + 1) * T],
                                                    modA[:, norm, s, k:k + 1], modB[:, norm, s, k:k + 1],
                                                    ALU.mult, ALU.add).then_inc(hT_dve.sem, 1)

            dve.wait_ge(consts_loaded, 48)
            mod_section(0, 0, 0, 8, 0, 0, 1)
            dve.wait_ge(consts_loaded, 80)
            for l in range(L):
                NS = streams(l)
                tok = NS * T
                lam_init = 0.8 - 0.6 * math.exp(-0.3 * l)
                normalise(2 * l, 2, xn_mix)
                modulate(2 * l, 0, 2)
                dve.wait_ge(par_loaded, 16 * (l + 1))
                lp = par[:, P_LAM:P_LAM + 256].rearrange("p (a b c) -> p a b c", a=2, b=2)
                lt = work[:, 7, 0:128].rearrange("p (a c) -> p a c", a=2)
                step(nc.vector.tensor_tensor(lt, lp[:, :, 0, :], lp[:, :, 1, :], ALU.mult))
                nc.vector.reduce_sum(lam[:, 0:2], lt, axis=AX.X).then_inc(lam_prod.sem, 1)
                dve.wait_ge(*lam_exp.at(l, 1))
                step(nc.vector.tensor_tensor(lam[:, 4:5], lam[:, 3:4], lam[:, 2:3], ALU.subtract))
                step(nc.vector.tensor_scalar(lam[:, 5:6], lam[:, 4:5], -lam_init, None, ALU.add))
                nc.vector.tensor_scalar(subg, par[:, P_SUBG:P_SUBG + 1], 1.0 - lam_init, None, ALU.mult)\
                    .then_inc(lam_ready.sem, 1)
                for n, u in enumerate(WU[l][0]):
                    if u["by"] != "dve":
                        continue
                    dve.wait_ge(*w_sum.at(l, n + 1))
                    dst = region[u["name"]]
                    if u["kind"] == "rope":
                        two = dst[:, 2 * u["pair"]:2 * u["pair"] + 2, 0:T]
                        turned = work[:, 0, :].rearrange("p (a b) -> p a b", a=2)
                        for c in range(2):
                            step(nc.vector.tensor_tensor(turned[:, c, :], PS[:, n % 8, c * T:(c + 1) * T], sinT, ALU.mult))
                            step(nc.vector.tensor_tensor(two[:, c, :], two[:, c, :], cosT, ALU.mult))
                        nc.vector.tensor_tensor(two, two, turned, ALU.add).then_inc(w_dve.sem, 1)
                        dve.wait_ge(*w_dve.at(l, u["nth"]))
                        continue
                    if u["kind"] == "f":
                        ch, w = 2 * u["half"] + u["c"], u["tokens"]
                        o, i_ = dst[:, ch, 0:w], PS[:, n % 8, 0:w]
                    else:
                        o = dst[:, 2 * u["c"]:2 * u["c"] + 2, u["half"] * MC:(u["half"] + 1) * MC]
                        i_ = PS[:, n % 8, :].rearrange("p (a b) -> p a b", a=2)
                    if u["name"] in ("dq", "nq"):
                        nc.vector.tensor_scalar(o, i_, 0.125, None, ALU.mult).then_inc(w_dve.sem, 1)
                    else:
                        nc.vector.tensor_copy(o, i_).then_inc(w_dve.sem, 1)
                last_pz = {"act": 0, "dve": 0}
                for u in WU[l][0]:
                    if u["name"] == "pz":
                        last_pz[u["by"]] = u["nth"]
                dve.wait_ge(*w_act.at(l, last_pz["act"]))
                dve.wait_ge(*w_dve.at(l, last_pz["dve"]))
                PW = T + 16
                za, zb = (work[:, 2 * i_:2 * i_ + 2, :].rearrange("p a b -> p (a b)")[:, 0:2 * PW].rearrange(
                    "p (s t) -> p s t", s=2) for i_ in (0, 1))
                for g, w in enumerate(POOL_W):
                    z = region["pz"][:, g, 0:tok].rearrange("p (s t) -> p s t", s=NS)
                    step(nc.vector.memset(za[:, 0:NS, 0:8], 0.0))
                    step(nc.vector.memset(za[:, 0:NS, T + 8:PW], 0.0))
                    step(nc.vector.tensor_copy(za[:, 0:NS, 8:8 + T], z))
                    cur, nxt, n, span = za, zb, PW, 1
                    while span < w:
                        n -= span
                        step(nc.vector.tensor_tensor(nxt[:, 0:NS, 0:n], cur[:, 0:NS, 0:n], cur[:, 0:NS, span:span + n],
                                                     ALU.add))
                        cur, nxt, span = nxt, cur, 2 * span
                    cnt = cst[:, C_CNT + g * T:C_CNT + (g + 1) * T].unsqueeze(1).broadcast_to([128, NS, T])
                    step(nc.vector.tensor_tensor(nxt[:, 0:NS, 0:T], cur[:, 0:NS, 8 - w // 2:8 - w // 2 + T], cnt, ALU.mult))
                    nc.vector.tensor_tensor(z, nxt[:, 0:NS, 0:T], z, ALU.subtract).then_inc(pooled.sem, 1)
                    dve.wait_ge(*pooled.at(l, g + 1))
                dve.wait_ge(*w_act.at(l, WU[l][1]["act"]))
                v_ = region["sv"]
                for m in range(2 * NS):
                    step(nc.vector.bn_stats(vst[:, m, :], v_[:, m, :]))
                    ins = nc.vector.bn_aggr(vmv[:, m, :], vst[:, m, :])
                    if m < 2 * NS - 1:
                        step(ins)
                ins.then_inc(v_stats.sem, 1)
                dve.wait_ge(*v_rstd.at(l, 1))
                for m in range(2 * NS):
                    nc.vector.tensor_scalar(v_[:, m, :], v_[:, m, :], vmv[:, m, 0:1], vrstd[:, m:m + 1],
                                            ALU.subtract, ALU.mult).then_inc(v_norm.sem, 1)
                for g in range(4):
                    dve.wait_ge(*sgu_sum.at(l, g + 1))
                    f_ = PS[:, g, 0:tok].rearrange("p (m q) -> p m q", q=128)
                    b_ = par[:, P_SGUB + g * 128:P_SGUB + (g + 1) * 128].unsqueeze(1).broadcast_to([128, 2 * NS, 128])
                    t_ = work[:, 4 + g % 2, 0:tok]
                    step(nc.vector.scalar_tensor_tensor(out=t_.rearrange("p (m q) -> p m q", q=128), in0=f_,
                                                        scalar=par[:, P_SGUG + g:P_SGUG + g + 1], in1=b_,
                                                        op0=ALU.mult, op1=ALU.add))
                    u_ = region["su"][:, g, 0:tok]
                    nc.vector.tensor_tensor(u_, u_, t_, ALU.mult).then_inc(sgu_out.sem, 1)
                    dve.wait_ge(*sgu_out.at(l, g + 1))
                dve.wait_ge(*sgu_out.at(l, 4))
                blocks, nb = BL[l], NB[l]
                tr = list(TU[l][0])
                for i_ in range(nb + 6):
                    if i_ < nb:
                        s = blocks[i_][1]
                        nk = 2 * T if s == 0 else T
                        dve.wait_ge(*scores.at(l, i_ + 1))
                        if i_ >= 2:
                            dve.wait_ge(*exps.at(l, i_ - 1))
                        nc.vector.reduce_max(nmx[:, i_ % 2, :], PS[:, 2 * (i_ % 2):2 * (i_ % 2) + 2, 0:nk], axis=AX.X,
                                             negate=True).then_inc(maxes.sem, 1)
                    b = i_ - 1
                    if 0 <= b < nb:
                        kind, s, qt, h = blocks[b]
                        nk = 2 * T if s == 0 else T
                        dve.wait_ge(*exps.at(l, b + 1))
                        if kind == "diff":
                            r_ = rr[:, b % 2, :]
                            step(nc.vector.reciprocal(r_, rs[:, b % 2, :]))
                            step(nc.vector.tensor_tensor(r_[:, 1:2], r_[:, 1:2], lam[:, 5:6], ALU.mult))
                            step(nc.vector.tensor_scalar(p_t[:, b % 2, 0, 0:nk], p_t[:, b % 2, 0, 0:nk], r_[:, 0:1], None,
                                                         ALU.mult))
                            nc.vector.scalar_tensor_tensor(out=p_t[:, b % 2, 0, 0:nk], in0=p_t[:, b % 2, 1, 0:nk],
                                                           scalar=r_[:, 1:2], in1=p_t[:, b % 2, 0, 0:nk],
                                                           op0=ALU.mult, op1=ALU.add).then_inc(probs.sem, 1)
                        else:
                            nc.vector.reciprocal(nar[:, (b // 4) % 4, 2 * h:2 * h + 2], rs[:, b % 2, :])\
                                .then_inc(probs.sem, 1)
                    while tr and ((tr[0]["kind"] == "p" and tr[0]["b"] == i_ - 1)
                                  or (tr[0]["kind"] == "o" and 4 * tr[0]["g"] + 7 == i_)):
                        u = tr.pop(0)
                        if u["by"] != "dve":
                            continue
                        nkt = 4 if blocks[u["b"]][1] == 0 else 2
                        dve.wait_ge(*tr_made.at(l, u["t"] + 1))
                        if u["b"] >= 1:
                            dve.wait_ge(*pv.at(l, u["b"]))
                        nc.vector.tensor_copy(at[:, u["t"] % 2, 0:nkt * 128], PS[:, 4 + u["t"] % 2, 0:nkt * 128])\
                            .then_inc(at_dve.sem, 1)
                    g = (i_ - 5) // 4
                    if (i_ - 5) % 4 == 0 and 0 <= g < NG[l]:
                        kind = blocks[4 * g][0]
                        o_ = PS[:, 6 + g % 2, :]
                        if g >= 1:
                            t_o = [u["t"] for u in TU[l][0] if u["kind"] == "o" and u["g"] == g - 1][0]
                            dve.wait_ge(*tr_made.at(l, t_o + 1))
                        if kind == "diff":
                            dve.wait_ge(*o_square.at(l, g + 1))
                            nc.vector.reduce_sum(oss, osq.rearrange("p (a b) -> p a b", a=4), axis=AX.X)\
                                .then_inc(o_ss.sem, 1)
                            dve.wait_ge(*o_rstd.at(l, g + 1))
                            nc.vector.tensor_tensor(on.rearrange("p (a b) -> p a b", a=4),
                                                    o_.rearrange("p (a b) -> p a b", a=4),
                                                    orstd.unsqueeze(2).broadcast_to([128, 4, 128]), ALU.mult)\
                                .then_inc(o_norm.sem, 1)
                        else:
                            dve.wait_ge(*pv.at(l, 4 * g + 4))
                            dve.wait_ge(*probs.at(l, 4 * g + 4))
                            nc.vector.tensor_tensor(on.rearrange("p (a b) -> p a b", a=8),
                                                    o_.rearrange("p (a b) -> p a b", a=8),
                                                    nar[:, g % 4, :].unsqueeze(2).broadcast_to([128, 8, 64]), ALU.mult)\
                                .then_inc(o_norm.sem, 1)
                dve.wait_ge(*at_act.at(l, TU[l][1]["act"]))
                dve.wait_ge(*pv.at(l, nb))
                for h in range(2):
                    nc.vector.memset(mT[:, 4 * h:4 * h + 4, 0:tok], 0.0).then_inc(merged.sem, 1)
                dve.wait_ge(*merged.at(l, 2))
                with dve.Fori(0, NBR) as i:
                    for v in range(8):
                        for sig in (sigs, projs):
                            sem, val = sig.at(l, v + 1)
                            dve.wait_ge(sem, i * 8 + val)
                        nc.vector.tensor_tensor(gtmp[:, v % 2, 0:tok], sgt[:, v % 2, 0:tok], PS[:, 2 + v % 2, 0:tok],
                                                ALU.mult).then_inc(gated.sem, 1)
                        sem, val = gated.at(l, v + 1)
                        dve.wait_ge(sem, i * 8 + val)
                        nc.vector.tensor_tensor(mT[:, v, 0:tok], mT[:, v, 0:tok], gtmp[:, v % 2, 0:tok], ALU.add)\
                            .then_inc(merged.sem, 1)
                mod_section(l, 1, 8, 16, l, 8 if l == 0 else 0, 2 if l == 0 else 1)
                if l + 1 < L:
                    mod_section(l + 1, 0, 0, 8, 0, 24, 3)
                dve.wait_ge(*gate_rows.at(l, 8))
                for c in range(2 * NT[l]):
                    m, h = c // 2, c % 2
                    dve.wait_ge(*mix_sum.at(l, c + 1))
                    t_ = work[:, 2 + c % 2, :]
                    step(nc.vector.tensor_tensor(t_, PS[:, c, :], g1b[:, m // 2, h * 512:(h + 1) * 512], ALU.mult))
                    nc.vector.tensor_tensor(x[:, m, h * 512:(h + 1) * 512], x[:, m, h * 512:(h + 1) * 512], t_, ALU.add)\
                        .then_inc(mix_x.sem, 1)
                dve.wait_ge(*mix_x.at(l, 2 * NT[l]))
                normalise(2 * l + 1, NS, xn_moe)
                modulate(2 * l + 1, 1, NS)
                dve.wait_ge(*logits.at(l, 1))
                nc.vector.reduce_max(rmx[:, 0:NT[l]], PS[:, 0, 0:NT[l] * E].rearrange("p (m e) -> p m e", e=E), axis=AX.X,
                                     negate=True).then_inc(r_max.sem, 1)
                dve.wait_ge(*r_exp.at(l, NT[l]))
                step(nc.vector.reciprocal(rinv[:, 0:NT[l]], rsum[:, 0:NT[l]]))
                for m in range(NT[l]):
                    ins = nc.vector.tensor_scalar(aff[:, m % 2, m // 2, :], rex[:, m, :], rinv[:, m:m + 1], None, ALU.mult)
                ins.then_inc(aff_ready.sem, 1)
                step(nc.vector.memset(selg[:, :, :], 0.0))
                RE = NS * E
                dve.wait_ge(*affT_made.at(l, 1))
                step(nc.vector.tensor_copy(afT[0:RE, :], PS[0:RE, 1, 0:T]))
                src = afT[0:RE, :]
                for r in range(CAP // 8):
                    step(nc.vector.max(top[0:RE, 8 * r:8 * r + 8], src))
                    step(nc.vector.match_replace(afR[0:RE, (r + 1) % 2, :], top[0:RE, 8 * r:8 * r + 8], src, -1.0))
                    src = afR[0:RE, (r + 1) % 2, :]
                assert (CAP // 8) % 2 == 0
                nc.vector.tensor_tensor(afR[0:RE, 0, :], afT[0:RE, :], afR[0:RE, 0, :], ALU.not_equal)\
                    .then_inc(mask_ready.sem, 1)
                dve.wait_ge(*maskT_made.at(l, 1))
                nc.vector.tensor_copy(msk[:, :, 0:RE], PS[:, 2, 0:64].rearrange("p (j e) -> p j e", j=2)[:, :, 0:RE])\
                    .then_inc(maskT_ready.sem, 1)
                dve.wait_ge(*maskT_ready.at(l, 1))
                dve.wait_ge(*count_made.at(l, 1))
                nc.vector.tensor_tensor(place[:, :, 0:NS, :].rearrange("p j s e -> p j (s e)"),
                                        PS[:, 3, 0:64].rearrange("p (j e) -> p j e", j=2)[:, :, 0:RE],
                                        msk[:, :, 0:RE], ALU.mult).then_inc(place_ready.sem, 1)
                dve.wait_ge(*place_ready.at(l, 1))
                G = GE[l]
                with dve.Fori(0, NP[l]) as i:
                    def when(sig, n, k):
                        sem, val = sig.at(l, k)
                        dve.wait_ge(sem, i * n + val)

                    for s in range(NS):
                        sp = selp[:, s * 2 * G * CAP:(s + 1) * 2 * G * CAP].rearrange("p (j g c) -> p j g c", j=2, g=G)
                        pl = place[:, :, s, ds(i * G, G)].unsqueeze(3).broadcast_to([128, 2, G, CAP])
                        io = iota1.unsqueeze(1).unsqueeze(1).broadcast_to([128, 2, G, CAP])
                        nc.vector.tensor_tensor(sp, pl, io, ALU.is_equal).then_inc(sel_ready.sem, 1)
                    when(sel_ready, NS, NS)
                    for s in range(NS):
                        sp = selp[:, s * 2 * G * CAP:(s + 1) * 2 * G * CAP].rearrange("p (j g c) -> p j g c", j=2, g=G)
                        af = aff[:, :, s, ds(i * G, G)].unsqueeze(3).broadcast_to([128, 2, G, CAP])
                        sg = selg[:, 2 * s:2 * s + 2, :].rearrange("p j (g s c) -> p j g s c", g=G, s=NS)[:, :, :, s, :]
                        nc.vector.tensor_tensor(sg, sp, af, ALU.mult).then_inc(selg_ready.sem, 1)
                    c = 0
                    for bk in range(2):
                        when(gathered, 2, bk + 1)
                        for s in range(NS):
                            o = xsT[:, 4 * bk:4 * bk + 4, :].rearrange("p k (g s c) -> p k g s c", g=G, s=NS)[:, :, :, s, :]
                            src = PS[:, 6 + bk, :].rearrange("p (k g s c) -> p k g s c", k=4, g=G, s=NS)[:, :, :, s, :]
                            ga = modA[:, 1, s, 4 * bk:4 * bk + 4].unsqueeze(2).unsqueeze(2).broadcast_to([128, 4, G, CAP])
                            sh = modB[:, 1, s, 4 * bk:4 * bk + 4].unsqueeze(2).unsqueeze(2).broadcast_to([128, 4, G, CAP])
                            nc.vector.tensor_tensor(o, src, ga, ALU.mult).then_inc(xs_mul.sem, 1)
                            c += 1
                            when(xs_mul, 2 * NS, c)
                            nc.vector.tensor_tensor(o, o, sh, ALU.add).then_inc(xs_ready.sem, 1)
                    when(h3_sum, 1, 1)
                    for h in range(2):
                        when(sil_ready, 2, h + 1)
                        nc.vector.tensor_tensor(hid[:, h * 512:(h + 1) * 512], sil[:, h * 512:(h + 1) * 512],
                                                PS[:, 2 + h, :], ALU.mult).then_inc(hid_ready.sem, 1)
                    when(hidT_made, 2, 2)
                    nc.vector.tensor_copy(hidT[:, 4:8, :].rearrange("p a b -> p (a b)"), PS[:, 7, :])\
                        .then_inc(hidT_dve.sem, 1)
                    when(y_sum, 1, 1)
                    for h in range(2):
                        nc.vector.tensor_tensor(ysb[:, h * 512:(h + 1) * 512], PS[:, 4 + h, :],
                                                g2r[:, h * 512:(h + 1) * 512], ALU.mult).then_inc(y_ready.sem, 1)
                    for c in range(2 * NT[l]):
                        m, h = c // 2, c % 2
                        when(comb_sum, 2 * NT[l], c + 1)
                        xs_ = x[:, m, h * 512:(h + 1) * 512]
                        nc.vector.tensor_tensor(xs_, xs_, PS[:, c % 4, :], ALU.add).then_inc(comb_x.sem, 1)
                dve.wait_ge(*comb_x.at(l, 2 * NT[l] * NP[l]))
            dve.wait_ge(*rstd_done.at(4, 1))
            gain = arena[:, 8, 0:D]
            dve.wait_ge(consts_loaded, 96)
            for m in range(2):
                o_ = hT[:, 2 * m:2 * m + 2, :].rearrange("p a b -> p (a b)")
                step(nc.vector.tensor_scalar(o_, x[:, m, :], rstd[:, m:m + 1], None, ALU.mult))
                nc.vector.tensor_tensor(o_, o_, gain, ALU.mult).then_inc(fin_ready, 1)


def layout(inputs):
    a = {k: np.ascontiguousarray(np.asarray(v)) for k, v in inputs.items()}
    cols = lambda v, n: np.ascontiguousarray(v.reshape(n, 128).T)
    wide = lambda v: np.broadcast_to(v.reshape(1, -1), (128, v.size))
    par = np.zeros((L, 128, P_ALL), np.float32)
    stay = np.zeros((128, S_ALL), np.float32)
    for l in range(L):
        par[l, :, P_POOLW:P_POOLW + 512] = a["pool_w"][l].transpose(1, 0, 2).reshape(128, 512)
        par[l, :, P_SGUW:P_SGUW + 512] = a["sgu_w"][l].transpose(2, 0, 1).reshape(128, 512)
        par[l, :, P_SGUB:P_SGUB + 512] = wide(a["sgu_b"][l])
        par[l, :, P_LAM:P_LAM + 256] = wide(a["diff_lambda"][l])
        par[l, :, P_RW:P_RW + KD * E] = a["router_w"][l].reshape(KD, 128, E).transpose(1, 0, 2).reshape(128, KD * E)
        par[l, :, P_PSC:P_PSC + 4] = cols(a["pool_scale"][l], 4)
        par[l, :, P_SUBG:P_SUBG + 1] = cols(a["diff_subln_g"][l], 1)
        par[l, :, P_SGUG:P_SGUG + 4] = cols(a["sgu_norm_g"][l], 4)
        stay[:, S_N1 + KD * l:S_N1 + KD * (l + 1)] = cols(a["norm1_g"][l], KD)
        stay[:, S_N2 + KD * l:S_N2 + KD * (l + 1)] = cols(a["norm2_g"][l], KD)
    stay[:, S_C:S_C + KD] = cols(a["c"][0], KD)
    stay[:, S_C + KD:S_C + 2 * KD] = cols(a["c_ctx"], KD)
    d = {n: a[n] for n in ("x", "ctx", "w_mod", "b_mod", "w_in", "w_br", "w_out", "na_rpb", "moe_w1", "moe_w3", "moe_w2")}
    d.update(par=par, stay=stay, cst=shape_constants(), final_g=np.ascontiguousarray(wide(a["final_g"])))
    return d


def kernel(**inputs):
    import concourse.bacc as bacc
    from concourse.bass_utils import run_bass_kernel_spmd

    nc = bacc.Bacc("TRN2", target_bir_lowering=False, num_devices=1)
    arrays = layout(inputs)
    aps = {k: nc.dram_tensor(f"in_{k}", v.shape, mybir.dt.from_np(v.dtype), kind="ExternalInput").ap()
           for k, v in arrays.items()}
    out = nc.dram_tensor("out", (1, T, D), mybir.dt.float32, kind="ExternalOutput").ap()
    build(nc, aps, out)
    r = run_bass_kernel_spmd(nc, [{f"in_{k}": v for k, v in arrays.items()}], core_ids=[0])
    return r.results[0]["out"]
```

```python
import math
from contextlib import ExitStack

import numpy as np
import concourse.bass as bass
from concourse import mybir

D = 1024
T = 256
L = 2
GRID_W = 64
BW = 512
NBR = 4
E = 16
CAP = 2 * T // E
NA_C = 16
RPB_R, RPB_C = 15, 31
POOL_W = (2, 4, 8, 16)
EPS = 1e-6
KD = D // 128
NEG = -1.0e30

NSLOT = 6
ESLOT = 12

GROUPS = [("su", "f", 3584), ("sv", "t", 4096), ("pz", "f", 3072), ("dk", "f", 0), ("dv", "t", 512),
          ("nk", "f", 1024), ("nv", "t", 1536), ("dq", "f", 2048), ("nq", "f", 2560)]
KV = ("dk", "dv", "nk", "nv")
GATE_COL = 4608
NW = 4 * len(GROUPS)
NC_ALL = NW + NBR * KD + KD
MERGE_ORDER = (0, 2, 1, 3)

C_ID, C_FLIP, C_PERM = 0, 128, 256
C_COS, C_SIN = 384, 640
C_TRI, C_ONE = 896, 1024
C_IOTA, C_MASK = 1152, 1184
C_SELC, C_SELR, C_SELY = 1248, 1250, 1506
C_CNT = 1634
C_ALL = C_CNT + 4 * 16

P_POOLW, P_SGUW, P_SGUB, P_LAM, P_RW = 0, 512, 1024, 1536, 1792
P_PSC, P_SUBG, P_SGUG = 1920, 1924, 1925
P_ALL = 1929
S_N1, S_N2, S_C = 0, 16, 32
S_ALL = 48


def shape_constants():
    c = np.zeros((128, C_ALL), np.float32)
    p = np.arange(128)
    c[:, C_ID:C_ID + 128] = np.eye(128)
    c[:, C_FLIP:C_FLIP + 128] = np.eye(128)[::-1]
    c[p ^ 16, C_PERM + p] = 1.0
    nf = 16
    inv = (10000.0 ** (-np.arange(nf, dtype=np.float32) / nf)).astype(np.float32)
    t = np.arange(T)
    pos = np.stack([(t // GRID_W), (t % GRID_W)]).astype(np.float32)
    f = p % 64
    ang = pos[f // 32] * inv[f % 16][:, None]
    c[:, C_COS:C_COS + T] = np.cos(ang.astype(np.float32))
    c[:, C_SIN:C_SIN + T] = np.sin(ang.astype(np.float32)) * np.where(f % 32 < 16, -1.0, 1.0)[:, None]
    c[:, C_TRI:C_TRI + 128] = p[:, None] <= p[None, :]
    c[:, C_ONE:C_ONE + 128] = 1.0
    c[:, C_IOTA:C_IOTA + CAP] = 1.0 + np.arange(CAP)
    col = 63 - p % 64
    start = np.clip(col - NA_C // 2, 0, GRID_W - NA_C)
    k = np.arange(GRID_W)
    inside = (k[None, :] >= start[:, None]) & (k[None, :] < start[:, None] + NA_C)
    c[:, C_MASK:C_MASK + GRID_W] = np.where(inside, 0.0, NEG)
    for s in range(2):
        c[p % 32 == s, C_SELC + s] = 1.0
        c[p % 32 == s, C_SELR + 128 * s:C_SELR + 128 * s + 128] = 1.0
        c[:, C_SELY:C_SELY + 128] += ((p % 32 == s)[:, None] & ((p // CAP) % 2 == s)[None, :])
    for g, w in enumerate(POOL_W):
        n = np.clip(t + w // 2, 0, T) - np.clip(t - w // 2, 0, T)
        c[:, C_CNT + g * 16:C_CNT + g * 16 + 8] = 1.0 / n[:8].astype(np.float32)
        c[:, C_CNT + g * 16 + 8:C_CNT + g * 16 + 16] = 1.0 / n[-8:].astype(np.float32)
    return c


class Signal:

    def __init__(self, sem, per_layer):
        self.sem, self.per_layer = sem, per_layer

    def at(self, layer, count):
        return self.sem, sum(self.per_layer[:layer]) + count


def streams(l):
    return 2 if l < L - 1 else 1


def by_engine(units):
    n = {"act": 0, "dve": 0}
    for u in units:
        n[u["by"]] += 1
        u["nth"] = n[u["by"]]
    return units, n


def w_units(l):
    units, later, nw, na, q = [], [], 0, 0, 0

    def aux(**u):
        nonlocal na
        units.append(dict(u, bank=4 + na % 4, order=na))
        na += 1

    for name, kind, col in GROUPS:
        wide = name in KV or streams(l) == 2
        for ch in range(4):
            units.append(dict(kind="w", name=name, ch=ch, q=q, tokens=2 * T if wide else T, bank=nw % 4,
                              order=nw, temp=kind == "t", by="act" if name in ("su", "sv") or q % 2 else "dve"))
            nw += 1
            q += 1
            for u in later:
                aux(**u)
            later = []
            if kind == "t":
                later.append(dict(kind="t", name=name, ch=ch, tiles=4 if wide else 2, by="dve" if q % 2 else "act"))
            if name in ("dk", "dq") and ch % 2:
                later.append(dict(kind="rope", name=name, pair=ch // 2, by="dve"))
            if name == "dk":
                later.append(dict(kind="f", name="su", g=ch, by="dve"))
    for u in later:
        aux(**u)
    return by_engine(units)


def attention_blocks(l):
    return [(kind, s, qt, h) for kind in ("diff", "na") for s in range(streams(l)) for qt in range(2)
            for h in range(4)]


def attention_slots(l):
    return len(attention_blocks(l)) + 6


def tr_units(l):
    blocks = attention_blocks(l)
    nb = len(blocks)
    units = []
    for i in range(attention_slots(l)):
        if 0 <= i - 1 < nb:
            units.append(dict(kind="p", b=i - 1, a=0, by="act", slot=i))
            if blocks[i - 1][0] == "na":
                units.append(dict(kind="p", b=i - 1, a=1, by="dve", slot=i))
        if i >= 7 and (i - 7) % 4 == 0 and (i - 7) // 4 < nb // 4:
            units.append(dict(kind="o", g=(i - 7) // 4, by="act", slot=i))
    for t, u in enumerate(units):
        u["t"] = t
    return by_engine(units)


def mod_steps(l):
    first = [(l, q) for q in range(3 * KD, 5 * KD)] + ([(l + 1, q) for q in range(2 * KD)] if l + 1 < L else [])
    second = [(l, q) for q in range(2 * KD, 3 * KD)] + [(l, q) for q in range(5 * KD, 6 * KD)]
    return first, second


def merge_steps(l):
    first, second = mod_steps(l)
    half, slots = 2 * KD, attention_slots(l)
    steps, m = [], 0
    for n in range(NBR * KD):
        u = dict(n=n, p=n // KD, v=n % KD, att=[], mod=[])
        if n < half:
            u["att"] = list(range(n * slots // half, (n + 1) * slots // half))
            todo, at_ = first, n
        else:
            todo, at_ = second, n - half
        u["mod"] = [(m_ + (0 if n < half else len(first)), todo[m_])
                    for m_ in range(at_ * len(todo) // half, (at_ + 1) * len(todo) // half)]
        steps.append(u)
    return steps


def build(nc, A, out):
    f32, f32r = mybir.dt.float32, mybir.dt.float32r
    ACT = mybir.ActivationFunctionType
    ALU = mybir.AluOpType
    AX = mybir.AxisListType
    ds = bass.ds

    ctx = ExitStack()
    with ctx:
        def sb(name, shape, dt=f32, where=ctx):
            return where.enter_context(nc.sbuf_tensor(name, shape, dt))

        def signal(name, *per_layer):
            return Signal(ctx.enter_context(nc.semaphore(name)), list(per_layer))

        def counter(name):
            return ctx.enter_context(nc.semaphore(name))

        ring = sb("ring", [128, NSLOT, 1024])
        x = sb("x", [128, 4, D])
        arena = sb("arena", [128, 8, 2048])
        cst = sb("cst", [128, C_ALL])
        par = sb("par", [128, P_ALL])
        stay = sb("stay", [128, S_ALL])
        bm = sb("bm", [48, L, 128])
        nab_all = sb("nab", [128, 8 * 6 * GRID_W])
        work = sb("work", [128, 9, 512])
        small = sb("small", [128, 256])
        cond = sb("cond", [128, KD, 32])
        modp = sb("modp", [128, 2, 128])
        modA = sb("modA", [128, 2, 2, KD])
        modB = sb("modB", [128, 2, 2, KD])
        rwr = sb("rwr", [128, 2, 128], f32r)
        selp = sb("selp", [128, 256])
        rex = sb("rex", [128, 4, E])
        aff = sb("aff", [128, 2, 2, E])
        msk = sb("msk", [128, 2, 2 * E])
        place = sb("place", [128, 2, 2, E])
        with ExitStack() as mixers:
            wr = sb("wr", [128, 2, 2, 1024], f32r, mixers)
            hTr = sb("hTr", [128, 2, KD, 2 * T], f32r, mixers)
        with ExitStack() as moe:
            e_wr = sb("e_wr", [128, 2, 2048], f32, moe)
            e_h = sb("e_h", [128, 4, 2048], f32, moe)
        PS = ctx.enter_context(nc.psum_tensor("PS", [128, 8, 512], f32))

        def unit_of(i, n=1):
            return arena[:, i:i + n, :].rearrange("p a b -> p (a b)")

        region = {nm: unit_of(i).rearrange("p (a b) -> p a b", a=4)
                  for nm, i in (("pz", 0), ("dq", 1), ("su", 2), ("nq", 3), ("sv", 3), ("dk", 4), ("nk", 5),
                                ("dv", 6), ("nv", 7))}
        branches = unit_of(0, 4).rearrange("p (i k t) -> p i k t", i=NBR, k=4)
        nab = nab_all[:, :].rearrange("p (h n) -> p h n", h=8)
        x_flat = x[:, :, :].rearrange("p a b -> p (a b)")
        mT = [x_flat[:, :].rearrange("p (k t) -> p k t", k=KD), x_flat[:, 2 * D:].rearrange("p (k t) -> p k t", k=KD)]
        g1b = unit_of(6).rearrange("p (a b) -> p a b", a=2)
        htmp = unit_of(6).rearrange("p (a b) -> p a b", a=4)
        g2r = unit_of(7)[:, 0:D]
        xn = work[:, 0:8, :].rearrange("p (m a) b -> p m (a b)", m=4)
        sq_junk = nab_all[:, 2048:3072]
        espace = [arena[:, 0, :], arena[:, 1, :], arena[:, 2, :], arena[:, 3, :], nab_all[:, 0:2048],
                  arena[:, 4, :], arena[:, 5, :], e_wr[:, 0, :], e_wr[:, 1, :], e_h[:, 0, :], e_h[:, 1, :], e_h[:, 2, :]]
        xsT = unit_of(6)[:, 0:1024].rearrange("p (a b) -> p a b", a=KD)
        hid = unit_of(6)[:, 1024:2048]
        sil = unit_of(7)[:, 1024:2048]
        hidT = e_h[:, 3, 0:1024].rearrange("p (a b) -> p a b", a=KD)
        ysb = e_h[:, 3, 1024:2048]
        combT = nab_all[:, 2048:2560].rearrange("p (a b) -> p a b", a=4)
        selg = nab_all[:, 2560:3072].rearrange("p (a b) -> p a b", a=4)
        afT = unit_of(6)[0:32, 0:256]
        afR = unit_of(6)[0:32, 256:768].rearrange("p (a b) -> p a b", a=2)
        top = unit_of(6)[0:32, 768:800]
        fin_out = unit_of(0, 1)
        fin_gain = unit_of(1)[:, 0:D]

        ident = cst[:, C_ID:C_ID + 128]
        cosT, sinT = cst[:, C_COS:C_COS + T], cst[:, C_SIN:C_SIN + T]
        iota1 = cst[:, C_IOTA:C_IOTA + CAP]

        ss, ms, rstd = small[:, 0:4], small[:, 4:8], small[:, 8:12]
        half = small[:, 12:16]
        nmx = small[:, 16:20].rearrange("p (a b) -> p a b", a=2)
        rs = small[:, 20:24].rearrange("p (a b) -> p a b", a=2)
        rr = small[:, 24:32].rearrange("p (a b) -> p a b", a=4)
        lam = small[:, 32:40]
        subg = small[:, 40:41]
        oss, oms, orstd = small[:, 44:48], small[:, 48:52], small[:, 52:56]
        vst = small[:, 56:80].rearrange("p (a b) -> p a b", a=4)
        vmv = small[:, 80:88].rearrange("p (a b) -> p a b", a=4)
        vms, vrstd = small[:, 88:92], small[:, 92:96]
        nar = small[:, 96:128].rearrange("p (a b) -> p a b", a=4)
        rmx, rsum, rinv = small[:, 128:132], small[:, 132:136], small[:, 136:140]

        p_t = work[:, 0:4, :].rearrange("p (a b) c -> p a b c", a=2)
        at = work[:, 4:6, :]
        on = work[:, 6, :]
        sgt = work[:, 7:9, :]
        vtmp = work[:, 7:9, :]

        NT = [2 * streams(l) for l in range(L)]
        norms = [(0, 0, 2), (0, 1, streams(0)), (1, 0, 2), (1, 1, streams(1)), (2, 0, 1)]
        loaded = [counter(f"slot_loaded{i}") for i in range(NSLOT)]
        e_loaded = [counter(f"expert_loaded{i}") for i in range(ESLOT)]
        e_freed = [counter(f"expert_freed{i}") for i in range(ESLOT)]
        consts_loaded = counter("consts_loaded")
        x_loaded = counter("x_loaded")
        par_loaded = counter("par_loaded")
        bias_loaded = counter("bias_loaded")
        bias_masked = signal("bias_masked", 1, 1)
        half_ready = counter("half_ready")
        cond_ready = counter("cond_ready")
        MOD0 = 2 * KD
        MS = [MOD0 + sum(len(x_) for x_ in mod_steps(0)), sum(len(x_) for x_ in mod_steps(1))]
        mod_sum = signal("mod_sum", *MS)
        mod_part = signal("mod_part", *MS)
        mod_cols = signal("mod_cols", 3, 1)
        mod_ready = signal("mod_ready", 3, 1)
        NGB = [KD * streams(l) + KD for l in range(L)]
        gate_bc = signal("gate_bc", *NGB)
        gate_rows = signal("gate_rows", *NGB)
        NN = [2 * n for _, _, n in norms]
        sq_done = signal("sq_done", *NN)
        ms_done = signal("ms_done", *[1] * 5)
        rstd_done = signal("rstd_done", *[1] * 5)
        xn_ready = signal("xn_ready", *NN)
        xt_ready = signal("xt_ready", *[4 * n for _, _, n in norms[:4]])
        tmp_act = signal("tmp_act", *[2 * n for _, _, n in norms[:4]])
        tmp_dve = signal("tmp_dve", *[2 * n for _, _, n in norms[:4]])
        h_hi = signal("h_hi", *[4 * n for _, _, n in norms[:4]])
        h_lo = signal("h_lo", *[4 * n for _, _, n in norms[:4]])
        w_hi = signal("w_hi", NC_ALL, NC_ALL)
        w_lo = signal("w_lo", NC_ALL, NC_ALL)
        chunk_sum = signal("chunk_sum", NC_ALL, NC_ALL)
        rw_hi = signal("rw_hi", 1, 1)
        rw_lo = signal("rw_lo", 1, 1)
        WU = [w_units(l) for l in range(L)]
        aux_sum = signal("aux_sum", *[sum(u["kind"] != "w" for u in us) for us, _ in WU])
        w_act = signal("w_act", *[n["act"] for _, n in WU])
        w_dve = signal("w_dve", *[n["dve"] for _, n in WU])
        dve_step = counter("dve_step")
        pool_step = counter("pool_step")
        lam_prod = signal("lam_prod", 1, 1)
        lam_exp = signal("lam_exp", 1, 1)
        lam_ready = signal("lam_ready", 1, 1)
        pooled = signal("pooled", 4, 4)
        pool_sum = signal("pool_sum", 4, 4)
        pool_out = signal("pool_out", 4, 4)
        v_stats = signal("v_stats", 1, 1)
        v_rstd = signal("v_rstd", 1, 1)
        v_norm = signal("v_norm", *NT)
        BL = [attention_blocks(l) for l in range(L)]
        NB = [len(b) for b in BL]
        TU = [tr_units(l) for l in range(L)]
        scores = signal("scores", *NB)
        maxes = signal("maxes", *NB)
        exps = signal("exps", *NB)
        probs = signal("probs", *NB)
        tr_made = signal("tr_made", *[len(u) for u, _ in TU])
        at_act = signal("at_act", *[n["act"] for _, n in TU])
        at_dve = signal("at_dve", *[n["dve"] for _, n in TU])
        pv = signal("pv", *NB)
        NG = [n // 4 for n in NB]
        o_square = signal("o_square", *[n // 2 for n in NG])
        o_ss = signal("o_ss", *[n // 2 for n in NG])
        o_rstd = signal("o_rstd", *[n // 2 for n in NG])
        o_norm = signal("o_norm", *NG)
        NM = NBR * KD
        projs = signal("projs", NM, NM)
        sigs = signal("sigs", NM, NM)
        gated = signal("gated", NM, NM)
        merged = signal("merged", NM, NM)
        m_hi = signal("m_hi", KD, KD)
        m_lo = signal("m_lo", KD, KD)
        x_back = counter("x_back")
        mix_sum = signal("mix_sum", *[2 * n for n in NT])
        mix_x = signal("mix_x", *[2 * n for n in NT])
        logits = signal("logits", 1, 1)
        r_max = signal("r_max", 1, 1)
        r_exp = signal("r_exp", *NT)
        aff_ready = signal("aff_ready", 1, 1)
        affT_made = signal("affT_made", 1, 1)
        mask_ready = signal("mask_ready", 1, 1)
        maskT_made = signal("maskT_made", 1, 1)
        maskT_ready = signal("maskT_ready", 1, 1)
        count_made = signal("count_made", 1, 1)
        place_ready = signal("place_ready", 1, 1)
        GE = [128 // (CAP * streams(l)) for l in range(L)]
        NP = [E // g for g in GE]

        def packs(name, n0, n1):
            return signal(name, n0 * NP[0], n1 * NP[1])

        sel_ready = packs("sel_ready", 2, 1)
        selg_ready = packs("selg_ready", 2, 1)
        gathered = packs("gathered", 2, 2)
        xs_mul = packs("xs_mul", 4, 2)
        xs_ready = packs("xs_ready", 4, 2)
        combT_made = packs("combT_made", 1, 1)
        combT_ready = packs("combT_ready", 1, 1)
        h1_sum = packs("h1_sum", 1, 1)
        h3_sum = packs("h3_sum", 1, 1)
        sil_ready = packs("sil_ready", 2, 2)
        hid_ready = packs("hid_ready", 2, 2)
        hidT_made = packs("hidT_made", 2, 2)
        hidT_act = packs("hidT_act", 1, 1)
        hidT_dve = packs("hidT_dve", 1, 1)
        y_sum = packs("y_sum", 1, 1)
        y_ready = packs("y_ready", 2, 2)
        comb_sum = packs("comb_sum", 2 * NT[0], 2 * NT[1])
        comb_x = packs("comb_x", 2 * NT[0], 2 * NT[1])
        fin_ready = counter("fin_ready")
        out_stored = counter("out_stored")

        E_USES = 12 * E // ESLOT

        MERGE = [merge_steps(l) for l in range(L)]
        items, item_at = [], {}

        def item(kind, l, idx, release):
            item_at[kind, l, idx] = (len(items) % NSLOT, len(items) // NSLOT)
            items.append((kind, l, idx, release))

        for n in range(MOD0):
            item("mod", 0, n, mod_sum.at(0, n + 1))
        for l in range(L):
            for q in range(NW):
                item("chunk", l, q, w_lo.at(l, q + 1))
            done = MOD0 if l == 0 else 0
            for u in MERGE[l]:
                item("chunk", l, NW + u["n"], w_lo.at(l, NW + u["n"] + 1))
                item("br", l, u["n"], projs.at(l, u["n"] + 1))
                for m_, _ in u["mod"]:
                    item("mod", l, done + m_, mod_sum.at(l, done + m_ + 1))
            for k in range(KD):
                item("chunk", l, NW + NM + k, w_lo.at(l, NW + NM + k + 1))

        def mod_of(l, n):
            if l == 0:
                if n < MOD0:
                    return 0, n
                n -= MOD0
            first, second = mod_steps(l)
            return (first + second)[n]

        block = ctx.enter_context(nc.Block())

        def own(u, a, d):
            return a if u["by"] == "act" else d

        def last_of(units, name, kind):
            n = {"act": 0, "dve": 0}
            for u in units:
                if u["name"] == name and u["kind"] == kind:
                    n[u["by"]] = u["nth"]
            return n

        @block.sync
        def _(sync):
            w_mod_v = A["w_mod"].rearrange("l (k p) n -> l p k n", p=128)
            w_in_v = A["w_in"].rearrange("l (k p) n -> l p k n", p=128)
            w_br_v = A["w_br"].rearrange("l i (k p) n -> l i p k n", p=128)
            w_out_v = A["w_out"].rearrange("l (k p) n -> l k p n", p=128)
            experts = [A[n].rearrange("l e (k p) n -> l (e k) p n", p=128) for n in ("moe_w1", "moe_w3", "moe_w2")]

            def load_items(lo, hi):
                for n in range(lo, hi):
                    kind, l, idx, _ = items[n]
                    if n >= NSLOT:
                        sync.wait_ge(*items[n - NSLOT][3])
                    dst = ring[:, n % NSLOT, :]
                    if kind == "mod":
                        ml, q = mod_of(l, idx)
                        src = w_mod_v[ml, :, :, q * 128:(q + 1) * 128]
                        dst = dst.rearrange("p (k n) -> p k n", k=KD)
                    elif kind == "br":
                        p, v = idx // KD, idx % KD
                        src = w_br_v[l, MERGE_ORDER[p], :, :, v * 128:(v + 1) * 128]
                        dst = dst[:, 0:512].rearrange("p (k n) -> p k n", k=4)
                    elif idx < NW:
                        c = GROUPS[idx // 4][2] + (idx % 4) * 128
                        src = w_in_v[l, :, :, c:c + 128]
                        dst = dst.rearrange("p (k n) -> p k n", k=KD)
                    elif idx < NW + NM:
                        n_ = idx - NW
                        c = GATE_COL + MERGE_ORDER[n_ // KD] * D + (n_ % KD) * 128
                        src = w_in_v[l, :, :, c:c + 128]
                        dst = dst.rearrange("p (k n) -> p k n", k=KD)
                    else:
                        src = w_out_v[l, idx - NW - NM]
                    sync.dma_start(dst, src).then_inc(loaded[n % NSLOT], 16)

            sync.dma_start(stay[:, :], A["stay"]).then_inc(consts_loaded, 16)
            sync.dma_start(cst[:, :], A["cst"]).then_inc(consts_loaded, 16)
            sync.dma_start(bm[:, :, :], A["b_mod"].rearrange("l (a b) -> a l b", b=128)).then_inc(consts_loaded, 16)
            sync.dma_start(x[:, 0:2, :], A["x"].rearrange("o (m p) d -> p (o m) d", p=128)).then_inc(x_loaded, 16)
            sync.dma_start(x[:, 2:4, :], A["ctx"].rearrange("o (m p) d -> p (o m) d", p=128)).then_inc(x_loaded, 16)
            at_item = 0
            for l in range(L):
                end = max(n for n, it in enumerate(items) if it[1] == l) + 1
                load_items(at_item, end)
                at_item = end
                G = GE[l]
                with sync.Fori(0, NP[l]) as i:
                    n = 0
                    for w in experts:
                        for j in range(4):
                            for g in range(G):
                                s, turn = n % ESLOT, n // ESLOT
                                sync.wait_ge(e_freed[s], i * (12 * G // ESLOT) + (l * (E_USES + 1) + 1 + turn))
                                sync.dma_start(espace[s].rearrange("p (k n) -> p k n", k=2),
                                               w[l, ds(i * (G * KD) + (g * KD + 2 * j), 2), :, :]
                                               .rearrange("k p n -> p k n")).then_inc(e_loaded[s], 16)
                                n += 1
            sync.wait_ge(e_freed[1], L * (E_USES + 1))
            sync.dma_start(fin_gain, A["final_g"]).then_inc(consts_loaded, 16)
            out_v = out.rearrange("o (m p) d -> p (o m) d", p=128)
            for m in range(2):
                sync.wait_ge(fin_ready, m + 1)
                sync.dma_start(out_v[:, m, :], fin_out[:, m * D:(m + 1) * D]).then_inc(out_stored, 16)
            sync.wait_ge(out_stored, 32)

        @block.tensor
        def _(pe):
            def mm(o, a, b, first, last):
                return nc.tensor.matmul(o, a, b, start=first, stop=last)

            def take(key):
                slot, use = item_at[key]
                pe.wait_ge(loaded[slot], 16 * (use + 1))
                return ring[:, slot, :]

            def three(o, wh, wl, ah, al, first, last, weights_move):
                if weights_move:
                    mm(o, ah, wh, first, False)
                    mm(o, ah, wl, False, False)
                    return mm(o, al, wh, False, last)
                mm(o, wh, ah, first, False)
                mm(o, wh, al, False, False)
                return mm(o, wl, ah, False, last)

            bc = [0, 0]

            def mod_post(l, n):
                ml, q = mod_of(l, n)
                part, ch = q // KD, q % KD
                pe.wait_ge(*mod_part.at(l, n + 1))
                if part % 3 == 2:
                    for s in range(streams(ml) if part == 2 else 1):
                        if bc[l] >= 2:
                            pe.wait_ge(*gate_rows.at(l, bc[l] - 1))
                        if part == 5 and streams(ml) == 2:
                            pick = cst[:, C_SELY:C_SELY + 128]
                        else:
                            pick = cst[:, C_SELR + 128 * s:C_SELR + 128 * s + 128]
                        mm(PS[:, bc[l] % 2, 0:128], pick, modp[:, n % 2, :], True, True).then_inc(gate_bc.sem, 1)
                        bc[l] += 1
                else:
                    col = 256 + 32 * (part // 3) + 2 * ((part % 3) * KD + ch)
                    i = mm(PS[:, 7, col:col + 2], modp[:, n % 2, :], cst[:, C_SELC:C_SELC + 2], True, True)
                    if part % 3 == 1 and ch == KD - 1:
                        i.then_inc(mod_cols.sem, 1)

            def mod_chunk(l, n):
                ml, q = mod_of(l, n)
                w = take(("mod", l, n))
                if n:
                    pe.wait_ge(*mod_part.at(l, n))
                if l == 0 and n == MOD0:
                    pe.wait_ge(*mod_ready.at(0, 1))
                if n == (MOD0 if l == 0 else 0) + len(mod_steps(l)[0]):
                    pe.wait_ge(*mod_ready.at(l, 3 if l == 0 else 1))
                o = PS[:, 7, 0:128]
                for kk in range(2):
                    for j in range(4):
                        k = 4 * kk + j
                        nc.tensor.matmul(o[32 * j:32 * j + 32, :], cond[:, k, :], w[:, k * 128:(k + 1) * 128],
                                         start=(kk == 0), stop=(kk == 1 and j > 0), tile_position=(0, 32 * j),
                                         skip_group_check=True)
                nc.tensor.matmul(o[0:2, :], cst[0:48, C_ID + q:C_ID + q + 1].broadcast_to([48, 2]), bm[:, ml, :],
                                 start=False, stop=True, tile_position=(0, 0), skip_group_check=True)\
                    .then_inc(mod_sum.sem, 1)

            def transposes(nn, n_streams):
                for s in range(n_streams):
                    pe.wait_ge(*xn_ready.at(nn, 2 * s + 2))
                    for kp in range(4):
                        for kk in range(2):
                            for j in range(2):
                                i = nc.tensor.transpose(PS[:, 4 * s + kp, kk * T + j * 128:kk * T + (j + 1) * 128],
                                                        xn[:, 2 * s + j, (2 * kp + kk) * 128:(2 * kp + kk + 1) * 128],
                                                        ident)
                        i.then_inc(xt_ready.sem, 1)

            pe.wait_ge(consts_loaded, 48)
            pe.wait_ge(cond_ready, 2)
            for n in range(MOD0):
                if n:
                    mod_post(0, n - 1)
                mod_chunk(0, n)
            mod_post(0, MOD0 - 1)
            pe.wait_ge(*mod_ready.at(0, 1))

            for l in range(L):
                NS = streams(l)
                tok = NS * T
                transposes(2 * l, 2)
                units, counts = WU[l]
                pe.wait_ge(*h_lo.at(2 * l, 8))
                seen = {"w": [], "aux": []}
                for u in units:
                    cls = seen["w" if u["kind"] == "w" else "aux"]
                    if len(cls) >= 4:
                        o = cls[-4]
                        pe.wait_ge(*own(o, w_act, w_dve).at(l, o["nth"]))
                    cls.append(u)
                    bank = PS[:, u["bank"], :]
                    if u["kind"] == "w":
                        q = u["q"]
                        pe.wait_ge(*w_lo.at(l, q + 1))
                        for k in range(KD):
                            i = three(bank[:, 0:u["tokens"]], wr[:, q % 2, 0, k * 128:(k + 1) * 128],
                                      wr[:, q % 2, 1, k * 128:(k + 1) * 128], hTr[:, 0, k, 0:u["tokens"]],
                                      hTr[:, 1, k, 0:u["tokens"]], k == 0, k == KD - 1, False)
                        i.then_inc(chunk_sum.sem, 1)
                    elif u["kind"] == "t":
                        src = [v for v in units if v["kind"] == "w" and v["name"] == u["name"] and v["ch"] == u["ch"]][0]
                        pe.wait_ge(*own(src, w_act, w_dve).at(l, src["nth"]))
                        for m in range(u["tiles"]):
                            i = nc.tensor.transpose(bank[:, m * 128:(m + 1) * 128],
                                                    vtmp[:, src["q"] % 2, m * 128:(m + 1) * 128], ident)
                        i.then_inc(aux_sum.sem, 1)
                    elif u["kind"] == "rope":
                        for v in units:
                            if v["kind"] == "w" and v["name"] == u["name"] and v["ch"] // 2 == u["pair"]:
                                pe.wait_ge(*own(v, w_act, w_dve).at(l, v["nth"]))
                        for c in range(2):
                            i = mm(bank[:, c * T:(c + 1) * T], cst[:, C_PERM:C_PERM + 128],
                                   region[u["name"]][:, 2 * u["pair"] + c, 0:T], True, True)
                        i.then_inc(aux_sum.sem, 1)
                    else:
                        g = u["g"]
                        pe.wait_ge(par_loaded, 16 * (l + 1))
                        pe.wait_ge(*v_norm.at(l, 2 * NS))
                        for m in range(2 * NS):
                            i = mm(bank[:, m * 128:(m + 1) * 128], region["sv"][:, m, g * 128:(g + 1) * 128],
                                   par[:, P_SGUW + g * 128:P_SGUW + (g + 1) * 128], True, True)
                        i.then_inc(aux_sum.sem, 1)
                pe.wait_ge(*w_act.at(l, counts["act"]))
                pe.wait_ge(*w_dve.at(l, counts["dve"]))
                for g in range(4):
                    pe.wait_ge(*pooled.at(l, g + 1))
                    mm(PS[:, 4 + g, 0:tok], par[:, P_POOLW + g * 128:P_POOLW + (g + 1) * 128],
                       region["pz"][:, g, 0:tok], True, True).then_inc(pool_sum.sem, 1)
                blocks, nb = BL[l], NB[l]
                tr, tr_n = TU[l]

                def score(b):
                    kind, s, qt, h = blocks[b]
                    q, k = (region["dq"], region["dk"]) if kind == "diff" else (region["nq"], region["nk"])
                    k0, nk = (0, 2 * T) if s == 0 else (T, T)
                    if b >= 1:
                        pe.wait_ge(*exps.at(l, b))
                    local = kind == "na" and s == 0
                    for a in range(2):
                        i = mm(PS[:, a, 0:nk], q[64 * a:64 * a + 64, h, s * T + qt * 128:s * T + (qt + 1) * 128],
                               k[64 * a:64 * a + 64, h, k0:k0 + nk], True, not local)
                    if local:
                        pe.wait_ge(*bias_masked.at(l, 1))
                        for a in range(2):
                            i = mm(PS[:, a, 0:T], cst[:, C_FLIP:C_FLIP + 128],
                                   nab[:, 2 * h + a, (2 - 2 * qt) * 64:(2 - 2 * qt) * 64 + T], False, True)
                    i.then_inc(scores.sem, 1)

                def emptied(t):
                    if t >= 2:
                        o = tr[t - 2]
                        pe.wait_ge(*own(o, at_act, at_dve).at(l, o["nth"]))

                def turn(u):
                    b = u["b"]
                    nkt = 4 if blocks[b][1] == 0 else 2
                    pe.wait_ge(*probs.at(l, b + 1))
                    emptied(u["t"])
                    for kt in range(nkt):
                        i = nc.tensor.transpose(PS[:, 2 + u["t"] % 2, kt * 128:(kt + 1) * 128],
                                                p_t[:, b % 2, u["a"], kt * 128:(kt + 1) * 128], ident)
                    i.then_inc(tr_made.sem, 1)

                def values(b):
                    kind, s, qt, h = blocks[b]
                    nkt, m0 = (4, 0) if s == 0 else (2, 2)
                    g = b // 4
                    if b % 4 == 0 and g >= 1:
                        pe.wait_ge(*o_norm.at(l, g))
                    mine = [u for u in tr if u["kind"] == "p" and u["b"] == b]
                    for u in mine:
                        pe.wait_ge(*own(u, at_act, at_dve).at(l, u["nth"]))
                    for u in mine:
                        w = 128 // len(mine)
                        c = h * 128 + u["a"] * w
                        v = region["dv"] if kind == "diff" else region["nv"]
                        for kt in range(nkt):
                            i = mm(PS[:, 4, c:c + w], at[:, u["t"] % 2, kt * 128:(kt + 1) * 128],
                                   v[:, m0 + kt, c:c + w], kt == 0, kt == nkt - 1)
                    i.then_inc(pv.sem, 1)

                def turn_out(u):
                    pe.wait_ge(*o_norm.at(l, u["g"] + 1))
                    emptied(u["t"])
                    for c in range(4):
                        i = nc.tensor.transpose(PS[:, 2 + u["t"] % 2, c * 128:(c + 1) * 128],
                                                on[:, c * 128:(c + 1) * 128], ident)
                    i.then_inc(tr_made.sem, 1)

                def attention(slot):
                    if slot < nb:
                        score(slot)
                    for u in tr:
                        if u["slot"] == slot and u["kind"] == "p":
                            turn(u)
                    if 0 <= slot - 2 < nb:
                        values(slot - 2)
                    for u in tr:
                        if u["slot"] == slot and u["kind"] == "o":
                            turn_out(u)

                done = MOD0 if l == 0 else 0
                open_mod = None
                pe.wait_ge(*pool_out.at(l, 4))
                for u in MERGE[l]:
                    n, j, v = u["n"], NW + u["n"], u["v"]
                    pe.wait_ge(*w_lo.at(l, j + 1))
                    if n:
                        pe.wait_ge(*sigs.at(l, n))
                    for k in range(KD):
                        i = three(PS[:, 5, 0:tok], wr[:, j % 2, 0, k * 128:(k + 1) * 128],
                                  wr[:, j % 2, 1, k * 128:(k + 1) * 128], hTr[:, 0, k, 0:tok], hTr[:, 1, k, 0:tok],
                                  k == 0, k == KD - 1, False)
                    i.then_inc(chunk_sum.sem, 1)
                    for slot in u["att"][0:1]:
                        attention(slot)
                    br = take(("br", l, n))
                    if n:
                        pe.wait_ge(*gated.at(l, n))
                    if v == 0:
                        if u["p"] >= 2:
                            pe.wait_ge(*at_act.at(l, tr_n["act"]))
                    for k in range(4):
                        i = mm(PS[:, 6, 0:tok], br[:, k * 128:(k + 1) * 128],
                               branches[:, MERGE_ORDER[u["p"]], k, 0:tok], k == 0, k == 3)
                    i.then_inc(projs.sem, 1)
                    for slot in u["att"][1:]:
                        attention(slot)
                    for m_, _ in u["mod"]:
                        if open_mod is not None:
                            mod_post(l, open_mod)
                        mod_chunk(l, done + m_)
                        open_mod = done + m_
                mod_post(l, open_mod)
                pe.wait_ge(*projs.at(l, NM))
                pe.wait_ge(*pv.at(l, nb))
                for s in range(7):
                    pe.sem_inc(e_freed[s], 1)
                for k in range(KD):
                    j = NW + NM + k
                    pe.wait_ge(*w_lo.at(l, j + 1))
                    pe.wait_ge(*m_lo.at(l, k + 1))
                    if k == 0:
                        pe.wait_ge(*gate_rows.at(l, NGB[l]))
                    for m in range(NT[l]):
                        for n in range(2):
                            i = three(PS[:, 2 * m + n, :], wr[:, j % 2, 0, n * 512:(n + 1) * 512],
                                      wr[:, j % 2, 1, n * 512:(n + 1) * 512], hTr[:, 0, k, m * 128:(m + 1) * 128],
                                      hTr[:, 1, k, m * 128:(m + 1) * 128], k == 0, k == KD - 1, True)
                            if k == KD - 1:
                                i.then_inc(mix_sum.sem, 1)
                            elif m == NT[l] - 1 and n == 1:
                                i.then_inc(chunk_sum.sem, 1)
                pe.wait_ge(*mix_sum.at(l, 2 * NT[l]))
                pe.sem_inc(chunk_sum.sem, 1)
                for s in (7, 8):
                    pe.sem_inc(e_freed[s], 1)
                pe.wait_ge(*mix_x.at(l, 2 * NT[l]))
                transposes(2 * l + 1, NS)
                pe.wait_ge(*h_lo.at(2 * l + 1, 4 * NS))
                pe.wait_ge(*rw_lo.at(l, 1))
                for m in range(NT[l]):
                    for k in range(KD):
                        i = three(PS[:, 0, m * E:(m + 1) * E], rwr[:, 0, k * E:(k + 1) * E], rwr[:, 1, k * E:(k + 1) * E],
                                  hTr[:, 0, k, m * 128:(m + 1) * 128], hTr[:, 1, k, m * 128:(m + 1) * 128],
                                  k == 0, k == KD - 1, True)
                i.then_inc(logits.sem, 1)
                pe.wait_ge(*logits.at(l, 1))
                for s in (9, 10, 11):
                    pe.sem_inc(e_freed[s], 1)
                pe.wait_ge(*aff_ready.at(l, 1))
                for j in range(2):
                    i = nc.tensor.transpose(PS[0:NS * E, 1, j * 128:(j + 1) * 128],
                                            aff[:, j, 0:NS, :].rearrange("p a b -> p (a b)"), ident)
                i.then_inc(affT_made.sem, 1)
                pe.wait_ge(*mask_ready.at(l, 1))
                for j in range(2):
                    i = nc.tensor.transpose(PS[:, 2, j * 32:j * 32 + NS * E], afR[0:NS * E, 0, j * 128:(j + 1) * 128],
                                            cst[0:NS * E, C_ID:C_ID + NS * E])
                i.then_inc(maskT_made.sem, 1)
                pe.wait_ge(*maskT_ready.at(l, 1))
                mm(PS[:, 3, 0:NS * E], cst[:, C_TRI:C_TRI + 128], msk[:, 0, 0:NS * E], True, True)
                mm(PS[:, 3, 32:32 + NS * E], cst[:, C_ONE:C_ONE + 128], msk[:, 0, 0:NS * E], True, False)
                mm(PS[:, 3, 32:32 + NS * E], cst[:, C_TRI:C_TRI + 128], msk[:, 1, 0:NS * E], False, True)\
                    .then_inc(count_made.sem, 1)
                G, R = GE[l], CAP * NS
                with pe.Fori(0, NP[l]) as i:
                    def when(sig, n, k):
                        sem, val = sig.at(l, k)
                        pe.wait_ge(sem, i * n + val)

                    when(sel_ready, NS, NS)
                    for bk in range(2):
                        for k4 in range(4):
                            k = 4 * bk + k4
                            for s in range(NS):
                                o = PS[:, 6 + bk, k4 * 128:(k4 + 1) * 128].rearrange(
                                    "p (g s c) -> p g s c", g=G, s=NS)[:, :, s, :]
                                for j in range(2):
                                    m = 2 * s + j
                                    ins = mm(o, xn[:, m, k * 128:(k + 1) * 128],
                                             selp[:, m * G * CAP:(m + 1) * G * CAP].rearrange("p (g c) -> p g c", g=G),
                                             j == 0, j == 1)
                        ins.then_inc(gathered.sem, 1)
                    when(selg_ready, NS, NS)
                    for m in range(NT[l]):
                        ins = nc.tensor.transpose(PS[:, 4, m * 128:(m + 1) * 128], selg[:, m, :], ident)
                    ins.then_inc(combT_made.sem, 1)
                    when(xs_ready, 2 * NS, 2 * NS)
                    n = 0
                    for w, (bank, done_) in enumerate(((0, h1_sum), (2, h3_sum), (4, y_sum))):
                        src = xsT if w < 2 else hidT
                        if w == 2:
                            when(hid_ready, 2, 2)
                            for bk in range(2):
                                for k4 in range(4):
                                    k = 4 * bk + k4
                                    ins = nc.tensor.transpose(PS[:, 6 + bk, k4 * 128:(k4 + 1) * 128],
                                                              hid[:, k * 128:(k + 1) * 128], ident)
                                ins.then_inc(hidT_made.sem, 1)
                            when(combT_ready, 1, 1)
                            when(hidT_act, 1, 1)
                            when(hidT_dve, 1, 1)
                        for j in range(4):
                            for g in range(G):
                                s, turn_ = (n + g) % ESLOT, (n + g) // ESLOT
                                pe.wait_ge(e_loaded[s], i * (16 * (12 * G // ESLOT)) + 16 * (l * E_USES + turn_ + 1))
                            for kk in range(2):
                                k = 2 * j + kk
                                for h in range(2):
                                    for g in range(G):
                                        s = (n + g) % ESLOT
                                        ins = nc.tensor.matmul(
                                            PS[g * R:(g + 1) * R, bank + h, :], src[:, k, g * R:(g + 1) * R],
                                            espace[s][:, kk * D + h * 512:kk * D + (h + 1) * 512],
                                            start=(k == 0), stop=(k == KD - 1), tile_position=(0, g * R))
                                        if kk == 1 and h == 1 and not (j == 3 and g == G - 1):
                                            ins.then_inc(e_freed[s], 1)
                            n += G
                        ins.then_inc(done_.sem, 1)
                        sem, val = done_.at(l, 1)
                        pe.wait_ge(sem, i * 1 + val)
                        pe.sem_inc(e_freed[(n - 1) % ESLOT], 1)
                    when(y_ready, 2, 2)
                    for c in range(2 * NT[l]):
                        m, h = c // 2, c % 2
                        if c >= 4:
                            when(comb_x, 2 * NT[l], c - 3)
                        mm(PS[:, c % 4, :], combT[:, m, :], ysb[:, h * 512:(h + 1) * 512], True, True)\
                            .then_inc(comb_sum.sem, 1)
                pe.wait_ge(*comb_x.at(l, 2 * NT[l] * NP[l]))

        @block.scalar
        def _(act):
            act.wait_ge(consts_loaded, 48)
            act.wait_ge(cond_ready, 1)
            nc.scalar.activation(cond[:, :, 0:2], stay[:, S_C:S_C + 16].rearrange("p (s k) -> p k s", s=2),
                                 ACT.Silu).then_inc(cond_ready, 1)

            def high(l, j):
                if j >= NC_ALL:
                    return
                slot, use = item_at["chunk", l, j]
                act.wait_ge(loaded[slot], 16 * (use + 1))
                if j >= 2:
                    act.wait_ge(*chunk_sum.at(l, j - 1))
                nc.scalar.activation(wr[:, j % 2, 0, :], ring[:, slot, :], ACT.Copy).then_inc(w_hi.sem, 1)

            def squares(nn, n_streams):
                for m in range(2 * n_streams):
                    nc.scalar.activation(sq_junk, x[:, m, :], ACT.Square, accum_out=ss[:, m:m + 1])\
                        .then_inc(sq_done.sem, 1)
                    act.wait_ge(*sq_done.at(nn, m + 1))

            def modulate(nn, norm, n_streams):
                for b in range(4 * n_streams):
                    s, kp = b // 4, b % 4
                    if b % 2 == 0:
                        act.wait_ge(*xt_ready.at(nn, b + 1))
                        if b >= 4:
                            act.wait_ge(*h_lo.at(nn, b - 3))
                        for kk in range(2):
                            k = 2 * kp + kk
                            ins = nc.scalar.activation(htmp[:, b % 4, kk * T:(kk + 1) * T], PS[:, b, kk * T:(kk + 1) * T],
                                                       ACT.Identity, bias=modB[:, norm, s, k:k + 1],
                                                       scale=modA[:, norm, s, k:k + 1])
                        ins.then_inc(tmp_act.sem, 1)
                        act.wait_ge(*tmp_act.at(nn, b // 2 + 1))
                    else:
                        act.wait_ge(*tmp_dve.at(nn, b // 2 + 1))
                    nc.scalar.activation(hTr[:, 0, 2 * kp:2 * kp + 2, s * T:(s + 1) * T],
                                         htmp[:, b % 4, :].rearrange("p (k t) -> p k t", k=2), ACT.Copy)\
                        .then_inc(h_hi.sem, 1)

            act.wait_ge(x_loaded, 32)
            for l in range(L):
                NS = streams(l)
                tok = NS * T
                if l:
                    act.wait_ge(*comb_x.at(l - 1, 2 * NT[l - 1] * NP[l - 1]))
                squares(2 * l, 2)
                high(l, 0)
                high(l, 1)
                act.wait_ge(*mod_ready.at(0, 1 if l == 0 else 3))
                modulate(2 * l, 0, 2)
                act.wait_ge(par_loaded, 16 * (l + 1))
                nc.scalar.activation(rwr[:, 0, :], par[:, P_RW:P_RW + KD * E], ACT.Copy).then_inc(rw_hi.sem, 1)
                act.wait_ge(*lam_prod.at(l, 1))
                nc.scalar.activation(lam[:, 2:4], lam[:, 0:2], ACT.Exp).then_inc(lam_exp.sem, 1)
                units, counts = WU[l]
                n_aux = 0
                for u in units:
                    if u["kind"] == "w":
                        high(l, u["q"] + 2)
                    else:
                        n_aux += 1
                    if u["by"] != "act":
                        continue
                    bank = PS[:, u["bank"], :]
                    if u["kind"] == "t":
                        act.wait_ge(*aux_sum.at(l, n_aux))
                        w = u["tiles"]
                        nc.scalar.activation(region[u["name"]][:, 0:w, u["ch"] * 128:(u["ch"] + 1) * 128],
                                             bank[:, 0:w * 128].rearrange("p (m c) -> p m c", m=w), ACT.Copy)\
                            .then_inc(w_act.sem, 1)
                        continue
                    act.wait_ge(*chunk_sum.at(l, u["q"] + 1))
                    w = u["tokens"]
                    if u["temp"]:
                        before = [v for v in units if v["kind"] == "t"]
                        mine = [i_ for i_, v in enumerate(units) if v is u][0]
                        t_before = sum(v["kind"] != "w" for v in units[:mine])
                        if t_before:
                            act.wait_ge(*aux_sum.at(l, t_before))
                        o = vtmp[:, u["q"] % 2, 0:w]
                    else:
                        o = region[u["name"]][:, u["ch"], 0:w]
                    if u["name"] in ("su", "sv"):
                        nc.scalar.activation(o, bank[:, 0:w], ACT.Gelu_apprx_tanh).then_inc(w_act.sem, 1)
                    elif u["name"] in ("dq", "nq"):
                        nc.scalar.activation(o, bank[:, 0:w], ACT.Copy, scale=0.125).then_inc(w_act.sem, 1)
                    else:
                        nc.scalar.activation(o, bank[:, 0:w], ACT.Copy).then_inc(w_act.sem, 1)
                for g in range(4):
                    act.wait_ge(*pool_sum.at(l, g + 1))
                    nc.scalar.activation(region["pz"][:, g, 0:tok], PS[:, 4 + g, 0:tok], ACT.Copy,
                                         scale=par[:, P_PSC + g:P_PSC + g + 1]).then_inc(pool_out.sem, 1)
                blocks, nb = BL[l], NB[l]
                tr, tr_n = TU[l]

                def attention(i_):
                    if i_ < nb:
                        kind, s, qt, h = blocks[i_]
                        nk = 2 * T if s == 0 else T
                        act.wait_ge(*maxes.at(l, i_ + 1))
                        if i_ >= 2:
                            t_last = max(u["t"] for u in tr if u["kind"] == "p" and u["b"] == i_ - 2)
                            act.wait_ge(*tr_made.at(l, t_last + 1))
                        for a in range(2):
                            ins = nc.scalar.activation(p_t[:, i_ % 2, a, 0:nk], PS[:, a, 0:nk], ACT.Exp,
                                                       bias=nmx[:, i_ % 2, a:a + 1],
                                                       accum_out=rs[:, i_ % 2, a:a + 1])
                        ins.then_inc(exps.sem, 1)
                    for u in tr:
                        if u["slot"] != i_ or u["by"] != "act":
                            continue
                        act.wait_ge(*tr_made.at(l, u["t"] + 1))
                        bank = PS[:, 2 + u["t"] % 2, :]
                        if u["kind"] == "p":
                            b = u["b"]
                            nkt = 4 if blocks[b][1] == 0 else 2
                            readers = [v["b"] for v in tr[:u["t"]] if v["kind"] == "p" and v["t"] % 2 == u["t"] % 2]
                            if readers:
                                act.wait_ge(*pv.at(l, readers[-1] + 1))
                            nc.scalar.activation(at[:, u["t"] % 2, 0:nkt * 128], bank[:, 0:nkt * 128], ACT.Copy)\
                                .then_inc(at_act.sem, 1)
                        else:
                            kind, s, qt, _ = blocks[4 * u["g"]]
                            dst = region["dq" if kind == "diff" else "nq"][:, :, s * T + qt * 128:s * T + (qt + 1) * 128]
                            src = bank.rearrange("p (a b) -> p a b", a=4)
                            if kind == "diff":
                                act.wait_ge(*lam_ready.at(l, 1))
                                nc.scalar.activation(dst, src, ACT.Copy, scale=subg).then_inc(at_act.sem, 1)
                            else:
                                nc.scalar.activation(dst, src, ACT.Copy).then_inc(at_act.sem, 1)
                    g = (i_ - 5) // 4
                    if (i_ - 5) % 4 == 0 and 0 <= g < NG[l] and blocks[4 * g][0] == "diff":
                        act.wait_ge(*pv.at(l, 4 * g + 4))
                        if g >= 1:
                            act.wait_ge(*tr_made.at(l, [u["t"] for u in tr if u["kind"] == "o" and u["g"] == g - 1][0] + 1))
                        nc.scalar.activation(on, PS[:, 4, :], ACT.Square).then_inc(o_square.sem, 1)

                bc = 0
                for u in MERGE[l]:
                    n = u["n"]
                    act.wait_ge(*chunk_sum.at(l, NW + n + 1))
                    if n >= 2:
                        act.wait_ge(*merged.at(l, n - 1))
                    nc.scalar.activation(sgt[:, n % 2, 0:tok], PS[:, 5, 0:tok], ACT.Sigmoid).then_inc(sigs.sem, 1)
                    for slot in u["att"]:
                        attention(slot)
                    high(l, NW + n + 2)
                    if n >= 2 * KD + 1:
                        for _, (ml, q) in MERGE[l][n - 1]["mod"]:
                            for s in range(streams(ml) if q // KD == 2 else 1):
                                act.wait_ge(*gate_bc.at(l, bc + 1))
                                dst = g1b[:, s, (q % KD) * 128:(q % KD + 1) * 128] if q // KD == 2 else \
                                    g2r[:, (q % KD) * 128:(q % KD + 1) * 128]
                                nc.scalar.activation(dst, PS[:, bc % 2, 0:128], ACT.Copy).then_inc(gate_rows.sem, 1)
                                bc += 1
                for _, (ml, q) in MERGE[l][-1]["mod"]:
                    for s in range(streams(ml) if q // KD == 2 else 1):
                        act.wait_ge(*gate_bc.at(l, bc + 1))
                        dst = g1b[:, s, (q % KD) * 128:(q % KD + 1) * 128] if q // KD == 2 else \
                            g2r[:, (q % KD) * 128:(q % KD + 1) * 128]
                        nc.scalar.activation(dst, PS[:, bc % 2, 0:128], ACT.Copy).then_inc(gate_rows.sem, 1)
                        bc += 1
                for k in range(KD):
                    act.wait_ge(*merged.at(l, NM - KD + k + 1))
                    act.wait_ge(*chunk_sum.at(l, NW + NM))
                    nc.scalar.activation(hTr[:, 0, k, 0:tok], mT[l][:, k, :], ACT.Copy).then_inc(m_hi.sem, 1)
                if l == 0:
                    act.wait_ge(*m_lo.at(l, KD))
                    act.dma_start(x[:, 0:2, :], A["x"].rearrange("o (m p) d -> p (o m) d", p=128)).then_inc(x_back, 16)
                    act.dma_start(x[:, 2:4, :], A["ctx"].rearrange("o (m p) d -> p (o m) d", p=128)).then_inc(x_back, 16)
                for k in range(2, KD):
                    high(l, NW + NM + k)
                act.wait_ge(*mix_x.at(l, 2 * NT[l]))
                squares(2 * l + 1, NS)
                act.wait_ge(*mod_ready.at(l, 2 if l == 0 else 1))
                modulate(2 * l + 1, 1, NS)
                act.wait_ge(*r_max.at(l, 1))
                for m in range(NT[l]):
                    nc.scalar.activation(rex[:, m, :], PS[:, 0, m * E:(m + 1) * E], ACT.Exp, bias=rmx[:, m:m + 1],
                                         accum_out=rsum[:, m:m + 1]).then_inc(r_exp.sem, 1)
                with act.Fori(0, NP[l]) as i:
                    def when(sig, n, k):
                        sem, val = sig.at(l, k)
                        act.wait_ge(sem, i * n + val)

                    when(combT_made, 1, 1)
                    nc.scalar.activation(combT[:, 0:NT[l], :].rearrange("p a b -> p (a b)"), PS[:, 4, 0:NT[l] * 128],
                                         ACT.Copy).then_inc(combT_ready.sem, 1)
                    when(h1_sum, 1, 1)
                    for h in range(2):
                        nc.scalar.activation(sil[:, h * 512:(h + 1) * 512], PS[:, h, :], ACT.Silu)\
                            .then_inc(sil_ready.sem, 1)
                    when(hidT_made, 2, 1)
                    nc.scalar.activation(hidT[:, 0:4, :].rearrange("p a b -> p (a b)"), PS[:, 6, :], ACT.Copy)\
                        .then_inc(hidT_act.sem, 1)
            act.wait_ge(*comb_x.at(L - 1, 2 * NT[L - 1] * NP[L - 1]))
            squares(4, 1)

        @block.gpsimd
        def _(pool):
            steps = [0]

            def step(ins):
                steps[0] += 1
                ins.then_inc(pool_step, 1)
                pool.wait_ge(pool_step, steps[0])

            rpb_v = A["na_rpb"]

            def load_bias(l):
                for h in range(8):
                    for r in range(2):
                        start = ((l * 8 + h) * RPB_R + (RPB_R // 2 - 3)) * RPB_C + RPB_C * r + RPB_C // 2 - 63
                        src = bass.AP(tensor=rpb_v.tensor, offset=rpb_v.offset + start,
                                      ap=[[1, 64], [RPB_C, 6], [1, GRID_W]])
                        pool.dma_start(nab[64 * r:64 * r + 64, h, :].rearrange("p (i c) -> p i c", i=6), src)\
                            .then_inc(bias_loaded, 16)

            def inverse_root(sq, mean, root, n, scale, ready):
                step(pool.tensor_scalar(mean[:, 0:n], sq, scale, EPS, ALU.mult, ALU.add))
                pool.tensor_tensor(root[:, 0:n], mean[:, 0:n], half[:, 0:n], ALU.pow).then_inc(ready, 1)

            pool.memset(cond[:, :, :], 0.0).then_inc(cond_ready, 1)
            pool.memset(half, -0.5).then_inc(half_ready, 1)
            pool.wait_ge(half_ready, 1)
            for l in range(L):
                NS = streams(l)
                tok = NS * T
                if l:
                    pool.wait_ge(*logits.at(l - 1, 1))
                pool.dma_start(par[:, :], A["par"][l]).then_inc(par_loaded, 16)
                pool.wait_ge(*sq_done.at(2 * l, 4))
                inverse_root(ss[:, 0:4], ms, rstd, 4, 1.0 / D, rstd_done.sem)
                load_bias(l)
                pool.wait_ge(*v_stats.at(l, 1))
                inverse_root(vmv[:, 0:2 * NS, 1], vms, vrstd, 2 * NS, 1.0, v_rstd.sem)
                n = last_of(WU[l][0], "pz", "w")
                pool.wait_ge(*w_act.at(l, n["act"]))
                pool.wait_ge(*w_dve.at(l, n["dve"]))
                pool.wait_ge(consts_loaded, 48)
                PW = T + 16
                za, zb = (work[:, 2 * i_:2 * i_ + 2, :].rearrange("p a b -> p (a b)")[:, 0:2 * PW].rearrange(
                    "p (s t) -> p s t", s=2) for i_ in (0, 1))
                for g, w in enumerate(POOL_W):
                    z = region["pz"][:, g, 0:tok].rearrange("p (s t) -> p s t", s=NS)
                    step(pool.memset(za[:, 0:NS, 0:8], 0.0))
                    step(pool.memset(za[:, 0:NS, T + 8:PW], 0.0))
                    step(pool.tensor_copy(za[:, 0:NS, 8:8 + T], z))
                    cur, nxt, n, span = za, zb, PW, 1
                    while span < w:
                        n -= span
                        step(pool.tensor_tensor(nxt[:, 0:NS, 0:n], cur[:, 0:NS, 0:n], cur[:, 0:NS, span:span + n],
                                                ALU.add))
                        cur, nxt, span = nxt, cur, 2 * span
                    c0 = 8 - w // 2
                    step(pool.tensor_scalar(nxt[:, 0:NS, 8:T - 8], cur[:, 0:NS, c0 + 8:c0 + T - 8], 1.0 / w, None, ALU.mult))
                    for e in range(2):
                        cnt = cst[:, C_CNT + g * 16 + 8 * e:C_CNT + g * 16 + 8 * e + 8].unsqueeze(1).broadcast_to([128, NS, 8])
                        o = e * (T - 8)
                        step(pool.tensor_tensor(nxt[:, 0:NS, o:o + 8], cur[:, 0:NS, c0 + o:c0 + o + 8], cnt, ALU.mult))
                    pool.tensor_tensor(z, nxt[:, 0:NS, 0:T], z, ALU.subtract).then_inc(pooled.sem, 1)
                    pool.wait_ge(*pooled.at(l, g + 1))
                pool.wait_ge(bias_loaded, 16 * 16 * (l + 1))
                tb = nab[:, :, :].rearrange("p h (i c) -> p (h i) c", c=GRID_W)
                pool.tensor_tensor(tb, tb, cst[:, C_MASK:C_MASK + GRID_W].unsqueeze(1).broadcast_to([128, 48, GRID_W]),
                                   ALU.add).then_inc(bias_masked.sem, 1)
                for g in range(NG[l] // 2):
                    pool.wait_ge(*o_ss.at(l, g + 1))
                    inverse_root(oss[:, 0:4], oms, orstd, 4, 1.0 / 128, o_rstd.sem)
                pool.wait_ge(*sq_done.at(2 * l + 1, 2 * NS))
                inverse_root(ss[:, 0:2 * NS], ms, rstd, 2 * NS, 1.0 / D, rstd_done.sem)
            pool.wait_ge(*sq_done.at(4, 2))
            inverse_root(ss[:, 0:2], ms, rstd, 2, 1.0 / D, rstd_done.sem)

        @block.vector
        def _(dve):
            steps = [0]

            def step(ins):
                steps[0] += 1
                ins.then_inc(dve_step, 1)
                dve.wait_ge(dve_step, steps[0])

            def low(l, j):
                if j >= NC_ALL:
                    return
                slot, _ = item_at["chunk", l, j]
                dve.wait_ge(*w_hi.at(l, j + 1))
                nc.vector.tensor_tensor(wr[:, j % 2, 1, :], ring[:, slot, :], wr[:, j % 2, 0, :].bitcast(f32),
                                        ALU.subtract).then_inc(w_lo.sem, 1)

            def mod_out(l, n):
                dve.wait_ge(*mod_sum.at(l, n + 1))
                nc.vector.tensor_copy(modp[:, n % 2, :], PS[:, 7, 0:128]).then_inc(mod_part.sem, 1)

            def mod_columns(l, ml, norm, sec):
                dve.wait_ge(*mod_cols.at(l, sec))
                cols = PS[:, 7, 256 + 32 * norm:288 + 32 * norm].rearrange("p (a k s) -> p a s k", a=2, s=2)
                g0 = (S_N1 if norm == 0 else S_N2) + KD * ml
                step(nc.vector.tensor_scalar(modA[:, norm, :, :], cols[:, 1, :, :], 1.0, None, ALU.add))
                for s in range(2):
                    step(nc.vector.tensor_tensor(modA[:, norm, s, :], modA[:, norm, s, :], stay[:, g0:g0 + KD], ALU.mult))
                nc.vector.tensor_copy(modB[:, norm, :, :], cols[:, 0, :, :]).then_inc(mod_ready.sem, 1)

            def normalise(nn, n_streams):
                dve.wait_ge(*rstd_done.at(nn, 1))
                for m in range(2 * n_streams):
                    nc.vector.tensor_scalar(xn[:, m, :], x[:, m, :], rstd[:, m:m + 1], None, ALU.mult)\
                        .then_inc(xn_ready.sem, 1)

            def modulate(nn, norm, n_streams):
                for b in range(4 * n_streams):
                    s, kp = b // 4, b % 4
                    if b % 2:
                        dve.wait_ge(*xt_ready.at(nn, b + 1))
                        if b >= 4:
                            dve.wait_ge(*h_lo.at(nn, b - 3))
                        for kk in range(2):
                            k = 2 * kp + kk
                            ins = nc.vector.tensor_scalar(htmp[:, b % 4, kk * T:(kk + 1) * T], PS[:, b, kk * T:(kk + 1) * T],
                                                          modA[:, norm, s, k:k + 1], modB[:, norm, s, k:k + 1],
                                                          ALU.mult, ALU.add)
                        ins.then_inc(tmp_dve.sem, 1)
                        dve.wait_ge(*tmp_dve.at(nn, b // 2 + 1))
                    dve.wait_ge(*h_hi.at(nn, b + 1))
                    nc.vector.tensor_tensor(hTr[:, 1, 2 * kp:2 * kp + 2, s * T:(s + 1) * T],
                                            htmp[:, b % 4, :].rearrange("p (k t) -> p k t", k=2),
                                            hTr[:, 0, 2 * kp:2 * kp + 2, s * T:(s + 1) * T].bitcast(f32),
                                            ALU.subtract).then_inc(h_lo.sem, 1)

            dve.wait_ge(consts_loaded, 48)
            for n in range(MOD0):
                mod_out(0, n)
            mod_columns(0, 0, 0, 1)
            dve.wait_ge(x_loaded, 32)
            for l in range(L):
                NS = streams(l)
                tok = NS * T
                lam_init = 0.8 - 0.6 * math.exp(-0.3 * l)
                normalise(2 * l, 2)
                low(l, 0)
                low(l, 1)
                modulate(2 * l, 0, 2)
                dve.wait_ge(*rw_hi.at(l, 1))
                nc.vector.tensor_tensor(rwr[:, 1, :], par[:, P_RW:P_RW + KD * E], rwr[:, 0, :].bitcast(f32), ALU.subtract)\
                    .then_inc(rw_lo.sem, 1)
                lp = par[:, P_LAM:P_LAM + 256].rearrange("p (a b c) -> p a b c", a=2, b=2)
                lt = modp[:, 0, :].rearrange("p (a c) -> p a c", a=2)
                step(nc.vector.tensor_tensor(lt, lp[:, :, 0, :], lp[:, :, 1, :], ALU.mult))
                nc.vector.reduce_sum(lam[:, 0:2], lt, axis=AX.X).then_inc(lam_prod.sem, 1)
                dve.wait_ge(*lam_exp.at(l, 1))
                step(nc.vector.tensor_tensor(lam[:, 4:5], lam[:, 3:4], lam[:, 2:3], ALU.subtract))
                step(nc.vector.tensor_scalar(lam[:, 5:6], lam[:, 4:5], -lam_init, None, ALU.add))
                nc.vector.tensor_scalar(subg, par[:, P_SUBG:P_SUBG + 1], 1.0 - lam_init, None, ALU.mult)\
                    .then_inc(lam_ready.sem, 1)
                units, counts = WU[l]
                n_aux = 0
                sv_last = last_of(units, "sv", "t")
                for pos, u in enumerate(units):
                    if u["kind"] == "w":
                        low(l, u["q"] + 2)
                    else:
                        n_aux += 1
                    if u["by"] == "dve":
                        bank = PS[:, u["bank"], :]
                        if u["kind"] == "rope":
                            dve.wait_ge(*aux_sum.at(l, n_aux))
                            two = region[u["name"]][:, 2 * u["pair"]:2 * u["pair"] + 2, 0:T]
                            turned = work[:, 4, :].rearrange("p (a b) -> p a b", a=2)
                            sin2, cos2 = (v.unsqueeze(1).broadcast_to([128, 2, T]) for v in (sinT, cosT))
                            step(nc.vector.tensor_tensor(turned, bank.rearrange("p (a b) -> p a b", a=2), sin2, ALU.mult))
                            step(nc.vector.tensor_tensor(two, two, cos2, ALU.mult))
                            nc.vector.tensor_tensor(two, two, turned, ALU.add).then_inc(w_dve.sem, 1)
                            dve.wait_ge(*w_dve.at(l, u["nth"]))
                        elif u["kind"] == "f":
                            g = u["g"]
                            dve.wait_ge(*aux_sum.at(l, n_aux))
                            b_ = par[:, P_SGUB + g * 128:P_SGUB + (g + 1) * 128].unsqueeze(1).broadcast_to([128, 2 * NS, 128])
                            t_ = work[:, 5, 0:tok]
                            step(nc.vector.scalar_tensor_tensor(
                                out=t_.rearrange("p (m q) -> p m q", q=128),
                                in0=bank[:, 0:tok].rearrange("p (m q) -> p m q", q=128),
                                scalar=par[:, P_SGUG + g:P_SGUG + g + 1], in1=b_, op0=ALU.mult, op1=ALU.add))
                            u_ = region["su"][:, g, 0:tok]
                            nc.vector.tensor_tensor(u_, u_, t_, ALU.mult).then_inc(w_dve.sem, 1)
                            dve.wait_ge(*w_dve.at(l, u["nth"]))
                        elif u["kind"] == "t":
                            dve.wait_ge(*aux_sum.at(l, n_aux))
                            w = u["tiles"]
                            nc.vector.tensor_copy(region[u["name"]][:, 0:w, u["ch"] * 128:(u["ch"] + 1) * 128],
                                                  bank[:, 0:w * 128].rearrange("p (m c) -> p m c", m=w))\
                                .then_inc(w_dve.sem, 1)
                        else:
                            dve.wait_ge(*chunk_sum.at(l, u["q"] + 1))
                            w = u["tokens"]
                            if u["temp"]:
                                t_before = sum(v["kind"] != "w" for v in units[:pos])
                                if t_before:
                                    dve.wait_ge(*aux_sum.at(l, t_before))
                                o = vtmp[:, u["q"] % 2, 0:w]
                            else:
                                o = region[u["name"]][:, u["ch"], 0:w]
                            if u["name"] in ("dq", "nq"):
                                nc.vector.tensor_scalar(o, bank[:, 0:w], 0.125, None, ALU.mult).then_inc(w_dve.sem, 1)
                            else:
                                nc.vector.tensor_copy(o, bank[:, 0:w]).then_inc(w_dve.sem, 1)
                    if u["kind"] == "w" and u["name"] == "pz" and u["ch"] == 1:
                        dve.wait_ge(*w_act.at(l, sv_last["act"]))
                        dve.wait_ge(*w_dve.at(l, sv_last["dve"]))
                        v_ = region["sv"]
                        for m in range(2 * NS):
                            step(nc.vector.bn_stats(vst[:, m, :], v_[:, m, :]))
                            ins = nc.vector.bn_aggr(vmv[:, m, :], vst[:, m, :])
                        ins.then_inc(v_stats.sem, 1)
                    if u["kind"] == "w" and u["name"] == "pz" and u["ch"] == 3:
                        dve.wait_ge(*v_rstd.at(l, 1))
                        for m in range(2 * NS):
                            nc.vector.tensor_scalar(v_[:, m, :], v_[:, m, :], vmv[:, m, 0:1], vrstd[:, m:m + 1],
                                                    ALU.subtract, ALU.mult).then_inc(v_norm.sem, 1)
                blocks, nb = BL[l], NB[l]
                tr, tr_n = TU[l]

                def attention(i_):
                    if i_ < nb:
                        s = blocks[i_][1]
                        nk = 2 * T if s == 0 else T
                        dve.wait_ge(*scores.at(l, i_ + 1))
                        if i_ >= 2:
                            dve.wait_ge(*exps.at(l, i_ - 1))
                        nc.vector.reduce_max(nmx[:, i_ % 2, :], PS[:, 0:2, 0:nk], axis=AX.X,
                                             negate=True).then_inc(maxes.sem, 1)
                    b = i_ - 1
                    if 0 <= b < nb:
                        kind, s, qt, h = blocks[b]
                        nk = 2 * T if s == 0 else T
                        dve.wait_ge(*exps.at(l, b + 1))
                        if kind == "diff":
                            r_ = rr[:, b % 2, :]
                            step(nc.vector.reciprocal(r_, rs[:, b % 2, :]))
                            step(nc.vector.tensor_tensor(r_[:, 1:2], r_[:, 1:2], lam[:, 5:6], ALU.mult))
                            step(nc.vector.tensor_scalar(p_t[:, b % 2, 0, 0:nk], p_t[:, b % 2, 0, 0:nk], r_[:, 0:1], None,
                                                         ALU.mult))
                            nc.vector.scalar_tensor_tensor(out=p_t[:, b % 2, 0, 0:nk], in0=p_t[:, b % 2, 1, 0:nk],
                                                           scalar=r_[:, 1:2], in1=p_t[:, b % 2, 0, 0:nk],
                                                           op0=ALU.mult, op1=ALU.add).then_inc(probs.sem, 1)
                        else:
                            nc.vector.reciprocal(nar[:, (b // 4) % 4, 2 * h:2 * h + 2], rs[:, b % 2, :])\
                                .then_inc(probs.sem, 1)
                    for u in tr:
                        if u["slot"] != i_ or u["by"] != "dve":
                            continue
                        nkt = 4 if blocks[u["b"]][1] == 0 else 2
                        dve.wait_ge(*tr_made.at(l, u["t"] + 1))
                        dve.wait_ge(*pv.at(l, u["b"]))
                        nc.vector.tensor_copy(at[:, u["t"] % 2, 0:nkt * 128], PS[:, 2 + u["t"] % 2, 0:nkt * 128])\
                            .then_inc(at_dve.sem, 1)
                    g = (i_ - 5) // 4
                    if (i_ - 5) % 4 == 0 and 0 <= g < NG[l]:
                        kind = blocks[4 * g][0]
                        o_ = PS[:, 4, :]
                        if g >= 1:
                            t_o = [u["t"] for u in tr if u["kind"] == "o" and u["g"] == g - 1][0]
                            dve.wait_ge(*tr_made.at(l, t_o + 1))
                        if kind == "diff":
                            dve.wait_ge(*o_square.at(l, g + 1))
                            nc.vector.reduce_sum(oss, on.rearrange("p (a b) -> p a b", a=4), axis=AX.X)\
                                .then_inc(o_ss.sem, 1)
                            dve.wait_ge(*o_rstd.at(l, g + 1))
                            nc.vector.tensor_tensor(on.rearrange("p (a b) -> p a b", a=4),
                                                    o_.rearrange("p (a b) -> p a b", a=4),
                                                    orstd.unsqueeze(2).broadcast_to([128, 4, 128]), ALU.mult)\
                                .then_inc(o_norm.sem, 1)
                        else:
                            dve.wait_ge(*pv.at(l, 4 * g + 4))
                            dve.wait_ge(*probs.at(l, 4 * g + 4))
                            nc.vector.tensor_tensor(on.rearrange("p (a b) -> p a b", a=8),
                                                    o_.rearrange("p (a b) -> p a b", a=8),
                                                    nar[:, g % 4, :].unsqueeze(2).broadcast_to([128, 8, 64]), ALU.mult)\
                                .then_inc(o_norm.sem, 1)

                done = MOD0 if l == 0 else 0
                for u in MERGE[l]:
                    n, v = u["n"], u["v"]
                    for slot in u["att"][0:1]:
                        attention(slot)
                    dve.wait_ge(*sigs.at(l, n + 1))
                    dve.wait_ge(*projs.at(l, n + 1))
                    if u["p"] == 0:
                        nc.vector.tensor_tensor(mT[l][:, v, :], sgt[:, n % 2, 0:tok], PS[:, 6, 0:tok], ALU.mult)\
                            .then_inc(gated.sem, 1)
                        dve.wait_ge(*gated.at(l, n + 1))
                        dve.sem_inc(merged.sem, 1)
                    else:
                        nc.vector.tensor_tensor(sgt[:, n % 2, 0:tok], sgt[:, n % 2, 0:tok], PS[:, 6, 0:tok], ALU.mult)\
                            .then_inc(gated.sem, 1)
                        dve.wait_ge(*gated.at(l, n + 1))
                        nc.vector.tensor_tensor(mT[l][:, v, :], mT[l][:, v, :], sgt[:, n % 2, 0:tok], ALU.add)\
                            .then_inc(merged.sem, 1)
                    for slot in u["att"][1:]:
                        attention(slot)
                    for m_, (ml, q) in u["mod"]:
                        if m_ == len(mod_steps(l)[0]):
                            mod_columns(l, l, 1, 3 if l == 0 else 1)
                            if l + 1 < L:
                                mod_columns(l, l + 1, 0, 3)
                        mod_out(l, done + m_)
                    low(l, NW + n + 2)
                for k in range(KD):
                    dve.wait_ge(*m_hi.at(l, k + 1))
                    nc.vector.tensor_tensor(hTr[:, 1, k, 0:tok], mT[l][:, k, :], hTr[:, 0, k, 0:tok].bitcast(f32),
                                            ALU.subtract).then_inc(m_lo.sem, 1)
                for k in range(2, KD):
                    low(l, NW + NM + k)
                dve.wait_ge(*gate_rows.at(l, NGB[l]))
                if l == 0:
                    dve.wait_ge(x_back, 32)
                for c in range(2 * NT[l]):
                    m, h = c // 2, c % 2
                    dve.wait_ge(*mix_sum.at(l, c + 1))
                    t_ = work[:, 7 + c % 2, :]
                    if c >= 2:
                        dve.wait_ge(*mix_x.at(l, c - 1))
                    step(nc.vector.tensor_tensor(t_, PS[:, c, :], g1b[:, m // 2, h * 512:(h + 1) * 512], ALU.mult))
                    nc.vector.tensor_tensor(x[:, m, h * 512:(h + 1) * 512], x[:, m, h * 512:(h + 1) * 512], t_, ALU.add)\
                        .then_inc(mix_x.sem, 1)
                dve.wait_ge(*mix_x.at(l, 2 * NT[l]))
                normalise(2 * l + 1, NS)
                modulate(2 * l + 1, 1, NS)
                dve.wait_ge(*logits.at(l, 1))
                nc.vector.reduce_max(rmx[:, 0:NT[l]], PS[:, 0, 0:NT[l] * E].rearrange("p (m e) -> p m e", e=E), axis=AX.X,
                                     negate=True).then_inc(r_max.sem, 1)
                dve.wait_ge(*r_exp.at(l, NT[l]))
                step(nc.vector.reciprocal(rinv[:, 0:NT[l]], rsum[:, 0:NT[l]]))
                for m in range(NT[l]):
                    ins = nc.vector.tensor_scalar(aff[:, m % 2, m // 2, :], rex[:, m, :], rinv[:, m:m + 1], None, ALU.mult)
                ins.then_inc(aff_ready.sem, 1)
                step(nc.vector.memset(selg[:, :, :], 0.0))
                RE = NS * E
                dve.wait_ge(*affT_made.at(l, 1))
                step(nc.vector.tensor_copy(afT[0:RE, :], PS[0:RE, 1, 0:T]))
                src = afT[0:RE, :]
                for r in range(CAP // 8):
                    step(nc.vector.max(top[0:RE, 8 * r:8 * r + 8], src))
                    step(nc.vector.match_replace(afR[0:RE, (r + 1) % 2, :], top[0:RE, 8 * r:8 * r + 8], src, -1.0))
                    src = afR[0:RE, (r + 1) % 2, :]
                assert (CAP // 8) % 2 == 0
                nc.vector.tensor_tensor(afR[0:RE, 0, :], afT[0:RE, :], afR[0:RE, 0, :], ALU.not_equal)\
                    .then_inc(mask_ready.sem, 1)
                dve.wait_ge(*maskT_made.at(l, 1))
                nc.vector.tensor_copy(msk[:, :, 0:RE], PS[:, 2, 0:64].rearrange("p (j e) -> p j e", j=2)[:, :, 0:RE])\
                    .then_inc(maskT_ready.sem, 1)
                dve.wait_ge(*maskT_ready.at(l, 1))
                dve.wait_ge(*count_made.at(l, 1))
                nc.vector.tensor_tensor(place[:, :, 0:NS, :].rearrange("p j s e -> p j (s e)"),
                                        PS[:, 3, 0:64].rearrange("p (j e) -> p j e", j=2)[:, :, 0:RE],
                                        msk[:, :, 0:RE], ALU.mult).then_inc(place_ready.sem, 1)
                dve.wait_ge(*place_ready.at(l, 1))
                G = GE[l]
                with dve.Fori(0, NP[l]) as i:
                    def when(sig, n, k):
                        sem, val = sig.at(l, k)
                        dve.wait_ge(sem, i * n + val)

                    for s in range(NS):
                        sp = selp[:, s * 2 * G * CAP:(s + 1) * 2 * G * CAP].rearrange("p (j g c) -> p j g c", j=2, g=G)
                        pl = place[:, :, s, ds(i * G, G)].unsqueeze(3).broadcast_to([128, 2, G, CAP])
                        io = iota1.unsqueeze(1).unsqueeze(1).broadcast_to([128, 2, G, CAP])
                        nc.vector.tensor_tensor(sp, pl, io, ALU.is_equal).then_inc(sel_ready.sem, 1)
                    when(sel_ready, NS, NS)
                    for s in range(NS):
                        sp = selp[:, s * 2 * G * CAP:(s + 1) * 2 * G * CAP].rearrange("p (j g c) -> p j g c", j=2, g=G)
                        af = aff[:, :, s, ds(i * G, G)].unsqueeze(3).broadcast_to([128, 2, G, CAP])
                        sg = selg[:, 2 * s:2 * s + 2, :].rearrange("p j (g s c) -> p j g s c", g=G, s=NS)[:, :, :, s, :]
                        nc.vector.tensor_tensor(sg, sp, af, ALU.mult).then_inc(selg_ready.sem, 1)
                    c = 0
                    for bk in range(2):
                        when(gathered, 2, bk + 1)
                        for s in range(NS):
                            o = xsT[:, 4 * bk:4 * bk + 4, :].rearrange("p k (g s c) -> p k g s c", g=G, s=NS)[:, :, :, s, :]
                            src = PS[:, 6 + bk, :].rearrange("p (k g s c) -> p k g s c", k=4, g=G, s=NS)[:, :, :, s, :]
                            ga = modA[:, 1, s, 4 * bk:4 * bk + 4].unsqueeze(2).unsqueeze(2).broadcast_to([128, 4, G, CAP])
                            sh = modB[:, 1, s, 4 * bk:4 * bk + 4].unsqueeze(2).unsqueeze(2).broadcast_to([128, 4, G, CAP])
                            nc.vector.tensor_tensor(o, src, ga, ALU.mult).then_inc(xs_mul.sem, 1)
                            c += 1
                            when(xs_mul, 2 * NS, c)
                            nc.vector.tensor_tensor(o, o, sh, ALU.add).then_inc(xs_ready.sem, 1)
                    when(h3_sum, 1, 1)
                    for h in range(2):
                        when(sil_ready, 2, h + 1)
                        nc.vector.tensor_tensor(hid[:, h * 512:(h + 1) * 512], sil[:, h * 512:(h + 1) * 512],
                                                PS[:, 2 + h, :], ALU.mult).then_inc(hid_ready.sem, 1)
                    when(hidT_made, 2, 2)
                    nc.vector.tensor_copy(hidT[:, 4:8, :].rearrange("p a b -> p (a b)"), PS[:, 7, :])\
                        .then_inc(hidT_dve.sem, 1)
                    when(y_sum, 1, 1)
                    for h in range(2):
                        nc.vector.tensor_tensor(ysb[:, h * 512:(h + 1) * 512], PS[:, 4 + h, :],
                                                g2r[:, h * 512:(h + 1) * 512], ALU.mult).then_inc(y_ready.sem, 1)
                    for c in range(2 * NT[l]):
                        m, h = c // 2, c % 2
                        when(comb_sum, 2 * NT[l], c + 1)
                        xs_ = x[:, m, h * 512:(h + 1) * 512]
                        nc.vector.tensor_tensor(xs_, xs_, PS[:, c % 4, :], ALU.add).then_inc(comb_x.sem, 1)
                dve.wait_ge(*comb_x.at(l, 2 * NT[l] * NP[l]))
            dve.wait_ge(*rstd_done.at(4, 1))
            dve.wait_ge(consts_loaded, 64)
            for m in range(2):
                o_ = fin_out[:, m * D:(m + 1) * D]
                step(nc.vector.tensor_scalar(o_, x[:, m, :], rstd[:, m:m + 1], None, ALU.mult))
                nc.vector.tensor_tensor(o_, o_, fin_gain, ALU.mult).then_inc(fin_ready, 1)


def layout(inputs):
    a = {k: np.ascontiguousarray(np.asarray(v)) for k, v in inputs.items()}
    cols = lambda v, n: np.ascontiguousarray(v.reshape(n, 128).T)
    wide = lambda v: np.broadcast_to(v.reshape(1, -1), (128, v.size))
    par = np.zeros((L, 128, P_ALL), np.float32)
    stay = np.zeros((128, S_ALL), np.float32)
    for l in range(L):
        par[l, :, P_POOLW:P_POOLW + 512] = a["pool_w"][l].transpose(1, 0, 2).reshape(128, 512)
        par[l, :, P_SGUW:P_SGUW + 512] = a["sgu_w"][l].transpose(2, 0, 1).reshape(128, 512)
        par[l, :, P_SGUB:P_SGUB + 512] = wide(a["sgu_b"][l])
        par[l, :, P_LAM:P_LAM + 256] = wide(a["diff_lambda"][l])
        par[l, :, P_RW:P_RW + KD * E] = a["router_w"][l].reshape(KD, 128, E).transpose(1, 0, 2).reshape(128, KD * E)
        par[l, :, P_PSC:P_PSC + 4] = cols(a["pool_scale"][l], 4)
        par[l, :, P_SUBG:P_SUBG + 1] = cols(a["diff_subln_g"][l], 1)
        par[l, :, P_SGUG:P_SGUG + 4] = cols(a["sgu_norm_g"][l], 4)
        stay[:, S_N1 + KD * l:S_N1 + KD * (l + 1)] = cols(a["norm1_g"][l], KD)
        stay[:, S_N2 + KD * l:S_N2 + KD * (l + 1)] = cols(a["norm2_g"][l], KD)
    stay[:, S_C:S_C + KD] = cols(a["c"][0], KD)
    stay[:, S_C + KD:S_C + 2 * KD] = cols(a["c_ctx"], KD)
    d = {n: a[n] for n in ("x", "ctx", "w_mod", "b_mod", "w_in", "w_br", "w_out", "na_rpb", "moe_w1", "moe_w3", "moe_w2")}
    d.update(par=par, stay=stay, cst=shape_constants(), final_g=np.ascontiguousarray(wide(a["final_g"])))
    return d


def kernel(**inputs):
    import concourse.bacc as bacc
    from concourse.bass_utils import run_bass_kernel_spmd

    nc = bacc.Bacc("TRN2", target_bir_lowering=False, num_devices=1)
    arrays = layout(inputs)
    aps = {k: nc.dram_tensor(f"in_{k}", v.shape, mybir.dt.from_np(v.dtype), kind="ExternalInput").ap()
           for k, v in arrays.items()}
    out = nc.dram_tensor("out", (1, T, D), mybir.dt.float32, kind="ExternalOutput").ap()
    build(nc, aps, out)
    r = run_bass_kernel_spmd(nc, [{f"in_{k}": v for k, v in arrays.items()}], core_ids=[0])
    return r.results[0]["out"]
```

```python
import math
from contextlib import ExitStack

import numpy as np
import concourse.bass as bass
from concourse import mybir

D = 1024
T = 256
L = 2
GRID_W = 64
NBR = 4
E = 16
CAP = 2 * T // E
NA_C = 16
RPB_R, RPB_C = 15, 31
POOL_W = (2, 4, 8, 16)
EPS = 1e-6
KD = D // 128
MQ = 256
PQ = D // MQ
NEG = -1.0e30

NSLOT = 6
ESLOT = 12
EXTRA = NSLOT // 2

GROUPS = [("su", "f", 3584), ("sv", "t", 4096), ("pz", "f", 3072), ("dk", "f", 0), ("dv", "t", 512),
          ("nk", "f", 1024), ("nv", "t", 1536), ("dq", "f", 2048), ("nq", "f", 2560)]
KV = ("dk", "dv", "nk", "nv")
GATE_COL = 4608
AUX = ("rope", "f", "pool")
POOL_AFTER = (("dq", 2), ("dq", 3), ("nq", 0), ("nq", 1))
NW = 4 * len(GROUPS)
NC_ALL = NW + NBR * KD + KD
MERGE_ORDER = (0, 2, 1, 3)

C_ID, C_FLIP, C_PERM = 0, 128, 256
C_COS, C_SIN = 384, 640
C_TRI, C_ONE = 896, 1024
C_IOTA, C_MASK = 1152, 1184
C_SELC, C_SELR, C_SELY = 1248, 1250, 1506
C_CNT = 1634
C_ALL = C_CNT + 4 * 16

P_POOLW, P_SGUW, P_RW, P_SGUB, P_LAM = 0, 512, 1024, 1152, 1664
RW_COLS = KD * E + 128 - E
P_PSC, P_SUBG, P_SGUG = 1920, 1924, 1925
P_ALL = 1929
S_N1, S_N2, S_C = 0, 16, 32
S_ALL = 48


def shape_constants():
    c = np.zeros((128, C_ALL), np.float32)
    p = np.arange(128)
    c[:, C_ID:C_ID + 128] = np.eye(128)
    c[:, C_FLIP:C_FLIP + 128] = np.eye(128)[::-1]
    c[p ^ 16, C_PERM + p] = 1.0
    nf = 16
    inv = (10000.0 ** (-np.arange(nf, dtype=np.float32) / nf)).astype(np.float32)
    t = np.arange(T)
    pos = np.stack([(t // GRID_W), (t % GRID_W)]).astype(np.float32)
    f = p % 64
    ang = pos[f // 32] * inv[f % 16][:, None]
    c[:, C_COS:C_COS + T] = np.cos(ang.astype(np.float32))
    c[:, C_SIN:C_SIN + T] = np.sin(ang.astype(np.float32)) * np.where(f % 32 < 16, -1.0, 1.0)[:, None]
    c[:, C_TRI:C_TRI + 128] = p[:, None] <= p[None, :]
    c[:, C_ONE:C_ONE + 128] = 1.0
    c[:, C_IOTA:C_IOTA + CAP] = 1.0 + np.arange(CAP)
    col = 63 - p % 64
    start = np.clip(col - NA_C // 2, 0, GRID_W - NA_C)
    k = np.arange(GRID_W)
    inside = (k[None, :] >= start[:, None]) & (k[None, :] < start[:, None] + NA_C)
    c[:, C_MASK:C_MASK + GRID_W] = np.where(inside, 0.0, NEG)
    for s in range(2):
        c[p % 32 == s, C_SELC + s] = 1.0
        c[p % 32 == s, C_SELR + 128 * s:C_SELR + 128 * s + 128] = 1.0
        c[:, C_SELY:C_SELY + 128] += ((p % 32 == s)[:, None] & ((p // CAP) % 2 == s)[None, :])
    for g, w in enumerate(POOL_W):
        n = np.clip(t + w // 2, 0, T) - np.clip(t - w // 2, 0, T)
        c[:, C_CNT + g * 16:C_CNT + g * 16 + 8] = 1.0 / n[:8].astype(np.float32)
        c[:, C_CNT + g * 16 + 8:C_CNT + g * 16 + 16] = 1.0 / n[-8:].astype(np.float32)
    return c


class Signal:

    def __init__(self, sem, per_layer):
        self.sem, self.per_layer = sem, per_layer

    def at(self, layer, count):
        return self.sem, sum(self.per_layer[:layer]) + count


def streams(l):
    return 2 if l < L - 1 else 1


def by_engine(units):
    n = {"act": 0, "dve": 0}
    for u in units:
        if "by" in u:
            n[u["by"]] += 1
            u["nth"] = n[u["by"]]
    return units, n


def w_units(l):
    units, later, nw, na, nt = [], [], 0, 0, 0
    for i, (name, kind, col) in enumerate(GROUPS):
        wide = name in KV or streams(l) == 2
        tiles = 4 if wide else 2
        for ch in range(4):
            q = 4 * i + ch
            if kind == "f":
                units.append(dict(kind="w", name=name, ch=ch, q=q, tokens=2 * T if wide else T, bank=nw % 4,
                                  by="act" if name == "su" or q % 2 else "dve"))
                nw += 1
            else:
                units.append(dict(kind="part", name=name, ch=ch, q=q, banks=[(nw + m) % 4 for m in range(tiles)]))
                if ch == 3:
                    for m in range(tiles):
                        nt += m < tiles - 1
                        units.append(dict(kind="tile", name=name, m=m, q=q, bank=(nw + m) % 4, last=m == tiles - 1,
                                          sums=nt, by="act" if name == "sv" or m % 2 else "dve"))
                    nw += tiles
            for u in later:
                units.append(dict(u, bank=4 + na % 4))
                na += 1
            later = []
            if name in ("dk", "dq") and ch % 2:
                later.append(dict(kind="rope", name=name, pair=ch // 2, by="dve"))
            if (name, ch) in POOL_AFTER:
                later.append(dict(kind="pool", name="pz", g=POOL_AFTER.index((name, ch)), by="act"))
            if name == "dk":
                later.append(dict(kind="f", name="su", g=ch, by="dve"))
    units += [dict(u, bank=4 + (na + n) % 4) for n, u in enumerate(later)]
    return by_engine(units)


def splits_here(u):
    return u["kind"] == "w" or (u["kind"] == "part" and u["ch"] < 3) or (u["kind"] == "tile" and u["last"])


def attention_blocks(l):
    return [(kind, s, qt, h) for kind in ("diff", "na") for s in range(streams(l)) for qt in range(2)
            for h in range(4)]


def attention_slots(l):
    return len(attention_blocks(l)) + 6


def tr_units(l):
    blocks = attention_blocks(l)
    nb = len(blocks)
    units = []
    for i in range(attention_slots(l)):
        if i >= 7 and (i - 7) % 4 == 0 and (i - 7) // 4 < nb // 4:
            units.append(dict(kind="o", g=(i - 7) // 4, by="act", slot=i))
        if 0 <= i - 1 < nb:
            units.append(dict(kind="p", b=i - 1, a=0, by="act", slot=i))
            if blocks[i - 1][0] == "na":
                units.append(dict(kind="p", b=i - 1, a=1, by="dve", slot=i))
    for t, u in enumerate(units):
        u["t"] = t
    return by_engine(units)


def mod_steps(l):
    first = [(l, q) for q in range(3 * PQ, 5 * PQ)] + ([(l + 1, q) for q in range(2 * PQ)] if l + 1 < L else [])
    second = [(l, q) for q in range(2 * PQ, 3 * PQ)] + [(l, q) for q in range(5 * PQ, 6 * PQ)]
    return first, second


def merge_steps(l):
    first, second = mod_steps(l)
    half, slots = NBR * KD // 2, attention_slots(l)
    steps = []
    for n in range(2 * half):
        u = dict(n=n, p=n // KD, v=n % KD, att=[], mod=[])
        if n < half:
            u["att"] = list(range(n * slots // half, (n + 1) * slots // half))
        todo, start, at_ = (first, 0, n) if n < half else (second, len(first), n - half)
        u["mod"] = [(start + t // 2, t % 2)
                    for t in range(at_ * 2 * len(todo) // half, (at_ + 1) * 2 * len(todo) // half)]
        steps.append(u)
    return steps


def unit_events(u):
    mods = [("mod", m) for m in u["mod"]]
    events = [("gates", 0)] + mods[:-1] + [("gates", 1)] + mods[-1:] + [("proj", None)]
    n, k, order = len(u["att"]), len(events), []
    for i, e in enumerate(events):
        order.append(e)
        order += [("att", u["att"][j]) for j in range(n) if (j + 1) * k // n - 1 == i]
    return order


def build(nc, A, out):
    f32, f32r = mybir.dt.float32, mybir.dt.float32r
    ACT = mybir.ActivationFunctionType
    ALU = mybir.AluOpType
    AX = mybir.AxisListType
    ds = bass.ds

    ctx = ExitStack()
    with ctx:
        def sb(name, shape, dt=f32, where=ctx):
            return where.enter_context(nc.sbuf_tensor(name, shape, dt))

        def signal(name, *per_layer):
            return Signal(ctx.enter_context(nc.semaphore(name)), list(per_layer))

        def counter(name):
            return ctx.enter_context(nc.semaphore(name))

        ring = sb("ring", [128, NSLOT, 1024])
        x = sb("x", [128, 4, D])
        with ExitStack() as rounded:
            arena_r = sb("arena_r", [128, 8, 2048], f32r, rounded)
            nab_r = sb("nab_r", [128, 8 * 6 * GRID_W], f32r, rounded)
        arena = sb("arena", [128, 8, 2048])
        nab_all = sb("nab", [128, 8 * 6 * GRID_W])
        cst = sb("cst", [128, C_ALL])
        par = sb("par", [128, P_ALL])
        stay = sb("stay", [128, S_ALL])
        bm = sb("bm", [6 * PQ, L, MQ])
        work = sb("work", [128, 9, 512])
        small = sb("small", [128, 256])
        cond = sb("cond", [128, KD, 32])
        modp = sb("modp", [128, 2, MQ])
        modA = sb("modA", [128, 2, 2, KD])
        modB = sb("modB", [128, 2, 2, KD])
        rwr = sb("rwr", [128, 2, RW_COLS], f32r)
        selp = sb("selp", [128, 256])
        rex = sb("rex", [128, 4, E])
        aff = sb("aff", [128, 2, 2, E])
        msk = sb("msk", [128, 2, 2 * E])
        place = sb("place", [128, 2, 2, E])
        with ExitStack() as mixers:
            wr = sb("wr", [128, 2, 2, 1024], f32r, mixers)
            hTr = sb("hTr", [128, 2, KD, 2 * T], f32r, mixers)
        with ExitStack() as moe:
            e_wr = sb("e_wr", [128, 2, 2048], f32, moe)
            e_h = sb("e_h", [128, 4, 2048], f32, moe)
        PS = ctx.enter_context(nc.psum_tensor("PS", [128, 8, 512], f32))

        def unit_of(i, n=1):
            return arena[:, i:i + n, :].rearrange("p a b -> p (a b)")

        region = {nm: unit_of(i).rearrange("p (a b) -> p a b", a=4)
                  for nm, i in (("pz", 0), ("dq", 1), ("su", 2), ("nq", 3), ("sv", 3), ("dk", 4), ("nk", 5),
                                ("dv", 6), ("nv", 7))}
        branches = unit_of(0, 4).rearrange("p (i k t) -> p i k t", i=NBR, k=4)
        nab = nab_all[:, :].rearrange("p (h n) -> p h n", h=8)
        split_hi = {1: 4, 3: 5}
        br_hi_of = {i: arena_r[:, u, :].rearrange("p (k t) -> p k t", k=4) for i, u in split_hi.items()}
        br_lo_of = {i: arena_r[:, i, :].rearrange("p (k t) -> p k t", k=4) for i in split_hi}
        wbr = nab_r[:, 0:2048].rearrange("p (a b c) -> p a b c", a=2, b=2)
        x_flat = x[:, :, :].rearrange("p a b -> p (a b)")
        mT = [x_flat[:, :].rearrange("p (k t) -> p k t", k=KD), x_flat[:, 2 * D:].rearrange("p (k t) -> p k t", k=KD)]
        g1b = unit_of(6).rearrange("p (a b) -> p a b", a=2)
        htmp = unit_of(6).rearrange("p (a b) -> p a b", a=4)
        g2r = unit_of(7)[:, 0:D]
        xn = work[:, 0:8, :].rearrange("p (m a) b -> p m (a b)", m=4)
        sq_junk = nab_all[:, 2048:3072]
        espace = [arena[:, 0, :], arena[:, 1, :], arena[:, 2, :], arena[:, 3, :], nab_all[:, 0:2048],
                  arena[:, 4, :], arena[:, 5, :], e_wr[:, 0, :], e_wr[:, 1, :], e_h[:, 0, :], e_h[:, 1, :], e_h[:, 2, :]]
        xspace = [ring[:, 2 * e:2 * e + 2, :].rearrange("p a b -> p (a b)") for e in range(EXTRA)]
        xsT = unit_of(6)[:, 0:1024].rearrange("p (a b) -> p a b", a=KD)
        hid = unit_of(6)[:, 1024:2048]
        toks = hid
        sil = unit_of(7)[:, 1024:2048]
        hidT = e_h[:, 3, 0:1024].rearrange("p (a b) -> p a b", a=KD)
        ysb = e_h[:, 3, 1024:2048]
        combT = nab_all[:, 2048:2560].rearrange("p (a b) -> p a b", a=4)
        selg = nab_all[:, 2560:3072].rearrange("p (a b) -> p a b", a=4)
        afT = unit_of(6)[0:32, 0:256]
        afR = unit_of(6)[0:32, 256:768].rearrange("p (a b) -> p a b", a=2)
        top = unit_of(6)[0:32, 768:800]
        fin_out = unit_of(0, 1)
        fin_gain = unit_of(1)[:, 0:D]

        ident = cst[:, C_ID:C_ID + 128]
        cosT, sinT = cst[:, C_COS:C_COS + T], cst[:, C_SIN:C_SIN + T]
        iota1 = cst[:, C_IOTA:C_IOTA + CAP]

        ss, ms, rstd = small[:, 0:4], small[:, 4:8], small[:, 8:12]
        half = small[:, 12:16]
        nmx = small[:, 16:20].rearrange("p (a b) -> p a b", a=2)
        rs = small[:, 20:24].rearrange("p (a b) -> p a b", a=2)
        rr = small[:, 24:32].rearrange("p (a b) -> p a b", a=4)
        lam = small[:, 32:40]
        subg = small[:, 40:41]
        oss, oms, orstd = small[:, 44:48], small[:, 48:52], small[:, 52:56]
        vst = small[:, 56:80].rearrange("p (a b) -> p a b", a=4)
        vmv = small[:, 80:88].rearrange("p (a b) -> p a b", a=4)
        vms, vrstd = small[:, 88:92], small[:, 92:96]
        nar = small[:, 96:128].rearrange("p (a b) -> p a b", a=4)
        rmx, rsum, rinv = small[:, 128:132], small[:, 132:136], small[:, 136:140]

        p_t = work[:, 0:4, :].rearrange("p (a b) c -> p a b c", a=2)
        at = work[:, 4:6, :]
        on = work[:, 6, :]
        sgt = work[:, 7:9, :]
        mix_tmp = lambda c: unit_of(7)[:, 1024 + 512 * (c % 2):1536 + 512 * (c % 2)]

        NT = [2 * streams(l) for l in range(L)]
        norms = [(0, 0, 2), (0, 1, streams(0)), (1, 0, 2), (1, 1, streams(1)), (2, 0, 1)]
        loaded = [counter(f"slot_loaded{i}") for i in range(NSLOT)]
        e_loaded = [counter(f"expert_loaded{i}") for i in range(ESLOT)]
        e_freed = [counter(f"expert_freed{i}") for i in range(ESLOT)]
        extra_loaded = [counter(f"extra_loaded{i}") for i in range(EXTRA)]
        extra_used = counter("extra_used")
        consts_loaded = counter("consts_loaded")
        x_loaded = counter("x_loaded")
        par_loaded = counter("par_loaded")
        bias_loaded = counter("bias_loaded")
        bias_masked = signal("bias_masked", 1, 1)
        half_ready = counter("half_ready")
        cond_ready = counter("cond_ready")
        MOD0 = 2 * PQ
        MODS = [len(mod_steps(l)[0]) + len(mod_steps(l)[1]) for l in range(L)]
        MS = [MOD0 + MODS[0], MODS[1]]
        mod_half = signal("mod_half", *MS)
        mod_sum = signal("mod_sum", *MS)
        mod_part = signal("mod_part", *MS)
        mod_cols = signal("mod_cols", 3, 1)
        mod_ready = signal("mod_ready", 3, 1)
        MODULATED = [(0, 1), (0, 2), (0, 3), (1, 1)]
        NGB = [PQ * streams(l) + PQ for l in range(L)]
        gate_bc = signal("gate_bc", *NGB)
        gate_rows = signal("gate_rows", *NGB)
        NN = [2 * n for _, _, n in norms]
        sq_done = signal("sq_done", *NN)
        rstd_done = signal("rstd_done", *[n for _, _, n in norms])
        xn_ready = signal("xn_ready", *NN)
        xt_ready = signal("xt_ready", *[4 * n for _, _, n in norms[:4]])
        tmp_act = signal("tmp_act", *[2 * n for _, _, n in norms[:4]])
        tmp_dve = signal("tmp_dve", *[2 * n for _, _, n in norms[:4]])
        h_hi = signal("h_hi", *[4 * n for _, _, n in norms[:4]])
        h_lo = signal("h_lo", *[4 * n for _, _, n in norms[:4]])
        w_hi = signal("w_hi", NC_ALL, NC_ALL)
        w_lo = signal("w_lo", NC_ALL, NC_ALL)
        chunk_sum = signal("chunk_sum", NC_ALL, NC_ALL)
        rw_hi = signal("rw_hi", 1, 1)
        rw_lo = signal("rw_lo", 1, 1)
        WU = [w_units(l) for l in range(L)]
        aux_sum = signal("aux_sum", *[sum(u["kind"] in AUX for u in us) for us, _ in WU])
        tile_sum = signal("tile_sum", *[max(u.get("sums", 0) for u in us) for us, _ in WU])
        w_act = signal("w_act", *[n["act"] for _, n in WU])
        w_dve = signal("w_dve", *[n["dve"] for _, n in WU])
        dve_step = counter("dve_step")
        pool_step = counter("pool_step")
        lam_prod = signal("lam_prod", 1, 1)
        lam_exp = signal("lam_exp", 1, 1)
        lam_ready = signal("lam_ready", 1, 1)
        pooled = signal("pooled", 4, 4)
        v_stats = signal("v_stats", 1, 1)
        v_rstd = signal("v_rstd", 1, 1)
        v_norm = signal("v_norm", *NT)
        BL = [attention_blocks(l) for l in range(L)]
        NB = [len(b) for b in BL]
        TU = [tr_units(l) for l in range(L)]
        scores = signal("scores", *NB)
        maxes = signal("maxes", *NB)
        exps = signal("exps", *NB)
        probs = signal("probs", *NB)
        tr_made = signal("tr_made", *[len(u) for u, _ in TU])
        at_act = signal("at_act", *[n["act"] for _, n in TU])
        at_dve = signal("at_dve", *[n["dve"] for _, n in TU])
        pv = signal("pv", *NB)
        NG = [n // 4 for n in NB]
        o_square = signal("o_square", *[n // 2 for n in NG])
        o_ss = signal("o_ss", *[n // 2 for n in NG])
        o_rstd = signal("o_rstd", *[n // 2 for n in NG])
        o_norm = signal("o_norm", *NG)
        NM = NBR * KD
        projs = signal("projs", NM, NM)
        sigs = signal("sigs", NM, NM)
        gated = signal("gated", NM, NM)
        merged = signal("merged", NM, NM)
        HALF = NM // 2
        branch_hi = signal("branch_hi", 8, 8)
        branch_lo = signal("branch_lo", 8, 8)
        wbr_hi = signal("wbr_hi", NM - HALF, NM - HALF)
        wbr_lo = signal("wbr_lo", NM - HALF, NM - HALF)
        m_hi = signal("m_hi", KD, KD)
        m_lo = signal("m_lo", KD, KD)
        x_back = counter("x_back")
        mix_sum = signal("mix_sum", *[2 * n for n in NT])
        mix_gated = signal("mix_gated", *[2 * n for n in NT])
        mix_x = signal("mix_x", *[2 * n for n in NT])
        logitsT = signal("logitsT", 1, 1)
        logits_copied = signal("logits_copied", 1, 1)
        logits = signal("logits", 1, 1)
        r_max = signal("r_max", 1, 1)
        r_exp = signal("r_exp", *NT)
        aff_ready = signal("aff_ready", 1, 1)
        affT_made = signal("affT_made", 1, 1)
        mask_ready = signal("mask_ready", 1, 1)
        maskT_made = signal("maskT_made", 1, 1)
        maskT_ready = signal("maskT_ready", 1, 1)
        count_made = signal("count_made", 1, 1)
        place_ready = signal("place_ready", 1, 1)
        GE = [128 // (CAP * streams(l)) for l in range(L)]
        NP = [E // g for g in GE]

        def packs(name, n0, n1):
            return signal(name, n0 * NP[0], n1 * NP[1])

        sel_ready = packs("sel_ready", 2, 1)
        selg_ready = packs("selg_ready", 2, 1)
        gathered = packs("gathered", 2, 2)
        tok_act = packs("tok_act", 1, 1)
        tok_dve = packs("tok_dve", 1, 1)
        xs_made = packs("xs_made", 2, 2)
        xs_mul = packs("xs_mul", 4, 2)
        xs_ready = packs("xs_ready", 4, 2)
        combT_made = packs("combT_made", 1, 1)
        combT_ready = packs("combT_ready", 1, 1)
        h1_sum = packs("h1_sum", 1, 1)
        h3_sum = packs("h3_sum", 1, 1)
        sil_ready = packs("sil_ready", 2, 2)
        hid_ready = packs("hid_ready", 2, 2)
        hidT_made = packs("hidT_made", 2, 2)
        hidT_act = packs("hidT_act", 1, 1)
        hidT_dve = packs("hidT_dve", 1, 1)
        y_sum = packs("y_sum", 1, 1)
        y_ready = packs("y_ready", 2, 2)
        comb_sum = packs("comb_sum", 2 * NT[0], 2 * NT[1])
        comb_x = packs("comb_x", 2 * NT[0], 2 * NT[1])
        fin_ready = counter("fin_ready")
        out_stored = counter("out_stored")

        e_uses = [len(range(s, 12 * E - EXTRA, ESLOT)) for s in range(ESLOT)]

        def e_place(n, first):
            if first and ESLOT <= n < ESLOT + EXTRA:
                return n - ESLOT, None, None
            if not first or n >= ESLOT:
                n -= EXTRA
            return None, n % ESLOT, n // ESLOT

        MERGE = [merge_steps(l) for l in range(L)]
        items, item_at = [], {}

        def item(kind, l, idx, release):
            item_at[kind, l, idx] = (len(items) % NSLOT, len(items) // NSLOT)
            items.append((kind, l, idx, release))

        def branch_items(n):
            if n < HALF - 1:
                return [n]
            return [n, n + 1] if n == HALF - 1 else [m for m in (n + 1,) if m < NM]

        def mod_item(l, n, half_):
            item("mod", l, 2 * n + half_, (mod_sum if half_ else mod_half).at(l, n + 1))

        for n in range(MOD0):
            mod_item(0, n, 0)
            mod_item(0, n, 1)
        for l in range(L):
            for q in range(NW + 2):
                item("chunk", l, q, w_lo.at(l, q + 1))
            done = MOD0 if l == 0 else 0
            for u in MERGE[l]:
                for m_, half_ in u["mod"][:-1]:
                    mod_item(l, done + m_, half_)
                item("chunk", l, NW + u["n"] + 2, w_lo.at(l, NW + u["n"] + 3))
                for m_, half_ in u["mod"][-1:]:
                    mod_item(l, done + m_, half_)
                for n in branch_items(u["n"]):
                    item("br", l, n, projs.at(l, n + 1) if n < HALF else wbr_lo.at(l, n - HALF + 1))
            for k in range(2, KD):
                item("chunk", l, NW + NM + k, w_lo.at(l, NW + NM + k + 1))

        def mod_of(l, n):
            if l == 0:
                if n < MOD0:
                    return 0, n
                n -= MOD0
            first, second = mod_steps(l)
            return (first + second)[n]

        block = ctx.enter_context(nc.Block())

        def tr_banks(nn, n_streams):
            if nn == 0:
                return [(s, kp) for s in range(2) for kp in range(4)]
            return [(s, kp) for kp in range(4) for s in range(n_streams)]

        def mod_pairs(nn, n_streams):
            order = tr_banks(nn, n_streams)
            return [(s, kp, order.index((s, kp))) for kp in range(4) for s in range(n_streams)]

        def mod_bank(l, n):
            return 5 + n % 2 if l == 0 and n < MOD0 else 7

        def own(u, a, d):
            return a if u["by"] == "act" else d

        def last_of(units, name, kind):
            n = {"act": 0, "dve": 0}
            for u in units:
                if u["kind"] == kind and u["name"] == name:
                    n[u["by"]] = u["nth"]
            return n

        @block.sync
        def _(sync):
            w_mod_v = A["w_mod"].rearrange("l (k p) n -> l p k n", p=128)
            w_in_v = A["w_in"].rearrange("l (k p) n -> l p k n", p=128)
            w_br_v = A["w_br"].rearrange("l i (k p) n -> l i p k n", p=128)
            w_out_v = A["w_out"].rearrange("l (k p) n -> l k p n", p=128)
            experts = [A[n].rearrange("l e (k p) n -> l (e k) p n", p=128) for n in ("moe_w1", "moe_w3", "moe_w2")]

            def load_items(lo, hi):
                for n in range(lo, hi):
                    kind, l, idx, _ = items[n]
                    if n >= NSLOT:
                        sync.wait_ge(*items[n - NSLOT][3])
                    dst = ring[:, n % NSLOT, :]
                    if kind == "mod":
                        ml, q = mod_of(l, idx // 2)
                        k0 = idx % 2 * (KD // 2)
                        src = w_mod_v[ml, :, k0:k0 + KD // 2, q * MQ:(q + 1) * MQ]
                        dst = dst.rearrange("p (k n) -> p k n", k=KD // 2)
                    elif kind == "br":
                        p, v = idx // KD, idx % KD
                        src = w_br_v[l, MERGE_ORDER[p], :, :, v * 128:(v + 1) * 128]
                        dst = dst[:, 0:512].rearrange("p (k n) -> p k n", k=4)
                    elif idx < NW:
                        _, form, c = GROUPS[idx // 4]
                        ch = idx % 4
                        if form == "f":
                            src = w_in_v[l, :, :, c + ch * 128:c + (ch + 1) * 128]
                            dst = dst.rearrange("p (k n) -> p k n", k=KD)
                        else:
                            src = w_in_v[l, :, 2 * ch:2 * ch + 2, c:c + 512]
                            dst = dst.rearrange("p (k n) -> p k n", k=2)
                    elif idx < NW + NM:
                        n_ = idx - NW
                        c = GATE_COL + MERGE_ORDER[n_ // KD] * D + (n_ % KD) * 128
                        src = w_in_v[l, :, :, c:c + 128]
                        dst = dst.rearrange("p (k n) -> p k n", k=KD)
                    else:
                        src = w_out_v[l, idx - NW - NM]
                    sync.dma_start(dst, src).then_inc(loaded[n % NSLOT], 16)

            sync.dma_start(stay[:, :], A["stay"]).then_inc(consts_loaded, 16)
            sync.dma_start(cst[:, :], A["cst"]).then_inc(consts_loaded, 16)
            sync.dma_start(bm[:, :, :], A["b_mod"].rearrange("l (a b) -> a l b", b=MQ)).then_inc(consts_loaded, 16)
            load_items(0, 4)
            sync.dma_start(x[:, 0:2, :], A["x"].rearrange("o (m p) d -> p (o m) d", p=128)).then_inc(x_loaded, 16)
            sync.dma_start(x[:, 2:4, :], A["ctx"].rearrange("o (m p) d -> p (o m) d", p=128)).then_inc(x_loaded, 16)
            at_item = 4
            for l in range(L):
                end = max(n for n, it in enumerate(items) if it[1] == l) + 1
                load_items(at_item, end)
                at_item = end
                G = GE[l]

                def load_pack(i, first):
                    n = 0
                    for w in experts:
                        for j in range(4):
                            for g in range(G):
                                src = w[l, ds(i * (G * KD) + (g * KD + 2 * j), 2), :, :].rearrange("k p n -> p k n")
                                extra, s, turn = e_place(n, first)
                                if extra is not None:
                                    if extra == 0:
                                        for m in range(end - NSLOT, end):
                                            sync.wait_ge(*items[m][3])
                                    sync.dma_start(xspace[extra].rearrange("p (k n) -> p k n", k=2), src)\
                                        .then_inc(extra_loaded[extra], 16)
                                else:
                                    sync.wait_ge(e_freed[s], i * G + (l * (e_uses[s] + 1) + 1 + turn))
                                    sync.dma_start(espace[s].rearrange("p (k n) -> p k n", k=2), src)\
                                        .then_inc(e_loaded[s], 16)
                                n += 1

                load_pack(0, True)
                with sync.Fori(1, NP[l]) as i:
                    load_pack(i, False)
                sync.wait_ge(extra_used, EXTRA * (l + 1))
            sync.wait_ge(e_freed[1], L * (e_uses[1] + 1))
            sync.dma_start(fin_gain, A["final_g"]).then_inc(consts_loaded, 16)
            out_v = out.rearrange("o (m p) d -> p (o m) d", p=128)
            for m in range(2):
                sync.wait_ge(fin_ready, m + 1)
                sync.dma_start(out_v[:, m, :], fin_out[:, m * D:(m + 1) * D]).then_inc(out_stored, 16)
            sync.wait_ge(out_stored, 32)

        @block.tensor
        def _(pe):
            def mm(o, a, b, first, last):
                return nc.tensor.matmul(o, a, b, start=first, stop=last)

            def take(key):
                slot, use = item_at[key]
                pe.wait_ge(loaded[slot], 16 * (use + 1))
                return ring[:, slot, :]

            def three(o, wh, wl, ah, al, first, last, weights_move):
                if weights_move:
                    mm(o, ah, wh, first, False)
                    mm(o, ah, wl, False, False)
                    return mm(o, al, wh, False, last)
                mm(o, wh, ah, first, False)
                mm(o, wh, al, False, False)
                return mm(o, wl, ah, False, last)

            bc = [0, 0]

            def mod_post(l, n):
                ml, q = mod_of(l, n)
                part, ch = q // PQ, q % PQ
                pe.wait_ge(*mod_part.at(l, n + 1))
                if part % 3 == 2:
                    for s in range(streams(ml) if part == 2 else 1):
                        if bc[l] >= 2:
                            pe.wait_ge(*gate_rows.at(l, bc[l] - 1))
                        if part == 5 and streams(ml) == 2:
                            pick = cst[:, C_SELY:C_SELY + 128]
                        else:
                            pick = cst[:, C_SELR + 128 * s:C_SELR + 128 * s + 128]
                        mm(PS[:, bc[l] % 2, 0:MQ], pick, modp[:, n % 2, :], True, True).then_inc(gate_bc.sem, 1)
                        bc[l] += 1
                else:
                    for c in range(MQ // 128):
                        col = 256 + 32 * (part // 3) + 2 * ((part % 3) * KD + ch * (MQ // 128) + c)
                        i = mm(PS[:, 7, col:col + 2], modp[:, n % 2, c * 128:(c + 1) * 128],
                               cst[:, C_SELC:C_SELC + 2], True, True)
                    if part % 3 == 1 and ch == PQ - 1:
                        i.then_inc(mod_cols.sem, 1)

            def mod_chunk(l, n, half_):
                ml, q = mod_of(l, n)
                w = take(("mod", l, 2 * n + half_))
                start = l == 0 and n < MOD0
                if half_ == 0:
                    if start and n >= 2:
                        pe.wait_ge(*mod_part.at(l, n - 1))
                    elif n and not start:
                        pe.wait_ge(*mod_part.at(l, n))
                    if l == 0 and n == MOD0:
                        pe.wait_ge(*mod_ready.at(0, 1))
                    if n == (MOD0 if l == 0 else 0) + len(mod_steps(l)[0]):
                        pe.wait_ge(*mod_ready.at(l, 3 if l == 0 else 1))
                o = PS[:, mod_bank(l, n), 0:MQ]
                for j in range(4):
                    i = nc.tensor.matmul(o[32 * j:32 * j + 32, :], cond[:, 4 * half_ + j, :], w[:, j * MQ:(j + 1) * MQ],
                                         start=(half_ == 0), stop=(half_ == 1 and j > 0), tile_position=(0, 32 * j),
                                         skip_group_check=True)
                if half_ == 0:
                    i.then_inc(mod_half.sem, 1)
                    return
                nc.tensor.matmul(o[0:2, :], cst[0:6 * PQ, C_ID + q:C_ID + q + 1].broadcast_to([6 * PQ, 2]), bm[:, ml, :],
                                 start=False, stop=True, tile_position=(0, 0), skip_group_check=True)\
                    .then_inc(mod_sum.sem, 1)

            def transposes(nn, banks):
                for s, kp in banks:
                    pe.wait_ge(*xn_ready.at(nn, 2 * s + 2))
                    for kk in range(2):
                        for j in range(2):
                            i = nc.tensor.transpose(PS[:, 4 * s + kp, kk * T + j * 128:kk * T + (j + 1) * 128],
                                                    xn[:, 2 * s + j, (2 * kp + kk) * 128:(2 * kp + kk + 1) * 128],
                                                    ident)
                    i.then_inc(xt_ready.sem, 1)

            pe.wait_ge(consts_loaded, 48)
            pe.wait_ge(cond_ready, 2)
            for n in range(MOD0):
                mod_chunk(0, n, 0)
                mod_chunk(0, n, 1)
                if n:
                    mod_post(0, n - 1)
                if n == MOD0 - 2:
                    transposes(0, tr_banks(0, 2)[0:4])
            mod_post(0, MOD0 - 1)
            pe.wait_ge(*mod_ready.at(0, 1))

            for l in range(L):
                NS = streams(l)
                tok = NS * T
                transposes(2 * l, tr_banks(2 * l, 2)[4 if l == 0 else 0:])
                units, counts = WU[l]
                held = {}

                def free(bank):
                    if bank in held:
                        o = held[bank]
                        pe.wait_ge(*own(o, w_act, w_dve).at(l, o["nth"]))

                for u in units:
                    if u["kind"] == "tile":
                        held[u["bank"]] = u
                        continue
                    if u["kind"] == "part":
                        q = u["q"]
                        pe.wait_ge(*w_lo.at(l, q + 1))
                        for m, bank in enumerate(u["banks"]):
                            if u["ch"] == 0:
                                free(bank)
                            for kk in range(2):
                                k = 2 * u["ch"] + kk
                                i = three(PS[:, bank, :], wr[:, q % 2, 0, kk * 512:(kk + 1) * 512],
                                          wr[:, q % 2, 1, kk * 512:(kk + 1) * 512], hTr[:, 0, k, m * 128:(m + 1) * 128],
                                          hTr[:, 1, k, m * 128:(m + 1) * 128], k == 0, k == KD - 1, True)
                            if m == len(u["banks"]) - 1:
                                i.then_inc(chunk_sum.sem, 1)
                            elif u["ch"] == 3:
                                i.then_inc(tile_sum.sem, 1)
                        continue
                    free(u["bank"])
                    held[u["bank"]] = u
                    bank = PS[:, u["bank"], :]
                    if u["kind"] == "w":
                        q = u["q"]
                        pe.wait_ge(*w_lo.at(l, q + 1))
                        for k in range(KD):
                            if q == 0 and k % 2 == 0:
                                pe.wait_ge(*h_lo.at(2 * l, k + 2))
                            i = three(bank[:, 0:u["tokens"]], wr[:, q % 2, 0, k * 128:(k + 1) * 128],
                                      wr[:, q % 2, 1, k * 128:(k + 1) * 128], hTr[:, 0, k, 0:u["tokens"]],
                                      hTr[:, 1, k, 0:u["tokens"]], k == 0, k == KD - 1, False)
                        i.then_inc(chunk_sum.sem, 1)
                    elif u["kind"] == "rope":
                        for v in units:
                            if v["kind"] == "w" and v["name"] == u["name"] and v["ch"] // 2 == u["pair"]:
                                pe.wait_ge(*own(v, w_act, w_dve).at(l, v["nth"]))
                        for c in range(2):
                            i = mm(bank[:, c * T:(c + 1) * T], cst[:, C_PERM:C_PERM + 128],
                                   region[u["name"]][:, 2 * u["pair"] + c, 0:T], True, True)
                        i.then_inc(aux_sum.sem, 1)
                    elif u["kind"] == "pool":
                        g = u["g"]
                        pe.wait_ge(*pooled.at(l, g + 1))
                        mm(bank[:, 0:tok], par[:, P_POOLW + g * 128:P_POOLW + (g + 1) * 128],
                           region["pz"][:, g, 0:tok], True, True).then_inc(aux_sum.sem, 1)
                    else:
                        g = u["g"]
                        pe.wait_ge(par_loaded, 16 * (l + 1))
                        pe.wait_ge(*v_norm.at(l, 2 * NS))
                        for m in range(2 * NS):
                            i = mm(bank[:, m * 128:(m + 1) * 128], region["sv"][:, m, g * 128:(g + 1) * 128],
                                   par[:, P_SGUW + g * 128:P_SGUW + (g + 1) * 128], True, True)
                        i.then_inc(aux_sum.sem, 1)
                for bank in range(4, 8):
                    free(bank)
                blocks, nb = BL[l], NB[l]
                tr, tr_n = TU[l]

                def score(b):
                    kind, s, qt, h = blocks[b]
                    q, k = (region["dq"], region["dk"]) if kind == "diff" else (region["nq"], region["nk"])
                    k0, nk = (0, 2 * T) if s == 0 else (T, T)
                    if b >= 1:
                        pe.wait_ge(*exps.at(l, b))
                    local = kind == "na" and s == 0
                    for a in range(2):
                        i = mm(PS[:, a, 0:nk], q[64 * a:64 * a + 64, h, s * T + qt * 128:s * T + (qt + 1) * 128],
                               k[64 * a:64 * a + 64, h, k0:k0 + nk], True, not local)
                    if local:
                        pe.wait_ge(*bias_masked.at(l, 1))
                        for a in range(2):
                            i = mm(PS[:, a, 0:T], cst[:, C_FLIP:C_FLIP + 128],
                                   nab[:, 2 * h + a, (2 - 2 * qt) * 64:(2 - 2 * qt) * 64 + T], False, True)
                    i.then_inc(scores.sem, 1)

                def emptied(t):
                    if t >= 2:
                        o = tr[t - 2]
                        pe.wait_ge(*own(o, at_act, at_dve).at(l, o["nth"]))

                def turn(u):
                    b = u["b"]
                    nkt = 4 if blocks[b][1] == 0 else 2
                    pe.wait_ge(*probs.at(l, b + 1))
                    emptied(u["t"])
                    for kt in range(nkt):
                        i = nc.tensor.transpose(PS[:, 2 + u["t"] % 2, kt * 128:(kt + 1) * 128],
                                                p_t[:, b % 2, u["a"], kt * 128:(kt + 1) * 128], ident)
                    i.then_inc(tr_made.sem, 1)

                def values(b):
                    kind, s, qt, h = blocks[b]
                    nkt, m0 = (4, 0) if s == 0 else (2, 2)
                    g = b // 4
                    if b % 4 == 0 and g >= 1:
                        pe.wait_ge(*o_norm.at(l, g))
                    mine = [u for u in tr if u["kind"] == "p" and u["b"] == b]
                    for u in mine:
                        pe.wait_ge(*own(u, at_act, at_dve).at(l, u["nth"]))
                    for u in mine:
                        w = 128 // len(mine)
                        c = h * 128 + u["a"] * w
                        v = region["dv"] if kind == "diff" else region["nv"]
                        for kt in range(nkt):
                            i = mm(PS[:, 4, c:c + w], at[:, u["t"] % 2, kt * 128:(kt + 1) * 128],
                                   v[:, m0 + kt, c:c + w], kt == 0, kt == nkt - 1)
                    i.then_inc(pv.sem, 1)

                def turn_out(u):
                    pe.wait_ge(*o_norm.at(l, u["g"] + 1))
                    emptied(u["t"])
                    for c in range(4):
                        i = nc.tensor.transpose(PS[:, 2 + u["t"] % 2, c * 128:(c + 1) * 128],
                                                on[:, c * 128:(c + 1) * 128], ident)
                    i.then_inc(tr_made.sem, 1)

                def attention(slot):
                    if slot == 0:
                        pe.wait_ge(*w_act.at(l, counts["act"]))
                        pe.wait_ge(*w_dve.at(l, counts["dve"]))
                    for u in tr:
                        if u["slot"] == slot and u["kind"] == "o":
                            turn_out(u)
                    if slot < nb:
                        score(slot)
                    if 0 <= slot - 2 < nb:
                        values(slot - 2)
                    for u in tr:
                        if u["slot"] == slot and u["kind"] == "p":
                            turn(u)

                done = MOD0 if l == 0 else 0
                for u in MERGE[l]:
                    n, j, v = u["n"], NW + u["n"], u["v"]
                    for what, arg in unit_events(u):
                        if what == "gates":
                            if arg == 0:
                                pe.wait_ge(*w_lo.at(l, j + 1))
                                if n:
                                    pe.wait_ge(*sigs.at(l, n))
                            for k in range(arg * KD // 2, (arg + 1) * KD // 2):
                                i = three(PS[:, 5, 0:tok], wr[:, j % 2, 0, k * 128:(k + 1) * 128],
                                          wr[:, j % 2, 1, k * 128:(k + 1) * 128], hTr[:, 0, k, 0:tok],
                                          hTr[:, 1, k, 0:tok], k == 0, k == KD - 1, False)
                            if arg == 1:
                                i.then_inc(chunk_sum.sem, 1)
                        elif what == "proj":
                            if n:
                                pe.wait_ge(*gated.at(l, n))
                            b = MERGE_ORDER[u["p"]]
                            if n < HALF:
                                br = take(("br", l, n))
                            else:
                                pe.wait_ge(*wbr_lo.at(l, n - HALF + 1))
                                pe.wait_ge(*branch_lo.at(l, 4 * (u["p"] - 1)))
                            for k in range(4):
                                c = slice(k * 128, (k + 1) * 128)
                                if n < HALF:
                                    i = mm(PS[:, 6, 0:tok], br[:, c], branches[:, b, k, 0:tok], k == 0, k == 3)
                                else:
                                    i = three(PS[:, 6, 0:tok], wbr[:, n % 2, 0, c], wbr[:, n % 2, 1, c],
                                              br_hi_of[b][:, k, 0:tok], br_lo_of[b][:, k, 0:tok], k == 0, k == 3, False)
                            i.then_inc(projs.sem, 1)
                        elif what == "att":
                            attention(arg)
                        else:
                            m_, half_ = arg
                            if half_ == 0 and m_:
                                mod_post(l, done + m_ - 1)
                            mod_chunk(l, done + m_, half_)
                mod_post(l, done + MODS[l] - 1)
                pe.wait_ge(*projs.at(l, NM))
                pe.wait_ge(*pv.at(l, nb))
                for s in range(7):
                    pe.sem_inc(e_freed[s], 1)
                for k in range(KD):
                    j = NW + NM + k
                    pe.wait_ge(*w_lo.at(l, j + 1))
                    pe.wait_ge(*m_lo.at(l, k + 1))
                    if k == 0:
                        pe.wait_ge(*gate_rows.at(l, NGB[l]))
                    for m in range(NT[l]):
                        for n in range(2):
                            if k == 0 and 2 * m + n == 6:
                                pe.wait_ge(*gated.at(l, NM))
                            i = three(PS[:, 2 * m + n, :], wr[:, j % 2, 0, n * 512:(n + 1) * 512],
                                      wr[:, j % 2, 1, n * 512:(n + 1) * 512], hTr[:, 0, k, m * 128:(m + 1) * 128],
                                      hTr[:, 1, k, m * 128:(m + 1) * 128], k == 0, k == KD - 1, True)
                            if k == KD - 1:
                                i.then_inc(mix_sum.sem, 1)
                            elif m == NT[l] - 1 and n == 1:
                                i.then_inc(chunk_sum.sem, 1)
                pe.wait_ge(*mix_sum.at(l, 2 * NT[l]))
                pe.sem_inc(chunk_sum.sem, 1)
                for s in (7, 8):
                    pe.sem_inc(e_freed[s], 1)
                pe.wait_ge(*mix_x.at(l, 2 * NT[l]))
                transposes(2 * l + 1, tr_banks(2 * l + 1, NS))
                pe.wait_ge(*rw_lo.at(l, 1))
                for k in range(KD):
                    if k % 2 == 0:
                        pe.wait_ge(*h_lo.at(2 * l + 1, NS * (k // 2 + 1)))
                    i = three(PS[:, 0, 0:tok], rwr[:, 0, k * E:k * E + 128], rwr[:, 1, k * E:k * E + 128],
                              hTr[:, 0, k, 0:tok], hTr[:, 1, k, 0:tok], k == 0, k == KD - 1, False)
                i.then_inc(logitsT.sem, 1)
                pe.wait_ge(*logitsT.at(l, 1))
                for s in (9, 10, 11):
                    pe.sem_inc(e_freed[s], 1)
                pe.wait_ge(*logits_copied.at(l, 1))
                for m in range(NT[l]):
                    i = nc.tensor.transpose(PS[:, 4, m * E:(m + 1) * E], work[0:E, 8, m * 128:(m + 1) * 128],
                                            cst[0:E, C_ID:C_ID + E])
                i.then_inc(logits.sem, 1)
                pe.wait_ge(*aff_ready.at(l, 1))
                for j in range(2):
                    i = nc.tensor.transpose(PS[0:NS * E, 1, j * 128:(j + 1) * 128],
                                            aff[:, j, 0:NS, :].rearrange("p a b -> p (a b)"), ident)
                i.then_inc(affT_made.sem, 1)
                pe.wait_ge(*mask_ready.at(l, 1))
                for j in range(2):
                    i = nc.tensor.transpose(PS[:, 2, j * 32:j * 32 + NS * E], afR[0:NS * E, 0, j * 128:(j + 1) * 128],
                                            cst[0:NS * E, C_ID:C_ID + NS * E])
                i.then_inc(maskT_made.sem, 1)
                pe.wait_ge(*maskT_ready.at(l, 1))
                mm(PS[:, 3, 0:NS * E], cst[:, C_TRI:C_TRI + 128], msk[:, 0, 0:NS * E], True, True)
                mm(PS[:, 3, 32:32 + NS * E], cst[:, C_ONE:C_ONE + 128], msk[:, 0, 0:NS * E], True, False)
                mm(PS[:, 3, 32:32 + NS * E], cst[:, C_TRI:C_TRI + 128], msk[:, 1, 0:NS * E], False, True)\
                    .then_inc(count_made.sem, 1)
                G, R = GE[l], CAP * NS
                def pack(i, first):
                    def when(sig, n, k):
                        sem, val = sig.at(l, k)
                        pe.wait_ge(sem, i * n + val)

                    when(sel_ready, NS, NS)
                    W = G * CAP
                    for h in range(2):
                        for j in range(2):
                            for s in range(NS):
                                m = 2 * s + j
                                ins = nc.tensor.matmul(PS[s * W:(s + 1) * W, 6 + h, :], selp[:, m * W:(m + 1) * W],
                                                       xn[:, m, h * 512:(h + 1) * 512], start=(j == 0), stop=(j == 1),
                                                       tile_position=(0, s * W))
                        ins.then_inc(gathered.sem, 1)
                    when(selg_ready, NS, NS)
                    for m in range(NT[l]):
                        ins = nc.tensor.transpose(PS[:, 4, m * 128:(m + 1) * 128], selg[:, m, :], ident)
                    ins.then_inc(combT_made.sem, 1)
                    for bk, copied in enumerate((tok_act, tok_dve)):
                        when(copied, 1, 1)
                        for k4 in range(4):
                            ins = nc.tensor.transpose(PS[:, 6 + bk, k4 * 128:(k4 + 1) * 128],
                                                      toks[:, (4 * bk + k4) * 128:(4 * bk + k4 + 1) * 128], ident)
                        ins.then_inc(xs_made.sem, 1)
                    when(xs_ready, 2 * NS, 2 * NS)
                    n = 0
                    for w, (bank, done_) in enumerate(((0, h1_sum), (2, h3_sum), (4, y_sum))):
                        src = xsT if w < 2 else hidT
                        if w == 2:
                            when(hid_ready, 2, 2)
                            for bk in range(2):
                                for k4 in range(4):
                                    k = 4 * bk + k4
                                    ins = nc.tensor.transpose(PS[:, 6 + bk, k4 * 128:(k4 + 1) * 128],
                                                              hid[:, k * 128:(k + 1) * 128], ident)
                                ins.then_inc(hidT_made.sem, 1)
                            when(combT_ready, 1, 1)
                            when(hidT_act, 1, 1)
                            when(hidT_dve, 1, 1)
                        for j in range(4):
                            for g in range(G):
                                extra, s, turn_ = e_place(n + g, first)
                                if extra is not None:
                                    pe.wait_ge(extra_loaded[extra], 16 * (l + 1))
                                else:
                                    pe.wait_ge(e_loaded[s], i * (16 * G) + 16 * (l * e_uses[s] + turn_ + 1))
                            for kk in range(2):
                                k = 2 * j + kk
                                for h in range(2):
                                    for g in range(G):
                                        extra, s, _ = e_place(n + g, first)
                                        space = espace[s] if extra is None else xspace[extra]
                                        ins = nc.tensor.matmul(
                                            PS[g * R:(g + 1) * R, bank + h, :], src[:, k, g * R:(g + 1) * R],
                                            space[:, kk * D + h * 512:kk * D + (h + 1) * 512],
                                            start=(k == 0), stop=(k == KD - 1), tile_position=(0, g * R))
                                        if kk == 1 and h == 1 and not (j == 3 and g == G - 1):
                                            ins.then_inc(e_freed[s] if extra is None else extra_used, 1)
                            n += G
                        ins.then_inc(done_.sem, 1)
                        sem, val = done_.at(l, 1)
                        pe.wait_ge(sem, i * 1 + val)
                        pe.sem_inc(e_freed[e_place(n - 1, first)[1]], 1)
                    when(y_ready, 2, 2)
                    for c in range(2 * NT[l]):
                        m, h = c // 2, c % 2
                        if c >= 4:
                            when(comb_x, 2 * NT[l], c - 3)
                        mm(PS[:, c % 4, :], combT[:, m, :], ysb[:, h * 512:(h + 1) * 512], True, True)\
                            .then_inc(comb_sum.sem, 1)

                pack(0, True)
                with pe.Fori(1, NP[l]) as i:
                    pack(i, False)
                pe.wait_ge(*comb_x.at(l, 2 * NT[l] * NP[l]))

        @block.scalar
        def _(act):
            act.wait_ge(consts_loaded, 48)
            act.wait_ge(cond_ready, 1)
            nc.scalar.activation(cond[:, :, 0:2], stay[:, S_C:S_C + 16].rearrange("p (s k) -> p k s", s=2),
                                 ACT.Silu).then_inc(cond_ready, 1)

            def high(l, j):
                if j >= NC_ALL:
                    return
                slot, use = item_at["chunk", l, j]
                act.wait_ge(loaded[slot], 16 * (use + 1))
                if j >= 2:
                    act.wait_ge(*chunk_sum.at(l, j - 1))
                nc.scalar.activation(wr[:, j % 2, 0, :], ring[:, slot, :], ACT.Copy).then_inc(w_hi.sem, 1)

            def squares(nn, n_streams, written=None):
                for m in range(2 * n_streams):
                    if written is not None:
                        sig, layer, before = written
                        act.wait_ge(*sig.at(layer, before + 2 * m + 2))
                    nc.scalar.activation(sil if nn % 2 == 0 else sq_junk, x[:, m, :], ACT.Square, accum_out=ss[:, m:m + 1])\
                        .then_inc(sq_done.sem, 1)
                    act.wait_ge(*sq_done.at(nn, m + 1))

            def modulate(nn, norm, n_streams):
                act.wait_ge(*mod_ready.at(*MODULATED[nn]))
                pairs = mod_pairs(nn, n_streams)

                def part_high(t):
                    if t % 2:
                        act.wait_ge(*tmp_dve.at(nn, t // 2 + 1))
                    else:
                        act.wait_ge(*tmp_act.at(nn, t // 2 + 1))
                    s, kp, _ = pairs[t]
                    nc.scalar.activation(hTr[:, 0, 2 * kp:2 * kp + 2, s * T:(s + 1) * T],
                                         htmp[:, t % 4, :].rearrange("p (k t) -> p k t", k=2), ACT.Copy)\
                        .then_inc(h_hi.sem, 1)

                for t in range(0, len(pairs), 2):
                    s, kp, turned = pairs[t]
                    act.wait_ge(*xt_ready.at(nn, turned + 1))
                    if t >= 4:
                        act.wait_ge(*h_lo.at(nn, t - 3))
                    for kk in range(2):
                        k = 2 * kp + kk
                        ins = nc.scalar.activation(htmp[:, t % 4, kk * T:(kk + 1) * T],
                                                   PS[:, 4 * s + kp, kk * T:(kk + 1) * T],
                                                   ACT.Identity, bias=modB[:, norm, s, k:k + 1],
                                                   scale=modA[:, norm, s, k:k + 1])
                    ins.then_inc(tmp_act.sem, 1)
                    if t:
                        part_high(t - 1)
                    part_high(t)
                part_high(len(pairs) - 1)

            act.wait_ge(x_loaded, 32)
            for l in range(L):
                NS = streams(l)
                tok = NS * T
                squares(2 * l, 2, (comb_x, l - 1, 2 * NT[l - 1] * (NP[l - 1] - 1)) if l else None)
                high(l, 0)
                high(l, 1)
                modulate(2 * l, 0, 2)
                act.wait_ge(par_loaded, 16 * (l + 1))
                nc.scalar.activation(rwr[:, 0, :], par[:, P_RW:P_RW + RW_COLS], ACT.Copy).then_inc(rw_hi.sem, 1)
                act.wait_ge(*lam_prod.at(l, 1))
                nc.scalar.activation(lam[:, 2:4], lam[:, 0:2], ACT.Exp).then_inc(lam_exp.sem, 1)
                units, counts = WU[l]
                n_aux = 0
                for u in units:
                    if splits_here(u):
                        high(l, u["q"] + 2)
                    n_aux += u["kind"] in AUX
                    if u.get("by") != "act":
                        continue
                    bank = PS[:, u["bank"], :]
                    if u["kind"] == "pool":
                        g = u["g"]
                        act.wait_ge(*aux_sum.at(l, n_aux))
                        nc.scalar.activation(region["pz"][:, g, 0:tok], bank[:, 0:tok], ACT.Copy,
                                             scale=par[:, P_PSC + g:P_PSC + g + 1]).then_inc(w_act.sem, 1)
                        continue
                    if u["kind"] == "tile":
                        act.wait_ge(*(chunk_sum.at(l, u["q"] + 1) if u["last"] else tile_sum.at(l, u["sums"])))
                        o, w = region[u["name"]][:, u["m"], :], 512
                    else:
                        act.wait_ge(*chunk_sum.at(l, u["q"] + 1))
                        w = u["tokens"]
                        o = region[u["name"]][:, u["ch"], 0:w]
                    if u["name"] in ("su", "sv"):
                        nc.scalar.activation(o, bank[:, 0:w], ACT.Gelu_apprx_tanh).then_inc(w_act.sem, 1)
                    elif u["name"] in ("dq", "nq"):
                        nc.scalar.activation(o, bank[:, 0:w], ACT.Copy, scale=0.125).then_inc(w_act.sem, 1)
                    else:
                        nc.scalar.activation(o, bank[:, 0:w], ACT.Copy).then_inc(w_act.sem, 1)
                blocks, nb = BL[l], NB[l]
                tr, tr_n = TU[l]

                def attention(i_):
                    for u in tr:
                        if u["slot"] == i_ and u["kind"] == "o":
                            kind, s, qt, _ = blocks[4 * u["g"]]
                            act.wait_ge(*tr_made.at(l, u["t"] + 1))
                            dst = region["dq" if kind == "diff" else "nq"][:, :, s * T + qt * 128:s * T + (qt + 1) * 128]
                            src = PS[:, 2 + u["t"] % 2, :].rearrange("p (a b) -> p a b", a=4)
                            if kind == "diff":
                                act.wait_ge(*lam_ready.at(l, 1))
                                nc.scalar.activation(dst, src, ACT.Copy, scale=subg).then_inc(at_act.sem, 1)
                            else:
                                nc.scalar.activation(dst, src, ACT.Copy).then_inc(at_act.sem, 1)
                    if i_ < nb:
                        kind, s, qt, h = blocks[i_]
                        nk = 2 * T if s == 0 else T
                        act.wait_ge(*maxes.at(l, i_ + 1))
                        if i_ >= 2:
                            t_last = max(u["t"] for u in tr if u["kind"] == "p" and u["b"] == i_ - 2)
                            act.wait_ge(*tr_made.at(l, t_last + 1))
                        for a in range(2):
                            ins = nc.scalar.activation(p_t[:, i_ % 2, a, 0:nk], PS[:, a, 0:nk], ACT.Exp,
                                                       bias=nmx[:, i_ % 2, a:a + 1],
                                                       accum_out=rs[:, i_ % 2, a:a + 1])
                        ins.then_inc(exps.sem, 1)
                    for u in tr:
                        if u["slot"] == i_ and u["by"] == "act" and u["kind"] == "p":
                            b = u["b"]
                            nkt = 4 if blocks[b][1] == 0 else 2
                            act.wait_ge(*tr_made.at(l, u["t"] + 1))
                            readers = [v["b"] for v in tr[:u["t"]] if v["kind"] == "p" and v["t"] % 2 == u["t"] % 2]
                            if readers:
                                act.wait_ge(*pv.at(l, readers[-1] + 1))
                            nc.scalar.activation(at[:, u["t"] % 2, 0:nkt * 128], PS[:, 2 + u["t"] % 2, 0:nkt * 128],
                                                 ACT.Copy).then_inc(at_act.sem, 1)
                    g = (i_ - 5) // 4
                    if (i_ - 5) % 4 == 0 and 0 <= g < NG[l] and blocks[4 * g][0] == "diff":
                        act.wait_ge(*pv.at(l, 4 * g + 4))
                        if g >= 1:
                            act.wait_ge(*tr_made.at(l, [u["t"] for u in tr if u["kind"] == "o" and u["g"] == g - 1][0] + 1))
                        nc.scalar.activation(on, PS[:, 4, :], ACT.Square).then_inc(o_square.sem, 1)

                bc = [0]
                done = MOD0 if l == 0 else 0

                def gate_rows_of(m_):
                    ml, q = mod_of(l, done + m_)
                    part, c = q // PQ, slice(q % PQ * MQ, (q % PQ + 1) * MQ)
                    for s in range(streams(ml) if part == 2 else 1):
                        act.wait_ge(*gate_bc.at(l, bc[0] + 1))
                        nc.scalar.activation(g1b[:, s, c] if part == 2 else g2r[:, c], PS[:, bc[0] % 2, 0:MQ], ACT.Copy)\
                            .then_inc(gate_rows.sem, 1)
                        bc[0] += 1

                def branch_high(t):
                    b, k = MERGE_ORDER[2 + t // 4], t % 4
                    act.wait_ge(*pv.at(l, nb))
                    act.wait_ge(*at_act.at(l, tr_n["act"]))
                    nc.scalar.activation(br_hi_of[b][:, k, 0:tok], branches[:, b, k, 0:tok], ACT.Copy)\
                        .then_inc(branch_hi.sem, 1)

                def projection_high(n):
                    if n >= NM:
                        return
                    slot, use = item_at["br", l, n]
                    act.wait_ge(loaded[slot], 16 * (use + 1))
                    if n >= HALF + 2:
                        act.wait_ge(*projs.at(l, n - 1))
                    nc.scalar.activation(wbr[:, n % 2, 0, :], ring[:, slot, 0:512], ACT.Copy).then_inc(wbr_hi.sem, 1)

                for u in MERGE[l]:
                    n = u["n"]
                    if n == HALF:
                        for t in range(4):
                            branch_high(t)
                        projection_high(HALF)
                    for what, arg in unit_events(u):
                        if what == "att":
                            attention(arg)
                        elif what == "gates" and arg == 1:
                            act.wait_ge(*chunk_sum.at(l, NW + n + 1))
                            if n >= 2:
                                act.wait_ge(*merged.at(l, n - 1))
                            nc.scalar.activation(sgt[:, n % 2, 0:tok], PS[:, 5, 0:tok], ACT.Tanh, scale=0.5)\
                                .then_inc(sigs.sem, 1)
                            high(l, NW + n + 2)
                    if n >= HALF:
                        projection_high(n + 1)
                    if HALF <= n < HALF + 4:
                        branch_high(4 + n - HALF)
                    for m_, half_ in u["mod"]:
                        if half_ == 0 and m_ > len(mod_steps(l)[0]):
                            gate_rows_of(m_ - 1)
                for k in range(KD):
                    if k == KD - 1:
                        gate_rows_of(MODS[l] - 1)
                    act.wait_ge(*merged.at(l, NM - KD + k + 1))
                    act.wait_ge(*chunk_sum.at(l, NW + NM))
                    nc.scalar.activation(hTr[:, 0, k, 0:tok], mT[l][:, k, :], ACT.Copy, scale=0.5).then_inc(m_hi.sem, 1)
                if l == 0:
                    act.wait_ge(*m_lo.at(l, KD))
                    act.dma_start(x[:, 0:2, :], A["x"].rearrange("o (m p) d -> p (o m) d", p=128)).then_inc(x_back, 16)
                    act.dma_start(x[:, 2:4, :], A["ctx"].rearrange("o (m p) d -> p (o m) d", p=128)).then_inc(x_back, 16)
                for k in range(2, KD):
                    high(l, NW + NM + k)
                squares(2 * l + 1, NS, (mix_x, l, 0))
                modulate(2 * l + 1, 1, NS)
                act.wait_ge(*logitsT.at(l, 1))
                nc.scalar.activation(work[0:E, 8, 0:tok], PS[0:E, 0, 0:tok], ACT.Copy).then_inc(logits_copied.sem, 1)
                act.wait_ge(*r_max.at(l, 1))
                for m in range(NT[l]):
                    nc.scalar.activation(rex[:, m, :], PS[:, 4, m * E:(m + 1) * E], ACT.Exp, bias=rmx[:, m:m + 1],
                                         accum_out=rsum[:, m:m + 1]).then_inc(r_exp.sem, 1)
                with act.Fori(0, NP[l]) as i:
                    def when(sig, n, k):
                        sem, val = sig.at(l, k)
                        act.wait_ge(sem, i * n + val)

                    when(gathered, 2, 1)
                    nc.scalar.activation(toks[:, 0:512], PS[:, 6, :], ACT.Copy).then_inc(tok_act.sem, 1)
                    when(combT_made, 1, 1)
                    nc.scalar.activation(combT[:, 0:NT[l], :].rearrange("p a b -> p (a b)"), PS[:, 4, 0:NT[l] * 128],
                                         ACT.Copy).then_inc(combT_ready.sem, 1)
                    when(h1_sum, 1, 1)
                    for h in range(2):
                        nc.scalar.activation(sil[:, h * 512:(h + 1) * 512], PS[:, h, :], ACT.Silu)\
                            .then_inc(sil_ready.sem, 1)
                    when(hidT_made, 2, 1)
                    nc.scalar.activation(hidT[:, 0:4, :].rearrange("p a b -> p (a b)"), PS[:, 6, :], ACT.Copy)\
                        .then_inc(hidT_act.sem, 1)
            squares(4, 1, (comb_x, L - 1, 2 * NT[L - 1] * (NP[L - 1] - 1)))

        @block.gpsimd
        def _(pool):
            steps = [0]

            def step(ins):
                steps[0] += 1
                ins.then_inc(pool_step, 1)
                pool.wait_ge(pool_step, steps[0])

            rpb_v = A["na_rpb"]

            def load_bias(l):
                for h in range(8):
                    for r in range(2):
                        start = ((l * 8 + h) * RPB_R + (RPB_R // 2 - 3)) * RPB_C + RPB_C * r + RPB_C // 2 - 63
                        src = bass.AP(tensor=rpb_v.tensor, offset=rpb_v.offset + start,
                                      ap=[[1, 64], [RPB_C, 6], [1, GRID_W]])
                        pool.dma_start(nab[64 * r:64 * r + 64, h, :].rearrange("p (i c) -> p i c", i=6), src)\
                            .then_inc(bias_loaded, 16)

            def inverse_root(sq, mean, root, n, scale, ready):
                step(pool.tensor_scalar(mean[:, 0:n], sq, scale, EPS, ALU.mult, ALU.add))
                pool.tensor_tensor(root[:, 0:n], mean[:, 0:n], half[:, 0:n], ALU.pow).then_inc(ready, 1)

            def norm_roots(nn, n_streams):
                for s in range(n_streams):
                    pool.wait_ge(*sq_done.at(nn, 2 * s + 2))
                    c = slice(2 * s, 2 * s + 2)
                    inverse_root(ss[:, c], ms[:, c], rstd[:, c], 2, 1.0 / D, rstd_done.sem)

            pool.memset(cond[:, :, :], 0.0).then_inc(cond_ready, 1)
            pool.memset(half, -0.5).then_inc(half_ready, 1)
            pool.wait_ge(half_ready, 1)
            for l in range(L):
                NS = streams(l)
                tok = NS * T
                if l:
                    pool.wait_ge(*logits.at(l - 1, 1))
                pool.dma_start(par[:, :], A["par"][l]).then_inc(par_loaded, 16)
                norm_roots(2 * l, 2)
                if l == 0:
                    pool.wait_ge(*mod_ready.at(0, 1))
                load_bias(l)
                pool.wait_ge(*v_stats.at(l, 1))
                inverse_root(vmv[:, 0:2 * NS, 1], vms, vrstd, 2 * NS, 1.0, v_rstd.sem)
                n = last_of(WU[l][0], "pz", "w")
                pool.wait_ge(*w_act.at(l, n["act"]))
                pool.wait_ge(*w_dve.at(l, n["dve"]))
                pool.wait_ge(consts_loaded, 48)
                PW = T + 16
                za, zb = (work[:, 2 * i_:2 * i_ + 2, :].rearrange("p a b -> p (a b)")[:, 0:2 * PW].rearrange(
                    "p (s t) -> p s t", s=2) for i_ in (0, 1))
                for g, w in enumerate(POOL_W):
                    z = region["pz"][:, g, 0:tok].rearrange("p (s t) -> p s t", s=NS)
                    step(pool.memset(za[:, 0:NS, 0:8], 0.0))
                    step(pool.memset(za[:, 0:NS, T + 8:PW], 0.0))
                    step(pool.tensor_copy(za[:, 0:NS, 8:8 + T], z))
                    cur, nxt, n, span = za, zb, PW, 1
                    while span < w:
                        n -= span
                        step(pool.tensor_tensor(nxt[:, 0:NS, 0:n], cur[:, 0:NS, 0:n], cur[:, 0:NS, span:span + n],
                                                ALU.add))
                        cur, nxt, span = nxt, cur, 2 * span
                    c0 = 8 - w // 2
                    step(pool.tensor_scalar(nxt[:, 0:NS, 8:T - 8], cur[:, 0:NS, c0 + 8:c0 + T - 8], 1.0 / w, None, ALU.mult))
                    for e in range(2):
                        cnt = cst[:, C_CNT + g * 16 + 8 * e:C_CNT + g * 16 + 8 * e + 8].unsqueeze(1).broadcast_to([128, NS, 8])
                        o = e * (T - 8)
                        step(pool.tensor_tensor(nxt[:, 0:NS, o:o + 8], cur[:, 0:NS, c0 + o:c0 + o + 8], cnt, ALU.mult))
                    pool.tensor_tensor(z, nxt[:, 0:NS, 0:T], z, ALU.subtract).then_inc(pooled.sem, 1)
                    pool.wait_ge(*pooled.at(l, g + 1))
                pool.wait_ge(bias_loaded, 16 * 16 * (l + 1))
                tb = nab[:, :, :].rearrange("p h (i c) -> p (h i) c", c=GRID_W)
                pool.tensor_tensor(tb, tb, cst[:, C_MASK:C_MASK + GRID_W].unsqueeze(1).broadcast_to([128, 48, GRID_W]),
                                   ALU.add).then_inc(bias_masked.sem, 1)
                for g in range(NG[l] // 2):
                    pool.wait_ge(*o_ss.at(l, g + 1))
                    inverse_root(oss[:, 0:4], oms, orstd, 4, 1.0 / 128, o_rstd.sem)
                norm_roots(2 * l + 1, NS)
            norm_roots(4, 1)

        @block.vector
        def _(dve):
            steps = [0]

            def step(ins):
                steps[0] += 1
                ins.then_inc(dve_step, 1)
                dve.wait_ge(dve_step, steps[0])

            def low(l, j):
                if j >= NC_ALL:
                    return
                slot, _ = item_at["chunk", l, j]
                dve.wait_ge(*w_hi.at(l, j + 1))
                nc.vector.tensor_tensor(wr[:, j % 2, 1, :], ring[:, slot, :], wr[:, j % 2, 0, :].bitcast(f32),
                                        ALU.subtract).then_inc(w_lo.sem, 1)

            def mod_out(l, n):
                dve.wait_ge(*mod_sum.at(l, n + 1))
                nc.vector.tensor_copy(modp[:, n % 2, :], PS[:, mod_bank(l, n), 0:MQ]).then_inc(mod_part.sem, 1)

            def mod_columns(l, ml, norm, sec):
                dve.wait_ge(*mod_cols.at(l, sec))
                cols = PS[:, 7, 256 + 32 * norm:288 + 32 * norm].rearrange("p (a k s) -> p a s k", a=2, s=2)
                g0 = (S_N1 if norm == 0 else S_N2) + KD * ml
                step(nc.vector.tensor_scalar(modA[:, norm, :, :], cols[:, 1, :, :], 1.0, None, ALU.add))
                for s in range(2):
                    step(nc.vector.tensor_tensor(modA[:, norm, s, :], modA[:, norm, s, :], stay[:, g0:g0 + KD], ALU.mult))
                nc.vector.tensor_copy(modB[:, norm, :, :], cols[:, 0, :, :]).then_inc(mod_ready.sem, 1)

            def normalise(nn, s):
                dve.wait_ge(*rstd_done.at(nn, s + 1))
                for m in range(2 * s, 2 * s + 2):
                    nc.vector.tensor_scalar(xn[:, m, :], x[:, m, :], rstd[:, m:m + 1], None, ALU.mult)\
                        .then_inc(xn_ready.sem, 1)

            def modulate(nn, norm, n_streams):
                dve.wait_ge(*mod_ready.at(*MODULATED[nn]))
                pairs = mod_pairs(nn, n_streams)

                def part_low(t):
                    s, kp, _ = pairs[t]
                    dve.wait_ge(*h_hi.at(nn, t + 1))
                    nc.vector.tensor_tensor(hTr[:, 1, 2 * kp:2 * kp + 2, s * T:(s + 1) * T],
                                            htmp[:, t % 4, :].rearrange("p (k t) -> p k t", k=2),
                                            hTr[:, 0, 2 * kp:2 * kp + 2, s * T:(s + 1) * T].bitcast(f32),
                                            ALU.subtract).then_inc(h_lo.sem, 1)

                for t in range(1, len(pairs), 2):
                    s, kp, turned = pairs[t]
                    dve.wait_ge(*xt_ready.at(nn, turned + 1))
                    if t >= 4:
                        dve.wait_ge(*h_lo.at(nn, t - 3))
                    for kk in range(2):
                        k = 2 * kp + kk
                        ins = nc.vector.tensor_scalar(htmp[:, t % 4, kk * T:(kk + 1) * T],
                                                      PS[:, 4 * s + kp, kk * T:(kk + 1) * T],
                                                      modA[:, norm, s, k:k + 1], modB[:, norm, s, k:k + 1],
                                                      ALU.mult, ALU.add)
                    ins.then_inc(tmp_dve.sem, 1)
                    if t > 1:
                        part_low(t - 2)
                    part_low(t - 1)
                part_low(len(pairs) - 1)

            dve.wait_ge(consts_loaded, 48)
            for n in range(MOD0):
                mod_out(0, n)
                if n == MOD0 - 3:
                    dve.wait_ge(x_loaded, 32)
                    normalise(0, 0)
                    normalise(0, 1)
            mod_columns(0, 0, 0, 1)
            for l in range(L):
                NS = streams(l)
                tok = NS * T
                lam_init = 0.8 - 0.6 * math.exp(-0.3 * l)
                if l:
                    normalise(2 * l, 0)
                    normalise(2 * l, 1)
                low(l, 0)
                low(l, 1)
                modulate(2 * l, 0, 2)
                dve.wait_ge(*rw_hi.at(l, 1))
                nc.vector.tensor_tensor(rwr[:, 1, :], par[:, P_RW:P_RW + RW_COLS], rwr[:, 0, :].bitcast(f32), ALU.subtract)\
                    .then_inc(rw_lo.sem, 1)
                lp = par[:, P_LAM:P_LAM + 256].rearrange("p (a b c) -> p a b c", a=2, b=2)
                lt = modp[:, 0, 0:128].rearrange("p (a c) -> p a c", a=2)
                step(nc.vector.tensor_tensor(lt, lp[:, :, 0, :], lp[:, :, 1, :], ALU.mult))
                nc.vector.reduce_sum(lam[:, 0:2], lt, axis=AX.X).then_inc(lam_prod.sem, 1)
                dve.wait_ge(*lam_exp.at(l, 1))
                step(nc.vector.tensor_tensor(lam[:, 4:5], lam[:, 3:4], lam[:, 2:3], ALU.subtract))
                step(nc.vector.tensor_scalar(lam[:, 5:6], lam[:, 4:5], -lam_init, None, ALU.add))
                nc.vector.tensor_scalar(subg, par[:, P_SUBG:P_SUBG + 1], 1.0 - lam_init, None, ALU.mult)\
                    .then_inc(lam_ready.sem, 1)
                units, counts = WU[l]
                n_aux = 0
                sv_last = last_of(units, "sv", "tile")
                for u in units:
                    if splits_here(u):
                        low(l, u["q"] + 2)
                    n_aux += u["kind"] in AUX
                    if u.get("by") == "dve":
                        bank = PS[:, u["bank"], :]
                        if u["kind"] == "rope":
                            dve.wait_ge(*aux_sum.at(l, n_aux))
                            two = region[u["name"]][:, 2 * u["pair"]:2 * u["pair"] + 2, 0:T]
                            turned = work[:, 4, :].rearrange("p (a b) -> p a b", a=2)
                            sin2, cos2 = (v.unsqueeze(1).broadcast_to([128, 2, T]) for v in (sinT, cosT))
                            step(nc.vector.tensor_tensor(turned, bank.rearrange("p (a b) -> p a b", a=2), sin2, ALU.mult))
                            step(nc.vector.tensor_tensor(two, two, cos2, ALU.mult))
                            nc.vector.tensor_tensor(two, two, turned, ALU.add).then_inc(w_dve.sem, 1)
                            dve.wait_ge(*w_dve.at(l, u["nth"]))
                        elif u["kind"] == "f":
                            g = u["g"]
                            dve.wait_ge(*aux_sum.at(l, n_aux))
                            b_ = par[:, P_SGUB + g * 128:P_SGUB + (g + 1) * 128].unsqueeze(1).broadcast_to([128, 2 * NS, 128])
                            t_ = work[:, 5, 0:tok]
                            step(nc.vector.scalar_tensor_tensor(
                                out=t_.rearrange("p (m q) -> p m q", q=128),
                                in0=bank[:, 0:tok].rearrange("p (m q) -> p m q", q=128),
                                scalar=par[:, P_SGUG + g:P_SGUG + g + 1], in1=b_, op0=ALU.mult, op1=ALU.add))
                            u_ = region["su"][:, g, 0:tok]
                            nc.vector.tensor_tensor(u_, u_, t_, ALU.mult).then_inc(w_dve.sem, 1)
                            dve.wait_ge(*w_dve.at(l, u["nth"]))
                        else:
                            if u["kind"] == "tile":
                                dve.wait_ge(*(chunk_sum.at(l, u["q"] + 1) if u["last"] else tile_sum.at(l, u["sums"])))
                                o, w = region[u["name"]][:, u["m"], :], 512
                            else:
                                dve.wait_ge(*chunk_sum.at(l, u["q"] + 1))
                                w = u["tokens"]
                                o = region[u["name"]][:, u["ch"], 0:w]
                            if u["name"] in ("dq", "nq"):
                                nc.vector.tensor_scalar(o, bank[:, 0:w], 0.125, None, ALU.mult).then_inc(w_dve.sem, 1)
                            else:
                                nc.vector.tensor_copy(o, bank[:, 0:w]).then_inc(w_dve.sem, 1)
                    if u["kind"] == "w" and u["name"] == "pz" and u["ch"] == 1:
                        dve.wait_ge(*w_act.at(l, sv_last["act"]))
                        dve.wait_ge(*w_dve.at(l, sv_last["dve"]))
                        v_ = region["sv"]
                        for m in range(2 * NS):
                            step(nc.vector.bn_stats(vst[:, m, :], v_[:, m, :]))
                            ins = nc.vector.bn_aggr(vmv[:, m, :], vst[:, m, :])
                        ins.then_inc(v_stats.sem, 1)
                    if u["kind"] == "w" and u["name"] == "pz" and u["ch"] == 3:
                        dve.wait_ge(*v_rstd.at(l, 1))
                        for m in range(2 * NS):
                            nc.vector.tensor_scalar(v_[:, m, :], v_[:, m, :], vmv[:, m, 0:1], vrstd[:, m:m + 1],
                                                    ALU.subtract, ALU.mult).then_inc(v_norm.sem, 1)
                blocks, nb = BL[l], NB[l]
                tr, tr_n = TU[l]

                def probabilities(i_):
                    g = (i_ - 6) // 4
                    if (i_ - 6) % 4 == 0 and 0 <= g < NG[l] and blocks[4 * g][0] == "diff":
                        dve.wait_ge(*o_rstd.at(l, g + 1))
                        nc.vector.tensor_tensor(on.rearrange("p (a b) -> p a b", a=4),
                                                PS[:, 4, :].rearrange("p (a b) -> p a b", a=4),
                                                orstd.unsqueeze(2).broadcast_to([128, 4, 128]), ALU.mult)\
                            .then_inc(o_norm.sem, 1)
                    b = i_ - 1
                    if 0 <= b < nb:
                        kind, s, qt, h = blocks[b]
                        nk = 2 * T if s == 0 else T
                        dve.wait_ge(*exps.at(l, b + 1))
                        if kind == "diff":
                            r_ = rr[:, b % 2, :]
                            step(nc.vector.reciprocal(r_, rs[:, b % 2, :]))
                            step(nc.vector.tensor_tensor(r_[:, 1:2], r_[:, 1:2], lam[:, 5:6], ALU.mult))
                            step(nc.vector.tensor_scalar(p_t[:, b % 2, 0, 0:nk], p_t[:, b % 2, 0, 0:nk], r_[:, 0:1], None,
                                                         ALU.mult))
                            nc.vector.scalar_tensor_tensor(out=p_t[:, b % 2, 0, 0:nk], in0=p_t[:, b % 2, 1, 0:nk],
                                                           scalar=r_[:, 1:2], in1=p_t[:, b % 2, 0, 0:nk],
                                                           op0=ALU.mult, op1=ALU.add).then_inc(probs.sem, 1)
                        else:
                            nc.vector.reciprocal(nar[:, (b // 4) % 4, 2 * h:2 * h + 2], rs[:, b % 2, :])\
                                .then_inc(probs.sem, 1)

                def attention(i_):
                    if i_ < nb:
                        s = blocks[i_][1]
                        nk = 2 * T if s == 0 else T
                        dve.wait_ge(*scores.at(l, i_ + 1))
                        if i_ >= 2:
                            dve.wait_ge(*exps.at(l, i_ - 1))
                        nc.vector.reduce_max(nmx[:, i_ % 2, :], PS[:, 0:2, 0:nk], axis=AX.X,
                                             negate=True).then_inc(maxes.sem, 1)
                    for u in tr:
                        if u["slot"] != i_ or u["by"] != "dve":
                            continue
                        nkt = 4 if blocks[u["b"]][1] == 0 else 2
                        dve.wait_ge(*tr_made.at(l, u["t"] + 1))
                        dve.wait_ge(*pv.at(l, u["b"]))
                        nc.vector.tensor_copy(at[:, u["t"] % 2, 0:nkt * 128], PS[:, 2 + u["t"] % 2, 0:nkt * 128])\
                            .then_inc(at_dve.sem, 1)
                    g = (i_ - 5) // 4
                    if (i_ - 5) % 4 == 0 and 0 <= g < NG[l]:
                        kind = blocks[4 * g][0]
                        o_ = PS[:, 4, :]
                        if g >= 1:
                            t_o = [u["t"] for u in tr if u["kind"] == "o" and u["g"] == g - 1][0]
                            dve.wait_ge(*tr_made.at(l, t_o + 1))
                        if kind == "diff":
                            dve.wait_ge(*o_square.at(l, g + 1))
                            nc.vector.reduce_sum(oss, on.rearrange("p (a b) -> p a b", a=4), axis=AX.X)\
                                .then_inc(o_ss.sem, 1)
                        else:
                            dve.wait_ge(*pv.at(l, 4 * g + 4))
                            dve.wait_ge(*probs.at(l, 4 * g + 4))
                            nc.vector.tensor_tensor(on.rearrange("p (a b) -> p a b", a=8),
                                                    o_.rearrange("p (a b) -> p a b", a=8),
                                                    nar[:, g % 4, :].unsqueeze(2).broadcast_to([128, 8, 64]), ALU.mult)\
                                .then_inc(o_norm.sem, 1)

                done = MOD0 if l == 0 else 0

                def branch_low(t):
                    b, k = MERGE_ORDER[2 + t // 4], t % 4
                    dve.wait_ge(*branch_hi.at(l, t + 1))
                    nc.vector.tensor_tensor(br_lo_of[b][:, k, 0:tok], branches[:, b, k, 0:tok],
                                            br_hi_of[b][:, k, 0:tok].bitcast(f32), ALU.subtract).then_inc(branch_lo.sem, 1)

                def projection_low(n):
                    if n >= NM:
                        return
                    slot, _ = item_at["br", l, n]
                    dve.wait_ge(*wbr_hi.at(l, n - HALF + 1))
                    nc.vector.tensor_tensor(wbr[:, n % 2, 1, :], ring[:, slot, 0:512], wbr[:, n % 2, 0, :].bitcast(f32),
                                            ALU.subtract).then_inc(wbr_lo.sem, 1)

                EARLY = 4

                def merged_low(k):
                    dve.wait_ge(*m_hi.at(l, k + 1))
                    nc.vector.scalar_tensor_tensor(out=hTr[:, 1, k, 0:tok], in0=mT[l][:, k, :], scalar=0.5,
                                                   in1=hTr[:, 0, k, 0:tok].bitcast(f32), op0=ALU.mult,
                                                   op1=ALU.subtract).then_inc(m_lo.sem, 1)

                for u in MERGE[l]:
                    n, v = u["n"], u["v"]
                    if n == HALF:
                        for t in range(4):
                            branch_low(t)
                        projection_low(HALF)
                    events = unit_events(u)
                    for (what, arg), after in zip(events, events[1:] + [(None, None)]):
                        if after[0] == "att":
                            probabilities(after[1])
                        if what == "att":
                            attention(arg)
                        elif what == "proj":
                            if n == NM - 1:
                                for k in range(EARLY):
                                    merged_low(k)
                            dve.wait_ge(*sigs.at(l, n + 1))
                            dve.wait_ge(*projs.at(l, n + 1))
                            first = u["p"] == 0
                            dst = mT[l][:, v, :] if first else sgt[:, n % 2, 0:tok]
                            nc.vector.scalar_tensor_tensor(out=dst, in0=sgt[:, n % 2, 0:tok], scalar=1.0,
                                                           in1=PS[:, 6, 0:tok], op0=ALU.add, op1=ALU.mult)\
                                .then_inc(gated.sem, 1)
                            dve.wait_ge(*gated.at(l, n + 1))
                            if first:
                                dve.sem_inc(merged.sem, 1)
                            else:
                                nc.vector.tensor_tensor(mT[l][:, v, :], mT[l][:, v, :], dst, ALU.add)\
                                    .then_inc(merged.sem, 1)
                        elif what == "mod":
                            m_, half_ = arg
                            if half_ == 0 and m_ == len(mod_steps(l)[0]):
                                mod_columns(l, l, 1, 3 if l == 0 else 1)
                                if l + 1 < L:
                                    mod_columns(l, l + 1, 0, 3)
                            if half_ == 1:
                                mod_out(l, done + m_)
                    low(l, NW + n + 2)
                    if n >= HALF:
                        projection_low(n + 1)
                    if HALF <= n < HALF + 4:
                        branch_low(4 + n - HALF)
                for k in range(EARLY, KD):
                    merged_low(k)
                for k in range(2, KD):
                    low(l, NW + NM + k)
                dve.wait_ge(*gate_rows.at(l, NGB[l]))
                if l == 0:
                    dve.wait_ge(x_back, 32)
                def residual(c):
                    m, h = c // 2, c % 2
                    dve.wait_ge(*mix_gated.at(l, c + 1))
                    xs_ = x[:, m, h * 512:(h + 1) * 512]
                    nc.vector.tensor_tensor(xs_, xs_, mix_tmp(c), ALU.add).then_inc(mix_x.sem, 1)

                for c in range(2 * NT[l]):
                    dve.wait_ge(*mix_sum.at(l, c + 1))
                    if c >= 2:
                        dve.wait_ge(*mix_x.at(l, c - 1))
                    nc.vector.tensor_tensor(mix_tmp(c), PS[:, c, :], g1b[:, c // 4, (c % 2) * 512:(c % 2 + 1) * 512],
                                            ALU.mult).then_inc(mix_gated.sem, 1)
                    if c:
                        residual(c - 1)
                residual(2 * NT[l] - 1)
                for s in range(NS):
                    normalise(2 * l + 1, s)
                modulate(2 * l + 1, 1, NS)
                dve.wait_ge(*logits.at(l, 1))
                nc.vector.reduce_max(rmx[:, 0:NT[l]], PS[:, 4, 0:NT[l] * E].rearrange("p (m e) -> p m e", e=E), axis=AX.X,
                                     negate=True).then_inc(r_max.sem, 1)
                dve.wait_ge(*r_exp.at(l, NT[l]))
                step(nc.vector.reciprocal(rinv[:, 0:NT[l]], rsum[:, 0:NT[l]]))
                for m in range(NT[l]):
                    ins = nc.vector.tensor_scalar(aff[:, m % 2, m // 2, :], rex[:, m, :], rinv[:, m:m + 1], None, ALU.mult)
                ins.then_inc(aff_ready.sem, 1)
                step(nc.vector.memset(selg[:, :, :], 0.0))
                RE = NS * E
                dve.wait_ge(*affT_made.at(l, 1))
                step(nc.vector.tensor_copy(afT[0:RE, :], PS[0:RE, 1, 0:T]))
                src = afT[0:RE, :]
                for r in range(CAP // 8):
                    step(nc.vector.max(top[0:RE, 8 * r:8 * r + 8], src))
                    step(nc.vector.match_replace(afR[0:RE, (r + 1) % 2, :], top[0:RE, 8 * r:8 * r + 8], src, -1.0))
                    src = afR[0:RE, (r + 1) % 2, :]
                assert (CAP // 8) % 2 == 0
                nc.vector.tensor_tensor(afR[0:RE, 0, :], afT[0:RE, :], afR[0:RE, 0, :], ALU.not_equal)\
                    .then_inc(mask_ready.sem, 1)
                dve.wait_ge(*maskT_made.at(l, 1))
                nc.vector.tensor_copy(msk[:, :, 0:RE], PS[:, 2, 0:64].rearrange("p (j e) -> p j e", j=2)[:, :, 0:RE])\
                    .then_inc(maskT_ready.sem, 1)
                dve.wait_ge(*maskT_ready.at(l, 1))
                dve.wait_ge(*count_made.at(l, 1))
                nc.vector.tensor_tensor(place[:, :, 0:NS, :].rearrange("p j s e -> p j (s e)"),
                                        PS[:, 3, 0:64].rearrange("p (j e) -> p j e", j=2)[:, :, 0:RE],
                                        msk[:, :, 0:RE], ALU.mult).then_inc(place_ready.sem, 1)
                dve.wait_ge(*place_ready.at(l, 1))
                G = GE[l]
                with dve.Fori(0, NP[l]) as i:
                    def when(sig, n, k):
                        sem, val = sig.at(l, k)
                        dve.wait_ge(sem, i * n + val)

                    for s in range(NS):
                        sp = selp[:, s * 2 * G * CAP:(s + 1) * 2 * G * CAP].rearrange("p (j g c) -> p j g c", j=2, g=G)
                        pl = place[:, :, s, ds(i * G, G)].unsqueeze(3).broadcast_to([128, 2, G, CAP])
                        io = iota1.unsqueeze(1).unsqueeze(1).broadcast_to([128, 2, G, CAP])
                        nc.vector.tensor_tensor(sp, pl, io, ALU.is_equal).then_inc(sel_ready.sem, 1)
                    when(sel_ready, NS, NS)
                    for s in range(NS):
                        sp = selp[:, s * 2 * G * CAP:(s + 1) * 2 * G * CAP].rearrange("p (j g c) -> p j g c", j=2, g=G)
                        af = aff[:, :, s, ds(i * G, G)].unsqueeze(3).broadcast_to([128, 2, G, CAP])
                        sg = selg[:, 2 * s:2 * s + 2, :].rearrange("p j (g s c) -> p j g s c", g=G, s=NS)[:, :, :, s, :]
                        nc.vector.tensor_tensor(sg, sp, af, ALU.mult).then_inc(selg_ready.sem, 1)
                    when(gathered, 2, 2)
                    nc.vector.tensor_copy(toks[:, 512:1024], PS[:, 7, :]).then_inc(tok_dve.sem, 1)
                    c = 0
                    for bk in range(2):
                        when(xs_made, 2, bk + 1)
                        for s in range(NS):
                            o = xsT[:, 4 * bk:4 * bk + 4, :].rearrange("p k (g s c) -> p k g s c", g=G, s=NS)[:, :, :, s, :]
                            src = PS[:, 6 + bk, :].rearrange("p (k s g c) -> p k s g c", k=4, s=NS, g=G)[:, :, s, :, :]
                            ga = modA[:, 1, s, 4 * bk:4 * bk + 4].unsqueeze(2).unsqueeze(2).broadcast_to([128, 4, G, CAP])
                            sh = modB[:, 1, s, 4 * bk:4 * bk + 4].unsqueeze(2).unsqueeze(2).broadcast_to([128, 4, G, CAP])
                            nc.vector.tensor_tensor(o, src, ga, ALU.mult).then_inc(xs_mul.sem, 1)
                            c += 1
                            when(xs_mul, 2 * NS, c)
                            nc.vector.tensor_tensor(o, o, sh, ALU.add).then_inc(xs_ready.sem, 1)
                    when(h3_sum, 1, 1)
                    for h in range(2):
                        when(sil_ready, 2, h + 1)
                        nc.vector.tensor_tensor(hid[:, h * 512:(h + 1) * 512], sil[:, h * 512:(h + 1) * 512],
                                                PS[:, 2 + h, :], ALU.mult).then_inc(hid_ready.sem, 1)
                    when(hidT_made, 2, 2)
                    nc.vector.tensor_copy(hidT[:, 4:8, :].rearrange("p a b -> p (a b)"), PS[:, 7, :])\
                        .then_inc(hidT_dve.sem, 1)
                    when(y_sum, 1, 1)
                    for h in range(2):
                        nc.vector.tensor_tensor(ysb[:, h * 512:(h + 1) * 512], PS[:, 4 + h, :],
                                                g2r[:, h * 512:(h + 1) * 512], ALU.mult).then_inc(y_ready.sem, 1)
                    for c in range(2 * NT[l]):
                        m, h = c // 2, c % 2
                        when(comb_sum, 2 * NT[l], c + 1)
                        xs_ = x[:, m, h * 512:(h + 1) * 512]
                        nc.vector.tensor_tensor(xs_, xs_, PS[:, c % 4, :], ALU.add).then_inc(comb_x.sem, 1)
                dve.wait_ge(*comb_x.at(l, 2 * NT[l] * NP[l]))
            dve.wait_ge(*rstd_done.at(4, 1))
            dve.wait_ge(consts_loaded, 64)
            for m in range(2):
                o_ = fin_out[:, m * D:(m + 1) * D]
                step(nc.vector.tensor_scalar(o_, x[:, m, :], rstd[:, m:m + 1], None, ALU.mult))
                nc.vector.tensor_tensor(o_, o_, fin_gain, ALU.mult).then_inc(fin_ready, 1)


def layout(inputs):
    a = {k: np.ascontiguousarray(np.asarray(v)) for k, v in inputs.items()}
    cols = lambda v, n: np.ascontiguousarray(v.reshape(n, 128).T)
    wide = lambda v: np.broadcast_to(v.reshape(1, -1), (128, v.size))
    par = np.zeros((L, 128, P_ALL), np.float32)
    stay = np.zeros((128, S_ALL), np.float32)
    for l in range(L):
        par[l, :, P_POOLW:P_POOLW + 512] = a["pool_w"][l].transpose(1, 0, 2).reshape(128, 512)
        par[l, :, P_SGUW:P_SGUW + 512] = a["sgu_w"][l].transpose(2, 0, 1).reshape(128, 512)
        par[l, :, P_SGUB:P_SGUB + 512] = wide(a["sgu_b"][l])
        par[l, :, P_LAM:P_LAM + 256] = wide(a["diff_lambda"][l])
        par[l, :, P_RW:P_RW + KD * E] = a["router_w"][l].reshape(KD, 128, E).transpose(1, 0, 2).reshape(128, KD * E)
        par[l, :, P_PSC:P_PSC + 4] = cols(a["pool_scale"][l], 4)
        par[l, :, P_SUBG:P_SUBG + 1] = cols(a["diff_subln_g"][l], 1)
        par[l, :, P_SGUG:P_SGUG + 4] = cols(a["sgu_norm_g"][l], 4)
        stay[:, S_N1 + KD * l:S_N1 + KD * (l + 1)] = cols(a["norm1_g"][l], KD)
        stay[:, S_N2 + KD * l:S_N2 + KD * (l + 1)] = cols(a["norm2_g"][l], KD)
    stay[:, S_C:S_C + KD] = cols(a["c"][0], KD)
    stay[:, S_C + KD:S_C + 2 * KD] = cols(a["c_ctx"], KD)
    d = {n: a[n] for n in ("x", "ctx", "w_mod", "b_mod", "w_in", "w_br", "w_out", "na_rpb", "moe_w1", "moe_w3", "moe_w2")}
    d.update(par=par, stay=stay, cst=shape_constants(), final_g=np.ascontiguousarray(wide(a["final_g"])))
    return d


def kernel(**inputs):
    import concourse.bacc as bacc
    from concourse.bass_utils import run_bass_kernel_spmd

    nc = bacc.Bacc("TRN2", target_bir_lowering=False, num_devices=1)
    arrays = layout(inputs)
    aps = {k: nc.dram_tensor(f"in_{k}", v.shape, mybir.dt.from_np(v.dtype), kind="ExternalInput").ap()
           for k, v in arrays.items()}
    out = nc.dram_tensor("out", (1, T, D), mybir.dt.float32, kind="ExternalOutput").ap()
    build(nc, aps, out)
    r = run_bass_kernel_spmd(nc, [{f"in_{k}": v for k, v in arrays.items()}], core_ids=[0])
    return r.results[0]["out"]
```
